# Optimizing a Trainium2 kernel written in Bass

```python
import jax, jax.numpy as jnp
from jax import lax
import numpy as np

D_MODEL = 2048
BATCH = 1
SEQ = 256
DEPTH = 1

GLA_HEADS = 4
GLA_DK = 128
GLA_DV = 256
GLA_RANK = 16
GLA_GATE_TEMP = 16.0
GLA_CHUNK = 64
GLA_K = GLA_HEADS * GLA_DK
GLA_V = GLA_HEADS * GLA_DV
MOBA_HEADS = 8
MOBA_HD = 128
MOBA_W = MOBA_HEADS * MOBA_HD
MOBA_BLOCK = 256
MOBA_TOPK = 3
MOBA_QCHUNK = 32
IN_SIZES = (GLA_K, GLA_K, GLA_V, GLA_V, GLA_RANK, MOBA_W, MOBA_W, MOBA_W, D_MODEL, D_MODEL)
IN_WIDTH = sum(IN_SIZES)
FFN_DIM = 5632
CONV_WIDTH = 3
N_MOD = 6
EPS = 1e-6

kernel_name = "hybrid_gla_moba_convffn_block"

def rmsnorm(x, gain):
    xf = x.astype(jnp.float32)
    y = xf * lax.rsqrt(jnp.mean(xf * xf, axis=-1, keepdims=True) + EPS) * gain.astype(jnp.float32)
    return y.astype(x.dtype)

def gla_chunked(q, k, v, log_a):
    B, S, H, dk = q.shape
    dv = v.shape[-1]
    C = GLA_CHUNK
    N = S // C

    def to_chunks(t):
        return t.reshape(B, N, C, H, t.shape[-1]).transpose(1, 0, 3, 2, 4)

    qs, ks, vs, gs = (to_chunks(t.astype(jnp.float32)) for t in (q * (dk ** -0.5), k, v, log_a))
    causal = jnp.tril(jnp.ones((C, C), dtype=bool))

    def step(state, inp):
        qc, kc, vc, gc = inp
        b = jnp.cumsum(gc, axis=2)
        o_inter = jnp.einsum('bhcd,bhde->bhce', qc * jnp.exp(b), state)
        diff = b[:, :, :, None, :] - b[:, :, None, :, :]
        decay = jnp.exp(jnp.where(causal[None, None, :, :, None], diff, -jnp.inf))
        attn = jnp.einsum('bhid,bhjd,bhijd->bhij', qc, kc, decay)
        o = o_inter + jnp.einsum('bhij,bhje->bhie', attn, vc)
        b_last = b[:, :, -1:, :]
        state = (jnp.exp(b_last[:, :, 0, :])[..., None] * state
                 + jnp.einsum('bhcd,bhce->bhde', kc * jnp.exp(b_last - b), vc))
        return state, o

    s0 = jnp.zeros((B, H, dk, dv), jnp.float32)
    _, outs = lax.scan(step, s0, (qs, ks, vs, gs))
    return outs.transpose(1, 0, 3, 2, 4).reshape(B, S, H, dv)

def moba_attention(q, k, v):
    B, S, H, hd = q.shape
    BLK = MOBA_BLOCK
    nb = -(-S // BLK)
    Sp = nb * BLK
    topk = min(MOBA_TOPK, nb - 1)
    scale = hd ** -0.5
    q = q.transpose(0, 2, 1, 3)
    pad = ((0, 0), (0, 0), (0, Sp - S), (0, 0))
    kblk = jnp.pad(k.transpose(0, 2, 1, 3), pad).reshape(B, H, nb, BLK, hd)
    vblk = jnp.pad(v.transpose(0, 2, 1, 3), pad).reshape(B, H, nb, BLK, hd)
    q_block = jnp.arange(S) // BLK

    if topk > 0:
        kmean = jnp.mean(kblk.astype(jnp.float32), axis=3)
        sblk = jnp.einsum('bhsd,bhnd->bhsn', q.astype(jnp.float32), kmean)
        past = jnp.arange(nb)[None, :] < q_block[:, None]
        sblk = jnp.where(past[None, None], sblk, -1e30)
        _, sel_idx = lax.top_k(sblk, topk)
        sel_valid = sel_idx < q_block[None, None, :, None]
    bi = jnp.arange(B)[:, None, None, None]
    hi = jnp.arange(H)[None, :, None, None]

    def chunk(ci):
        start = ci * MOBA_QCHUNK
        qc = lax.dynamic_slice_in_dim(q, start, MOBA_QCHUNK, axis=2)
        blk = start // BLK
        kown = lax.dynamic_index_in_dim(kblk, blk, axis=2, keepdims=False)
        vown = lax.dynamic_index_in_dim(vblk, blk, axis=2, keepdims=False)
        qpos = start + jnp.arange(MOBA_QCHUNK)
        kpos = blk * BLK + jnp.arange(BLK)
        s_own = jnp.einsum('bhqd,bhtd->bhqt', qc, kown).astype(jnp.float32) * scale
        s_own = jnp.where((kpos[None, :] <= qpos[:, None])[None, None], s_own, -jnp.inf)
        if topk == 0:
            p = jax.nn.softmax(s_own, axis=-1)
            return jnp.einsum('bhqt,bhtd->bhqd', p.astype(v.dtype), vown)
        idx = lax.dynamic_slice_in_dim(sel_idx, start, MOBA_QCHUNK, axis=2)
        valid = lax.dynamic_slice_in_dim(sel_valid, start, MOBA_QCHUNK, axis=2)
        ksel = kblk[bi, hi, idx]
        vsel = vblk[bi, hi, idx]
        s_sel = jnp.einsum('bhqd,bhqjtd->bhqjt', qc, ksel).astype(jnp.float32) * scale
        s_sel = jnp.where(valid[..., None], s_sel, -jnp.inf)
        s_all = jnp.concatenate([s_sel.reshape(B, H, MOBA_QCHUNK, topk * BLK), s_own], axis=-1)
        p = jax.nn.softmax(s_all, axis=-1).astype(v.dtype)
        p_sel = p[..., :topk * BLK].reshape(B, H, MOBA_QCHUNK, topk, BLK)
        p_own = p[..., topk * BLK:]
        return (jnp.einsum('bhqjt,bhqjtd->bhqd', p_sel, vsel)
                + jnp.einsum('bhqt,bhtd->bhqd', p_own, vown))

    outs = lax.map(chunk, jnp.arange(S // MOBA_QCHUNK))
    out = outs.transpose(1, 2, 0, 3, 4).reshape(B, H, S, hd)
    return out.transpose(0, 2, 1, 3).reshape(B, S, H * hd)

def token_mixer(h, w_in, w_alpha_up, b_alpha, g_head, w_gla_out, w_moba_out, w_o):
    B, S, _ = h.shape
    proj = h @ w_in
    offs = np.cumsum(IN_SIZES)[:-1].tolist()
    gq, gk, gv, gr, ga_low, mq, mk, mv, gate_a, gate_b = jnp.split(proj, offs, axis=-1)
    log_a = jax.nn.log_sigmoid((ga_low @ w_alpha_up + b_alpha).astype(jnp.float32)) / GLA_GATE_TEMP
    o_gla = gla_chunked(gq.reshape(B, S, GLA_HEADS, GLA_DK), gk.reshape(B, S, GLA_HEADS, GLA_DK),
                        gv.reshape(B, S, GLA_HEADS, GLA_DV), log_a.reshape(B, S, GLA_HEADS, GLA_DK))
    o_gla = rmsnorm(o_gla.astype(h.dtype), g_head) * jax.nn.silu(gr.reshape(B, S, GLA_HEADS, GLA_DV))
    y_a = o_gla.reshape(B, S, GLA_V) @ w_gla_out
    o_moba = moba_attention(mq.reshape(B, S, MOBA_HEADS, MOBA_HD), mk.reshape(B, S, MOBA_HEADS, MOBA_HD),
                            mv.reshape(B, S, MOBA_HEADS, MOBA_HD))
    y_b = o_moba @ w_moba_out
    merged = jax.nn.sigmoid(gate_a) * y_a + jax.nn.sigmoid(gate_b) * y_b
    return merged @ w_o

def conv_ffn(h, w_up, w_conv, b_conv, w_down):
    up = h @ w_up
    C = up.shape[-1]
    up = lax.conv_general_dilated(up, w_conv[:, None, :], window_strides=(1,),
                                  padding=[(CONV_WIDTH - 1, 0)],
                                  dimension_numbers=('NWC', 'WIO', 'NWC'),
                                  feature_group_count=C) + b_conv
    u, g = jnp.split(up, 2, axis=-1)
    return (jax.nn.gelu(g) * u) @ w_down

def setup_inputs(seed: int = 0) -> dict:
    key = jax.random.key(seed)
    ks = jax.random.split(key, 20)
    D, L = D_MODEL, DEPTH

    def w(k, shape, fan_in, s=1.0):
        return jax.random.normal(k, shape, jnp.float32) * (s * fan_in ** -0.5)

    def gain(k, shape):
        return 1.0 + 0.05 * jax.random.normal(k, shape, jnp.float32)

    return {
        "x": jax.random.normal(ks[0], (BATCH, SEQ, D), jnp.float32),
        "c": jax.random.normal(ks[1], (BATCH, D), jnp.float32),
        "w_ada": w(ks[2], (L, D, N_MOD * D), D, 0.5),
        "b_ada": 0.02 * jax.random.normal(ks[3], (L, N_MOD * D), jnp.float32),
        "g_pre_mix": gain(ks[4], (L, D)),
        "w_in": w(ks[5], (L, D, IN_WIDTH), D),
        "w_alpha_up": w(ks[6], (L, GLA_RANK, GLA_K), GLA_RANK),
        "b_alpha": 0.1 * jax.random.normal(ks[7], (L, GLA_K), jnp.float32),
        "g_gla_head": gain(ks[8], (L, GLA_DV)),
        "w_gla_out": w(ks[9], (L, GLA_V, D), GLA_V),
        "w_moba_out": w(ks[10], (L, MOBA_W, D), MOBA_W),
        "w_o": w(ks[11], (L, D, D), D),
        "g_post_mix": gain(ks[12], (L, D)),
        "g_pre_ffn": gain(ks[13], (L, D)),
        "w_up": w(ks[14], (L, D, 2 * FFN_DIM), D),
        "w_conv": w(ks[15], (L, CONV_WIDTH, 2 * FFN_DIM), CONV_WIDTH),
        "b_conv": 0.02 * jax.random.normal(ks[16], (L, 2 * FFN_DIM), jnp.float32),
        "w_down": w(ks[17], (L, FFN_DIM, D), FFN_DIM),
        "g_post_ffn": gain(ks[18], (L, D)),
    }

def reference(x, c, w_ada, b_ada, g_pre_mix, w_in, w_alpha_up, b_alpha, g_gla_head,
              w_gla_out, w_moba_out, w_o, g_post_mix, g_pre_ffn, w_up, w_conv, b_conv,
              w_down, g_post_ffn):
    for l in range(DEPTH):
        mod = jax.nn.silu(c) @ w_ada[l] + b_ada[l]
        sh1, sc1, gt1, sh2, sc2, gt2 = (m[:, None, :] for m in jnp.split(mod, N_MOD, axis=-1))
        h = rmsnorm(x, g_pre_mix[l]) * (1.0 + sc1) + sh1
        y = token_mixer(h, w_in[l], w_alpha_up[l], b_alpha[l], g_gla_head[l],
                        w_gla_out[l], w_moba_out[l], w_o[l])
        x = x + gt1 * rmsnorm(y, g_post_mix[l])
        h = rmsnorm(x, g_pre_ffn[l]) * (1.0 + sc2) + sh2
        y = conv_ffn(h, w_up[l], w_conv[l], b_conv[l], w_down[l])
        x = x + gt2 * rmsnorm(y, g_post_ffn[l])
    return x


_drawn_inputs = setup_inputs


def setup_inputs(seed=0):
    import zlib

    import numpy as np

    out = dict(_drawn_inputs(seed))
    spreads = {}
    factors = {'b_alpha': 4.361,
     'g_gla_head': 4.412,
     'g_post_mix': 3.842,
     'g_pre_ffn': 2.85,
     'b_conv': 7.648,
     'g_post_ffn': 4.078}
    for name, (base, spread) in spreads.items():
        noise = np.random.default_rng([zlib.crc32(name.encode()), seed]).standard_normal(out[name].shape)
        drawn = base * np.exp(spread * noise) if base else spread * noise
        out[name] = __import__('jax').numpy.asarray(drawn.astype(out[name].dtype))
    for name, factor in factors.items():
        out[name] = (out[name] * factor).astype(out[name].dtype)
    return out
```

```python
import concourse.bass as bass
from concourse import mybir
from contextlib import ExitStack

F32 = mybir.dt.float32
F32R = mybir.dt.float32r
U8 = mybir.dt.uint8
ALU = mybir.AluOpType
ACT = mybir.ActivationFunctionType
AX = mybir.AxisListType
ds = bass.ds

P = 128
KB = 1024


def layer_kernel(nc, x, c, w_ada, b_ada, g_pre_mix, w_in, w_alpha_up, b_alpha, g_gla_head, w_gla_out,
                 w_moba_out, w_o, g_post_mix, g_pre_ffn, w_up, w_conv, b_conv, w_down, g_post_ffn, out):
    TOK, D = x.shape[1], x.shape[2]
    TT = TOK // P
    KT = D // P
    FFN = w_down.shape[1]
    FT = FFN // P
    RANK, GLA_K = w_alpha_up.shape[1], w_alpha_up.shape[2]
    DV = g_gla_head.shape[1]
    HEADS = GLA_K // P
    GLA_V = HEADS * DV
    MOBA_W = w_moba_out.shape[1]
    EPS = 1e-6
    SCALE = float(P) ** -0.5
    GATE_TEMP = 16.0
    CW = 2048
    C_GQ, C_GK, C_GV = 0, GLA_K, 2 * GLA_K
    C_GR = C_GV + GLA_V
    C_LOW = C_GR + GLA_V
    C_MQ = C_LOW + RANK
    C_MK, C_MV = C_MQ + MOBA_W, C_MQ + 2 * MOBA_W
    C_GA = C_MQ + 3 * MOBA_W
    C_GB = C_GA + D
    assert (TOK, D, TT, KT, DV, HEADS, GLA_V, MOBA_W) == (256, 2048, 2, 16, 256, 4, 1024, 1024)

    HEAD_N, MERGE_N = 12, 6
    A_HEAD, A_MERGE, A_WO = 1, 1 + HEADS * HEAD_N, 1 + HEADS * HEAD_N + 8 * MERGE_N
    UP_ITERS = FFN // 256
    W_UP, W_DOWN = KT, KT + 4 * UP_ITERS
    SLOT4 = [(A_WO + 0) % 3, (A_WO + 1) % 3, (A_WO + 2) % 3, 3]
    ADA_HEAD = [2, 1, 1, 1, 1, 1, 1, 1, 1, 2, 2, 2]
    ADA_MERGE = [2, 2, 2, 1, 1, 0]
    M_SH1, M_SC1, M_GT1, M_SH2, M_SC2, M_GT2 = range(6)

    win = w_in[0].rearrange("(k p) n -> p k n", p=P)
    wup = w_up[0].rearrange("(k p) n -> p k n", p=P)
    wgo = w_gla_out[0].rearrange("(k p) n -> p k n", p=P)
    wmo = w_moba_out[0].rearrange("(k p) n -> p k n", p=P)
    wo = w_o[0].rearrange("(k p) n -> p k n", p=P)
    wdn = w_down[0].rearrange("(k p) n -> p k n", p=P)
    wada = w_ada[0].rearrange("(p t) n -> p t n", t=KT)
    x_v = x[0].rearrange("(t p) d -> p t d", p=P)
    out_v = out[0].rearrange("(t p) d -> p t d", p=P)

    ctx = ExitStack()
    with ctx:
        base = -(-nc.sbuf_base // 64) * 64

        def at(name, kb, shape, dt=F32):
            return nc.alloc_sbuf_tensor_at(name, [P] + shape, dt, offset=base + int(kb * KB))

        def sem(name):
            return ctx.enter_context(nc.semaphore(name))

        raw = at("raw", 0, [4, CW])
        ws = at("ws", 32, [4, 8, 2, 256], F32R)
        hT = at("hT", 96, [KT, 2 * TOK], F32R)
        NCOL = 96 + 66 + 352
        cols = at("cols", 128, [NCOL])
        ident = at("ident", 130.25, [P])
        ones = at("ones", 130.75, [P])
        mods = at("mods", 131.25, [6, KT])
        ccol = at("ccol", 131.625, [KT])
        scol = at("scol", 131.6875, [KT])
        stat = at("stat", 131.75, [48])
        eps = at("eps", 131.9375, [1])
        xnat = at("xnat", 132, [TT, D])
        xn = at("xn", 148, [TT, D])
        junk = at("junk", 80, [D])
        rows = at("rows", 88, [6, P])
        maskf = at("maskf", 91, [8, P])
        acc0 = at("acc0", 180, [2 * D])
        h32 = at("h32", 196, [4, TOK])
        walpha = at("walpha", 203.5, [GLA_K])
        balpha = at("balpha", 205.5, [GLA_K])
        zabs = at("zabs", 180, [TT, GLA_K])
        zmin = at("zmin", 184, [TT, GLA_K])
        loga = at("loga", 188, [TT, GLA_K])
        galow = at("galow", 194, [TOK])
        galow_x = at("galow_x", 195, [TOK])
        og = at("og", 132, [8, 2 * TOK], F32R)
        om = at("om", 148, [8, 2 * TOK], F32R)
        ada = at("ada", 164, [2, 1024])
        acc = at("acc", 172, [D])
        bT = at("bT", 24, [HEADS, TOK])
        bc = at("bc", 28, [TOK])
        eb = at("eb", 29, [2, TOK])
        rs = at("rs", 31, [TOK])
        Mb = at("Mb", 80, [2, TOK])
        A = at("A", 82, [3, P])
        ot = at("ot", 84, [2, TOK])
        sq = at("sq", 86, [2, TOK])
        ssb = at("ssb", 88, [2, 2 * TOK])
        pT = at("pT", 92, [2, 3 * P])
        qk = at("qk", 180, [2, TOK])
        vv = at("vv", 182, [TT, DV])
        grt = at("grt", 184, [2, TOK])
        tg = at("tg", 186, [2, TOK])
        mqk = at("mqk", 188, [2, 2, TOK])
        mv = at("mv", 192, [TT, 256])
        tmp = at("tmp", 196, [2, 2, TOK])
        tri = at("tri", 200, [P])
        causal = at("causal", 200.5, [2 * TOK])
        mask8 = at("mask8", 202.5, [8, P], U8)
        tmp3 = at("tmp3", 24, [2, 2, TOK])
        gx = at("gx", 28, [2, 2, TOK])
        sg = at("sg", 80, [2, 2, TOK])
        ya = at("ya", 84, [2, TOK])
        yb = at("yb", 86, [2, TOK])
        mT = at("mT", 180, [KT, TOK])
        G = at("G", 196, [D])
        x2 = at("x2", 132, [TT, D])
        yt = at("yt", 148, [TT, D])
        junk2 = at("junk2", 164, [D])
        h32b = at("h32b", 188, [4, TOK])
        dg2 = at("dg2", 172, [D])
        aT = at("aT", 148, [FT, TOK])
        cv = at("cv", 192, [2, TOK])
        ub = at("ub", 194, [2, TOK])
        up = at("up", 204, [2, TOK + 2])
        asp = at("asp", 96, [4, 2 * TOK], F32R)
        yo = at("yo", 104, [TT, D])
        junk3 = at("junk3", 120, [D])
        ps = ctx.enter_context(nc.psum_tensor("ps", [P, 8, 512], F32))

        COL_BADA, COL_PRE1, COL_POST1, COL_PRE2, COL_POST2, COL_GH, COL_CONV = 0, 96, 112, 128, 144, 160, 162
        COL_CB = COL_CONV + 3 * 2 * FT

        c_in, x_in, rows_in, gate_in, xr_in = sem("c_in"), sem("x_in"), sem("rows_in"), sem("gate_in"), sem("xr_in")
        head_in = [sem(f"head_in{i}") for i in range(4)]
        raw3_in = [sem(f"raw3_in{i}") for i in range(3)]
        raw4_in = [sem(f"raw4_in{i}") for i in range(4)]
        ada_in = [sem(f"ada_in{i}") for i in range(2)]
        head_used = sem("head_used")
        ada_used = sem("ada_used")
        hi3, split3, used3 = sem("hi3"), sem("split3"), sem("used3")
        hi4, split4, used4 = sem("hi4"), sem("split4"), sem("used4")
        pool_step = sem("pool_step")
        dve_step, act_step = sem("dve_step"), sem("act_step")
        scol_ready, xsq, xsqrt, xn_ready = sem("scol_ready"), sem("xsq"), sem("xsqrt"), sem("xn_ready")
        colsT, cols_ready = sem("colsT"), sem("cols_ready")
        mod_done, mods_ready, acc_zero = sem("mod_done"), sem("mods_ready"), sem("acc_zero")
        xT_done, h_even, h_odd, h_hi, h_ready = sem("xT_done"), sem("h_even"), sem("h_odd"), sem("h_hi"), sem("h_ready")
        z_done, z_abs, z_ln, la_ready, tri_done, bT_ready = (sem("z_done"), sem("z_abs"), sem("z_ln"),
                                                             sem("la_ready"), sem("tri_done"), sem("bT_ready"))
        low_x, low_ready = sem("low_x"), sem("low_ready")
        cross, evac = sem("cross"), sem("evac")
        e_ready, exp_done, level_ready, gram_done = sem("e_ready"), sem("exp_done"), sem("level_ready"), sem("gram_done")
        select_done, a01_done, av_done, ot_done, sq_done, ss_done = (sem("select_done"), sem("a01_done"), sem("av_done"),
                                                                     sem("ot_done"), sem("sq_done"), sem("ss_done"))
        rs_done, tanh_done, og_f, og_hi, og_ready = sem("rs_done"), sem("tanh_done"), sem("og_f"), sem("og_hi"), sem("og_ready")
        qk_done, nb_ready, p_ready, pn_ready, pt_done, ptc_done, pv_done, om_hi, om_ready = (
            sem("qk_done"), sem("nb_ready"), sem("p_ready"), sem("pn_ready"), sem("pt_done"), sem("ptc_done"),
            sem("pv_done"), sem("om_hi"), sem("om_ready"))
        cross3, evac3, sig_done = sem("cross3"), sem("evac3"), sem("sig_done")
        dg_ready, g_done, g_ready = sem("dg_ready"), sem("g_done"), sem("g_ready")
        m_done, m_hi, m_ready = sem("m_done"), sem("m_hi"), sem("m_ready")
        ysq, ysqrt, x2_ready = sem("ysq"), sem("ysqrt"), sem("x2_ready")
        cross5, up_ready, cb_done, conv_g, gelu_done = (sem("cross5"), sem("up_ready"), sem("cb_done"), sem("conv_g"),
                                                        sem("gelu_done"))
        conv_done = sem("conv_done")
        a_hi, a_ready = sem("a_hi"), sem("a_ready")
        out_ready, out_done = sem("out_ready"), sem("out_done")

        block = ctx.enter_context(nc.Block())

        def raw_blocks(slot):
            return raw[:, slot, :].rearrange("p (b n) -> p b n", n=256)

        def arrived4(w, k):
            return (w - k) // 4 + (1 if k == 3 else 0)

        @block.sync
        def _(sp):
            def load(slot, arrival, src, lo, hi, n):
                dst = raw[:, slot, :].rearrange("p (b n) -> p b n", n=n)
                sp.dma_start(dst[:, lo:hi, :], src).then_inc(arrival, 16)

            def load_k(slot, arrival, w, kh, col, n=256, step=8):
                h = step // 2
                for j in (1, 0):
                    load(slot, arrival, w[:, step * kh + h * j:step * kh + h * (j + 1), ds(col, n)], h * j, h * (j + 1), n)

            def load_row(slot, arrival, w, kt):
                for j in range(2):
                    sp.dma_start(raw[:, slot, 1024 * j:1024 * (j + 1)], w[:, kt, 1024 * j:1024 * (j + 1)]).then_inc(arrival, 16)

            with sp.Fori(0, KT // 2) as i:
                for j in range(4):
                    sp.wait_ge(head_used, 4 * i + j + 1)
                    sp.dma_start(raw[:, j, :], wada[:, ds(2 * i + j // 2, 1), (j % 2) * D:(j % 2 + 1) * D]).then_inc(head_in[j], 16)
            sp.wait_ge(head_used, 4 + 31)
            load_k(0, raw3_in[0], win, 0, C_LOW, n=P, step=16)
            for half in range(2):
                with sp.Fori(0, 2) as i:
                    I = i + 2 * half
                    for n in range(HEAD_N):
                        slot, arrival, kh = (1 + n) % 3, raw3_in[(1 + n) % 3], n % 2
                        sp.wait_ge(split3, HEAD_N * I + A_HEAD + n + 1)
                        if n < 2:
                            dst = raw[:, slot, :].rearrange("p (k two n) -> p k two n", two=2, n=P)
                            for j, col in enumerate((C_GQ, C_GK)):
                                sp.dma_start(dst[:, :, j, :], win[:, 8 * kh:8 * kh + 8, ds(I * P + col, P)]).then_inc(arrival, 16)
                        else:
                            col = (C_GV, C_MQ, C_MK, C_MV, C_GR)[n // 2 - 1]
                            load_k(slot, arrival, win, kh, I * 256 + col)
            for half in range(2):
                with sp.Fori(0, 4) as i:
                    J = i + 4 * half
                    for n in range(MERGE_N):
                        slot, arrival = (1 + n) % 3, raw3_in[(1 + n) % 3]
                        sp.wait_ge(split3, MERGE_N * J + A_MERGE + n + 1)
                        if n < 4:
                            load_k(slot, arrival, win, n % 2, J * 256 + (C_GA if n < 2 else C_GB))
                        else:
                            load_k(slot, arrival, wgo if n == 4 else wmo, 0, J * 256)
            for w in range(KT):
                k = w % 4
                if w < 3:
                    sp.wait_ge(split3, A_WO + w + 1)
                    load_row(SLOT4[k], raw3_in[SLOT4[k]], wo, w)
                else:
                    if w in (4, 5, 6):
                        sp.wait_ge(split3, 3 + A_WO + w - 4 + 1)
                    if w >= 7:
                        sp.wait_ge(split4, w - 6)
                    if w == 3:
                        sp.wait_ge(evac3, 8 + 8 * 8)
                        sp.wait_ge(sig_done, 16)
                    load_row(SLOT4[k], raw4_in[k], wo, w)
                if w == 6:
                    sp.wait_ge(used3, A_WO)
                    sp.dma_start(x2[:, :, :], x_v).then_inc(xr_in, 16)
            with sp.Fori(0, UP_ITERS) as i:
                for n in range(4):
                    sp.wait_ge(split4, 4 * i + W_UP + n - 6)
                    load_k(SLOT4[n], raw4_in[n], wup, n % 2, i * 256 + (FFN if n >= 2 else 0))
            with sp.Fori(0, FT // 4) as i:
                for n in range(4):
                    sp.wait_ge(split4, 4 * i + W_DOWN + n - 6)
                    for j in range(2):
                        sp.dma_start(raw[:, SLOT4[n], 1024 * j:1024 * (j + 1)],
                                     wdn[:, ds(4 * i + n, 1), 1024 * j:1024 * (j + 1)]).then_inc(raw4_in[n], 16)
            for tt in range(TT):
                sp.wait_ge(out_ready, tt + 1)
                sp.dma_start(out_v[:, tt, :], yo[:, tt, :]).then_inc(out_done, 16)
            sp.wait_ge(out_done, 16 * TT)

        @block.gpsimd
        def _(pool):
            step = [0]

            def made(ins):
                step[0] += 1
                ins.then_inc(pool_step, 1)
                pool.wait_ge(pool_step, step[0])

            made(pool.memset(ones[:, :], 1.0))
            made(pool.memset(eps[:, :], EPS))
            made(pool.memset(ident[:, :], 0.0))
            made(pool.affine_select(out=ident[:, :], in_=ident[:, :], compare_op=ALU.not_equal, fill=1.0, base=0,
                                    pattern=[[-1, P]], channel_multiplier=1))
            made(pool.memset(maskf[:, 0, :], 0.0))
            made(pool.memset(tri[:, :], 1.0 / GATE_TEMP))
            made(pool.affine_select(out=tri[:, :], in_=tri[:, :], compare_op=ALU.is_ge, fill=0.0, base=0,
                                    pattern=[[1, P]], channel_multiplier=-1))
            made(pool.memset(causal[:, :], 0.0))
            cv4 = causal[:, :].rearrange("p (t k) -> p t k", t=TT)
            made(pool.affine_select(out=cv4, in_=cv4, compare_op=ALU.is_ge, fill=-1e30, base=0,
                                    pattern=[[P, TT], [-1, TOK]], channel_multiplier=1))
            for lv in range(1, 8):
                s = 2 ** (lv - 1)
                m = maskf[:, lv, :].rearrange("p (g two s) -> p g two s", two=2, s=s)
                made(pool.memset(maskf[:, lv, :], 0.0))
                made(pool.memset(m[:, :, 1, :], 1.0))
                m2 = maskf[:, lv, :].rearrange("p (g r) -> p g r", r=2 * s)
                made(pool.affine_select(out=m2, in_=m2, compare_op=ALU.is_ge, fill=0.0, base=0,
                                        pattern=[[-2 * s, P // (2 * s)], [0, 2 * s]], channel_multiplier=1))
                made(pool.affine_select(out=m2, in_=m2, compare_op=ALU.is_ge, fill=0.0, base=s - 1,
                                        pattern=[[2 * s, P // (2 * s)], [0, 2 * s]], channel_multiplier=-1))
            made(pool.affine_select(out=maskf[:, 0, :], in_=maskf[:, 0, :], compare_op=ALU.not_equal, fill=1.0, base=0,
                                    pattern=[[-1, P]], channel_multiplier=1))
            for m, vector in enumerate((M_GT2, M_GT1, M_SC2, M_SH2)):
                with pool.Fori(0, KT) as t:
                    for s in range(2):
                        pool.wait_ge(ada_used, 2 * t + (2 * KT * m + s + 1))
                        pool.dma_start(ada[:, s, :], wada[:, ds(t, 1), vector * D + 1024 * s:vector * D + 1024 * (s + 1)]).then_inc(ada_in[s], 16)

        @block.scalar
        def _(act):
            steps = [0]

            def link(ins):
                steps[0] += 1
                ins.then_inc(act_step, 1)
                act.wait_ge(act_step, steps[0])

            def split_hi(slot, hi):
                act.activation(ws[:, slot, :, 0, :], raw_blocks(slot), ACT.Copy).then_inc(hi, 1)

            def split3_hi(n, group, need):
                act.wait_ge(raw3_in[n % 3], group * 32 + 32)
                if need is not None:
                    act.wait_ge(used3, need)
                split_hi(n % 3, hi3)

            def split4_hi(k, group, need, sem_used=used4):
                act.wait_ge(raw4_in[k], group * 32)
                if need is not None:
                    act.wait_ge(sem_used, need)
                split_hi(SLOT4[k], hi4)

            def norm_factor(n, srcs, junk_, col, count, done, rooted):
                for i in range(n):
                    act.activation(junk_, srcs[i], ACT.Square, accum_out=stat[:, col + i:col + i + 1]).then_inc(done, 1)

            def to_h(first, hb, sc, sh, need_free):
                for kt in range(KT):
                    n = first * KT + kt
                    if kt % 2 == 0:
                        act.wait_ge(xT_done, n + 1)
                        if kt >= 4:
                            act.wait_ge(h_ready, n - 3)
                        act.activation(hb[:, kt % 4, :], ps[:, 4 + kt % 4, 0:TOK], ACT.Identity,
                                       bias=mods[:, sh, kt:kt + 1], scale=mods[:, sc, kt:kt + 1]).then_inc(h_even, 1)
                        act.wait_ge(h_even, n // 2 + 1)
                    else:
                        act.wait_ge(h_odd, n // 2 + 1)
                    act.activation(hT[:, kt, 0:TOK], hb[:, kt % 4, :], ACT.Copy).then_inc(h_hi, 1)

            act.dma_start(ccol[:, :], c[0].rearrange("(p t) -> p t", t=KT)).then_inc(c_in, 16)
            act.dma_start(xnat[:, :, :], x_v).then_inc(x_in, 16)
            act.dma_start(rows[0:96, 0, :], b_ada[0].rearrange("(r p) -> r p", p=P)).then_inc(rows_in, 16)
            for j, g in enumerate((g_pre_mix, g_post_mix, g_pre_ffn, g_post_ffn)):
                act.dma_start(rows[KT * j:KT * (j + 1), 1, :], g[0].rearrange("(r p) -> r p", p=P)).then_inc(rows_in, 16)
            act.dma_start(rows[64:66, 1, :], g_gla_head[0].rearrange("(r p) -> r p", p=P)).then_inc(rows_in, 16)
            for j in range(3):
                act.dma_start(rows[0:2 * FT, 2 + j, :], w_conv[0, j].rearrange("(r p) -> r p", p=P)).then_inc(rows_in, 16)
            act.dma_start(rows[0:2 * FT, 5, :], b_conv[0].rearrange("(r p) -> r p", p=P)).then_inc(rows_in, 16)
            act.dma_start(walpha[0:RANK, :], w_alpha_up[0]).then_inc(gate_in, 16)
            act.dma_start(balpha[0:1, :], b_alpha).then_inc(gate_in, 16)
            act.wait_ge(c_in, 16)
            act.activation(scol[:, :], ccol[:, :], ACT.Silu).then_inc(scol_ready, 1)
            act.wait_ge(x_in, 16)
            act.wait_ge(pool_step, 2)
            for tt in range(TT):
                act.activation(junk[:, :], xnat[:, tt, :], ACT.Square, accum_out=stat[:, tt:tt + 1]).then_inc(xsq, 1)
                act.wait_ge(xsq, tt + 1)
            act.activation(stat[:, 2:4], stat[:, 0:2], ACT.Sqrt, scale=1.0 / D, bias=eps[:, :]).then_inc(xsqrt, 1)
            act.wait_ge(mods_ready, 1)
            to_h(0, h32, M_SC1, M_SH1, None)
            for n in range(3):
                split3_hi(n, 0, None)

            act.wait_ge(used3, 1)
            act.activation(galow_x[0:RANK, :], ps[0:RANK, 6, TOK:2 * TOK], ACT.Copy).then_inc(low_x, 1)
            split3_hi(0, 1, 1)
            act.wait_ge(z_done, 1)
            act.activation(zabs[:, :, :], ps[:, 4:6, :], ACT.Abs).then_inc(z_abs, 1)
            act.wait_ge(z_abs, 1)
            link(act.activation(zabs[:, :, :], zabs[:, :, :], ACT.Exp, scale=-1.0))
            act.activation(zabs[:, :, :], zabs[:, :, :], ACT.Ln, bias=1.0).then_inc(z_ln, 1)

            for half in range(2):
                with act.Fori(0, 2) as i:
                    I = i + 2 * half
                    for n in range(HEAD_N):
                        a = HEAD_N * I + A_HEAD + n
                        split3_hi(1 + n, 4 * I + (1 + n + 3) // 3, a + 1)
                        if n % 2 == 1:
                            g = n // 2
                            b = 2 * (g % 2)
                            act.wait_ge(evac, 12 * I + 2 * g + 2)
                            if g == 0:
                                act.activation(tmp[:, 0, 0, :], ps[:, 0, TOK:], ACT.Copy, scale=SCALE).then_inc(cross, 1)
                                act.activation(tmp[:, 0, 1, :], ps[:, 1, TOK:], ACT.Copy).then_inc(cross, 1)
                            else:
                                act.activation(tmp[:, g % 2, :, :], ps[:, b:b + 2, TOK:], ACT.Copy).then_inc(cross, 1)
                        for p in ((0, 1) if n == 1 else (n,) if 2 <= n <= 7 else ()):
                            act.wait_ge(e_ready, 8 * I + p + 1)
                            act.activation(eb[:, p % 2, :], eb[:, p % 2, :], ACT.Exp).then_inc(exp_done, 1)
                        if n == 3:
                            act.wait_ge(gram_done, 9 * I + 2)
                            act.activation(A[:, 1, :], ps[:, 5, 0:P], ACT.Copy).then_inc(a01_done, 1)
                        if n == 8:
                            act.wait_ge(nb_ready, I + 1)
                            for hd in range(2):
                                for qt in range(TT):
                                    v = ssb[:, hd, TOK * qt:TOK * (qt + 1)]
                                    j = 2 * hd + qt
                                    act.activation(v, v, ACT.Exp, scale=SCALE, bias=stat[:, 20 + j:21 + j],
                                                   accum_out=stat[:, 24 + j:25 + j]).then_inc(p_ready, 1)
                        if n == 10:
                            for hd in range(2):
                                act.wait_ge(pt_done, 2 * I + hd + 1)
                                act.activation(pT[:, hd, :], ps[:, 6 + hd, 0:3 * P], ACT.Copy).then_inc(ptc_done, 1)
                            act.wait_ge(av_done, I + 1)
                            act.activation(ot[:, :, :], ps[:, 4, :].rearrange("p (e t) -> p e t", e=2), ACT.Copy).then_inc(ot_done, 1)
                            act.activation(sq[:, :, :], ps[:, 4, :].rearrange("p (e t) -> p e t", e=2), ACT.Square).then_inc(sq_done, 1)
                        if n == 11:
                            act.wait_ge(pv_done, I + 1)
                            act.activation(om[:, ds(2 * I, 2), 0:TOK], ps[:, 6:8, 0:TOK], ACT.Copy).then_inc(om_hi, 1)
                            act.wait_ge(ss_done, I + 1)
                            act.activation(rs[:, :], ps[:, 5, 0:TOK], ACT.Sqrt, scale=1.0 / DV, bias=eps[:, :]).then_inc(rs_done, 1)
                            act.wait_ge(evac, 12 * I + 12 + 4)
                            act.activation(tg[:, :, :], grt[:, :, :], ACT.Tanh, scale=0.5).then_inc(tanh_done, 1)
                            act.wait_ge(og_f, I + 1)
                            act.activation(og[:, ds(2 * I, 2), 0:TOK], ot[:, :, :], ACT.Copy).then_inc(og_hi, 1)

            for half in range(2):
                with act.Fori(0, 4) as i:
                    J = i + 4 * half
                    for n in range(MERGE_N):
                        a = MERGE_N * J + A_MERGE + n
                        split3_hi(1 + n, 2 * J + 16 + (1 + n + 3) // 3, a + 1)
                        if n in (1, 3, 4, 5):
                            g = {1: 0, 3: 1, 4: 2, 5: 3}[n]
                            act.wait_ge(evac3, 8 * J + 2 * g + 6)
                            act.activation(tmp3[:, g % 2, :, :], ps[:, 2 * g:2 * g + 2, TOK:], ACT.Copy).then_inc(cross3, 1)
                            if g < 2:
                                act.wait_ge(evac3, 8 * J + 2 * (g + 1) + 8)
                                act.activation(sg[:, g, :, :], gx[:, g, :, :], ACT.Sigmoid).then_inc(sig_done, 1)
                if half == 0:
                    act.wait_ge(g_done, 1)
                    act.activation(G[:, :], ps[:, 0:4, :].rearrange("p b n -> p (b n)"), ACT.Copy).then_inc(g_ready, 1)

            def merged_hi(kt):
                act.activation(hT[:, kt, 0:TOK], mT[:, kt, :], ACT.Copy).then_inc(m_hi, 1)

            act.wait_ge(m_done, 8)
            act.wait_ge(used3, A_WO)
            for kt in range(4):
                merged_hi(kt)
            split4_hi(3, 1, None)
            for w in range(4, KT + 4):
                if w < 7:
                    split4_hi(w % 4, w // 4, A_WO + w - 4 + 1, used3)
                else:
                    split4_hi(w % 4, arrived4(w, w % 4), w - 6)
                if w < KT:
                    merged_hi(w)

            act.wait_ge(used4, KT - 3)
            for j in range(8):
                act.activation(junk2[:, 0:512], ps[:, j, :], ACT.Square, accum_out=stat[:, 32 + j:33 + j]).then_inc(ysq, 1)
                act.wait_ge(ysq, j + 1)
            act.wait_ge(ysqrt, 1)
            act.activation(stat[:, 4:6], stat[:, 4:6], ACT.Sqrt, scale=1.0 / D, bias=eps[:, :]).then_inc(ysqrt, 1)
            for tt in range(TT):
                act.wait_ge(x2_ready, tt + 1)
                act.activation(junk2[:, :], x2[:, tt, :], ACT.Square, accum_out=stat[:, 6 + tt:7 + tt]).then_inc(xsq, 1)
                act.wait_ge(xsq, TT + tt + 1)
            act.activation(stat[:, 6:8], stat[:, 6:8], ACT.Sqrt, scale=1.0 / D, bias=eps[:, :]).then_inc(xsqrt, 1)
            act.wait_ge(g_done, 2)
            act.activation(G[:, :], ps[:, 0:4, :].rearrange("p b n -> p (b n)"), ACT.Copy).then_inc(g_ready, 1)
            to_h(1, h32b, M_SC2, M_SH2, None)

            def up_tasks(i, n):
                g = (n - 1) // 2
                q = 2 * i + g
                act.wait_ge(used4, 4 * i + W_UP + n - 2)
                act.wait_ge(conv_done, q + 2)
                act.activation(cv[:, :, :], ps[:, 2 * g:2 * g + 2, TOK:], ACT.Copy).then_inc(cross5, 1)
                act.wait_ge(up_ready, q + 1)
                for ct in range(2):
                    f = 2 * i + FT * g + ct
                    act.activation(cv[:, ct, :], up[:, ct, 2:], ACT.Identity, scale=cols[:, ds(f + COL_CONV + 4 * FT, 1)],
                                   bias=cols[:, ds(f + COL_CB, 1)]).then_inc(cb_done, 1)
                if g == 1:
                    act.wait_ge(conv_g, i + 1)
                    act.activation(cv[:, :, :], cv[:, :, :], ACT.Gelu_apprx_tanh).then_inc(gelu_done, 1)

            with act.Fori(0, UP_ITERS) as i:
                for n in range(4):
                    split4_hi(n, i + (W_UP + 4) // 4 + (n == 3), 4 * i + W_UP + n + 4 - 6)
                    if n % 2 == 1:
                        up_tasks(i, n)

            def act_hi(kt, k, need):
                if need is not None:
                    act.wait_ge(used4, need)
                act.activation(asp[:, k, 0:TOK], aT[:, ds(kt, 1), :], ACT.Copy).then_inc(a_hi, 1)

            act.wait_ge(conv_done, 2 + 2 * UP_ITERS)
            act.wait_ge(used4, W_DOWN - 3)
            for k in range(4):
                act_hi(k, k, None)
            with act.Fori(0, FT // 4 - 1) as i:
                for n in range(4):
                    act_hi(4 * i + 4 + n, n, 4 * i + W_DOWN + n + 4 - 6)
                    split4_hi(n, i + (W_DOWN + 4) // 4 + (n == 3), 4 * i + W_DOWN + n + 4 - 6)
            act.wait_ge(used4, W_DOWN + FT - 3)
            for j in range(8):
                act.activation(junk3[:, 0:512], ps[:, j, :], ACT.Square, accum_out=stat[:, 32 + j:33 + j]).then_inc(ysq, 1)
                act.wait_ge(ysq, 8 + j + 1)
            act.wait_ge(ysqrt, 3)
            act.activation(stat[:, 4:6], stat[:, 4:6], ACT.Sqrt, scale=1.0 / D, bias=eps[:, :]).then_inc(ysqrt, 1)

        @block.vector
        def _(dve):
            steps = [0]

            class Loop:
                def __init__(self, base, i=None, size=0):
                    self.base, self.i, self.size, self.k = base, i, size, 0

                def link(self, ins, wait=True):
                    ins.then_inc(dve_step, 1)
                    self.k += 1
                    if wait:
                        self.wait()

                def wait(self):
                    if self.i is None:
                        dve.wait_ge(dve_step, self.base + self.k)
                    else:
                        dve.wait_ge(dve_step, self.i * self.size + (self.base + self.k))

            S = Loop(0)
            link = S.link

            def split_lo(slot, hi, need, done):
                dve.wait_ge(hi, need)
                dve.tensor_tensor(ws[:, slot, :, 1, :], raw_blocks(slot), ws[:, slot, :, 0, :].bitcast(F32),
                                  ALU.subtract).then_inc(done, 1)

            def accumulate(u, s, arrivals, t):
                dve.wait_ge(ada_in[s], arrivals * 16 + 16)
                dve.wait_ge(ada_used, u + 1)
                v = acc[:, 1024 * s:1024 * (s + 1)]
                dve.scalar_tensor_tensor(v, ada[:, s, :], scol[:, ds(t, 1)], v, ALU.mult, ALU.add).then_inc(ada_used, 1)

            def to_h(first, hb, sc, sh):
                for kt in range(KT):
                    n = first * KT + kt
                    if kt % 2 == 1:
                        dve.wait_ge(xT_done, n + 1)
                        dve.tensor_scalar(hb[:, kt % 4, :], ps[:, 4 + kt % 4, 0:TOK], mods[:, sc, kt:kt + 1],
                                          mods[:, sh, kt:kt + 1], ALU.mult, ALU.add).then_inc(h_odd, 1)
                    dve.wait_ge(h_hi, n + 1)
                    dve.tensor_tensor(hT[:, kt, TOK:2 * TOK], hb[:, kt % 4, :], hT[:, kt, 0:TOK].bitcast(F32),
                                      ALU.subtract).then_inc(h_ready, 1)

            def zero_acc(times):
                dve.memset(acc[:, :], 0.0).then_inc(acc_zero, 1)
                dve.wait_ge(acc_zero, times)

            dve.memset(acc0[:, :], 0.0).then_inc(head_used, 4)
            dve.memset(acc[:, :], 0.0).then_inc(ada_used, 2)
            dve.memset(stat[:, 8:9], 0.0).then_inc(split3, 3)
            dve.memset(stat[:, 9:10], 0.0).then_inc(evac, 4)
            dve.memset(stat[:, 10:11], 0.0).then_inc(evac3, 8)
            dve.memset(stat[:, 11:12], 0.0).then_inc(conv_done, 2)
            dve.wait_ge(scol_ready, 1)

            def head_units(lo, hi):
                with dve.Fori(lo, hi) as i:
                    for j in range(4):
                        dve.wait_ge(head_in[j], i * 16 + 16)
                        dve.wait_ge(head_used, 4 * i + j + 3)
                        v = acc0[:, (j % 2) * D:(j % 2 + 1) * D]
                        dve.scalar_tensor_tensor(v, raw[:, j, :], scol[:, ds(2 * i + j // 2, 1)], v,
                                                 ALU.mult, ALU.add).then_inc(head_used, 1)

            head_units(0, 3)
            dve.wait_ge(colsT, 1)
            link(dve.tensor_copy(cols[:, 0:426], ps[:, 0, 0:426]), wait=False)
            link(dve.tensor_copy(cols[:, 426:NCOL], ps[:, 1, 0:NCOL - 426]))
            link(dve.tensor_scalar(cols[:, COL_GH:COL_GH + 2], cols[:, COL_GH:COL_GH + 2], 0.5, None, ALU.mult), wait=False)
            dve.wait_ge(pool_step, 38)
            link(dve.tensor_copy(mask8[:, :, :], maskf[:, :, :]), wait=False)
            dve.wait_ge(xsqrt, 1)
            link(dve.reciprocal(stat[:, 2:4], stat[:, 2:4]))
            for tt in range(TT):
                dve.tensor_scalar(xn[:, tt, :], xnat[:, tt, :], stat[:, 2 + tt:3 + tt], None, ALU.mult).then_inc(xn_ready, 1)
            head_units(3, KT // 2)

            dve.wait_ge(mod_done, 1)
            link(dve.tensor_tensor(mods[:, M_SH1:M_SC1 + 1, :], ps[:, 2, 0:2 * KT].rearrange("p (m k) -> p m k", m=2),
                                   cols[:, 0:2 * KT].rearrange("p (m k) -> p m k", m=2), ALU.add))
            dve.scalar_tensor_tensor(mods[:, M_SC1, :], mods[:, M_SC1, :], 1.0, cols[:, COL_PRE1:COL_PRE1 + KT],
                                     ALU.add, ALU.mult).then_inc(mods_ready, 1)
            to_h(0, h32, M_SC1, M_SH1)
            for n in range(3):
                split_lo(n, hi3, n + 1, split3)

            dve.wait_ge(low_x, 1)
            dve.tensor_tensor(galow[0:RANK, :], ps[0:RANK, 6, 0:TOK], galow_x[0:RANK, :], ALU.add).then_inc(low_ready, 1)
            split_lo(0, hi3, 4, split3)
            dve.wait_ge(z_abs, 1)
            link(dve.tensor_scalar(zmin[:, :, :], ps[:, 4:6, :], 0.0, None, ALU.min))
            dve.wait_ge(z_ln, 1)
            dve.tensor_tensor(loga[:, :, :], zmin[:, :, :], zabs[:, :, :], ALU.subtract).then_inc(la_ready, 1)
            dve.wait_ge(tri_done, 1)
            dve.tensor_copy(bT[:, :, :].rearrange("p h t -> p (h t)"), ps[:, 6:8, :].rearrange("p b n -> p (b n)")).then_inc(bT_ready, 1)
            dve.wait_ge(bT_ready, 1)

            def level_decay(L, I, p):
                s = P if p == 0 else 2 ** (p - 1)
                v = bc[:, :].rearrange("p (g two s) -> p g two s", two=2, s=s)
                e = eb[:, p % 2, :].rearrange("p (g two s) -> p g two s", two=2, s=s)
                grp = TOK // (2 * s)
                ref = v[:, :, 0, s - 1:s].to_broadcast([P, grp, s])
                if p >= 2:
                    dve.wait_ge(level_ready, 8 * I + p - 1)
                dve.tensor_tensor(e[:, :, 0, :], ref, v[:, :, 0, :], ALU.subtract)
                if p == 0:
                    last = dve.tensor_copy(e[:, :, 1, :], v[:, :, 1, :])
                else:
                    last = dve.tensor_tensor(e[:, :, 1, :], v[:, :, 1, :], ref, ALU.subtract)
                last.then_inc(e_ready, 1)

            def level_operands(I, p):
                s = P if p == 0 else 2 ** (p - 1)
                def halves(t):
                    return t.rearrange("p (g two s) -> p g two s", two=2, s=s)
                e, m = halves(eb[:, p % 2, :]), halves(Mb[:, p % 2, :])
                dve.wait_ge(exp_done, 8 * I + p + 1)
                if p >= 2:
                    dve.wait_ge(gram_done, 9 * I + p)
                dve.tensor_tensor(m[:, :, 0, :], halves(qk[:, 1, :])[:, :, 0, :], e[:, :, 0, :], ALU.mult)
                dve.tensor_tensor(m[:, :, 1, :], halves(qk[:, 0, :])[:, :, 1, :], e[:, :, 1, :], ALU.mult).then_inc(level_ready, 1)

            def before_select(I, lv):
                if lv:
                    dve.wait_ge(select_done, 8 * I + lv)
                dve.wait_ge(gram_done, 9 * I + (1 if lv == 0 else lv + 2))

            def select(I, lv):
                bank = 4 if lv == 0 or lv % 2 else 5
                dve.copy_predicated(A[:, 0:3:2, :], mask8[:, lv, :].unsqueeze(1).to_broadcast([P, 2, P]),
                                    ps[:, bank, 0:TOK].rearrange("p (t i) -> p t i", t=2)).then_inc(select_done, 1)

            def evacuate(I, g, dst):
                b = 2 * (g % 2)
                dve.wait_ge(cross, 7 * I + g + 2)
                dve.tensor_tensor(dst, ps[:, b:b + 2, 0:TOK], tmp[:, g % 2, :, :], ALU.add).then_inc(evac, 2)

            HEAD_STEPS = 10
            for half in range(2):
                start = S.base + S.k
                with dve.Fori(0, 2) as i:
                    I = i + 2 * half
                    L = Loop(start, i, HEAD_STEPS)
                    u = 0
                    for n in range(HEAD_N):
                        a = HEAD_N * I + A_HEAD + n
                        split_lo((1 + n) % 3, hi3, a + 3 + 1, split3)
                        for _u in range(ADA_HEAD[n]):
                            accumulate(16 * I + u, u % 2, 8 * I + u // 2, 8 * i + u // 2)
                            u += 1
                        if n == 0:
                            L.link(dve.tensor_copy(bc[:, :], bT[:, ds(I, 1), :]), wait=False)
                        if n == 1:
                            dve.wait_ge(cross, 7 * I + 1)
                            dve.scalar_tensor_tensor(qk[:, 0, :], ps[:, 0, 0:TOK], SCALE, tmp[:, 0, 0, :],
                                                     ALU.mult, ALU.add).then_inc(evac, 1)
                            dve.wait_ge(cross, 7 * I + 2)
                            dve.tensor_tensor(qk[:, 1, :], ps[:, 1, 0:TOK], tmp[:, 0, 1, :], ALU.add).then_inc(evac, 1)
                            dve.wait_ge(dve_step, i * HEAD_STEPS + (start + 1))
                            level_decay(L, I, 0)
                            level_decay(L, I, 1)
                        if n == 2:
                            L.link(dve.memset(A[:, 0:3:2, :], 0.0))
                            dve.wait_ge(evac, 12 * I + 2 + 4)
                            before_select(I, 0)
                            level_operands(I, 0)
                            select(I, 0)
                            level_operands(I, 1)
                            level_decay(L, I, 2)
                        if 3 <= n <= 8:
                            before_select(I, n - 2)
                            level_operands(I, n - 1)
                            select(I, n - 2)
                            if n <= 7:
                                level_decay(L, I, n)
                        if n == 3:
                            evacuate(I, 1, vv[:, :, :])
                        if n == 5:
                            evacuate(I, 2, mqk[:, 0, :, :])
                        if n == 7:
                            evacuate(I, 3, mqk[:, 1, :, :])
                        if n == 9:
                            before_select(I, 7)
                            evacuate(I, 4, mv[:, :, :])
                            select(I, 7)
                        if n == 8:
                            for hd in range(2):
                                dve.wait_ge(qk_done, 2 * I + hd + 1)
                                L.link(dve.tensor_tensor(ssb[:, hd, :], ps[:, 6 + hd, :], causal[:, :], ALU.add))
                                L.link(dve.reduce_max(stat[:, 16 + 2 * hd:18 + 2 * hd],
                                                      ssb[:, hd, :].rearrange("p (t k) -> p t k", t=TT), AX.X))
                            dve.tensor_scalar(stat[:, 20:24], stat[:, 16:20], -SCALE, None, ALU.mult).then_inc(nb_ready, 1)
                        if n == 9:
                            dve.wait_ge(p_ready, 4 * I + 4)
                            L.link(dve.reciprocal(stat[:, 28:32], stat[:, 24:28]))
                            for hd in range(2):
                                for qt in range(TT):
                                    v = ssb[:, hd, TOK * qt:TOK * (qt + 1)]
                                    j = 28 + 2 * hd + qt
                                    ins = dve.tensor_scalar(v, v, stat[:, j:j + 1], None, ALU.mult)
                                ins.then_inc(pn_ready, 1)
                        if n == 11:
                            evacuate(I, 5, grt[:, :, :])
                            dve.wait_ge(om_hi, I + 1)
                            dve.tensor_tensor(om[:, ds(2 * I, 2), TOK:], ps[:, 6:8, 0:TOK],
                                              om[:, ds(2 * I, 2), 0:TOK].bitcast(F32), ALU.subtract).then_inc(om_ready, 1)
                            dve.wait_ge(rs_done, I + 1)
                            L.link(dve.reciprocal(rs[:, :], rs[:, :]))
                            dve.wait_ge(ot_done, I + 1)
                            L.link(dve.tensor_tensor(ot[:, :, :], ot[:, :, :], rs[:, :].unsqueeze(1).to_broadcast([P, 2, TOK]), ALU.mult), wait=False)
                            dve.wait_ge(tanh_done, I + 1)
                            L.link(dve.scalar_tensor_tensor(tg[:, :, :], tg[:, :, :], 1.0, grt[:, :, :], ALU.add, ALU.mult))
                            for e in range(2):
                                ins = dve.scalar_tensor_tensor(ot[:, e, :], ot[:, e, :], cols[:, COL_GH + e:COL_GH + e + 1],
                                                               tg[:, e, :], ALU.mult, ALU.mult)
                            ins.then_inc(og_f, 1)
                            dve.wait_ge(og_hi, I + 1)
                            dve.tensor_tensor(og[:, ds(2 * I, 2), TOK:], ot[:, :, :],
                                              og[:, ds(2 * I, 2), 0:TOK].bitcast(F32), ALU.subtract).then_inc(og_ready, 1)
                assert L.k == HEAD_STEPS, L.k
                S.base += 2 * HEAD_STEPS
                m = (M_GT2, M_GT1)[half]
                dve.wait_ge(mod_done, 2 + half)
                zero_acc(1 + half)
                link(dve.tensor_tensor(mods[:, m, :], ps[:, 4, 0:KT], cols[:, m * KT:(m + 1) * KT], ALU.add))
                post = (COL_POST2, COL_POST1)[half]
                link(dve.tensor_tensor(mods[:, m, :], mods[:, m, :], cols[:, post:post + KT], ALU.mult))

            def diagonal(G, m):
                for j in range(KT):
                    ins = dve.tensor_scalar(G[:, P * j:P * (j + 1)], ident[:, :], mods[:, m, j:j + 1], None, ALU.mult)
                ins.then_inc(dg_ready, 1)

            diagonal(G, M_GT1)

            MERGE_STEPS = 2
            for half in range(2):
                start = S.base + S.k
                with dve.Fori(0, 4) as i:
                    J = i + 4 * half
                    L = Loop(start, i, MERGE_STEPS)
                    u = 0
                    for n in range(MERGE_N):
                        a = MERGE_N * J + A_MERGE + n
                        split_lo((1 + n) % 3, hi3, a + 3 + 1, split3)
                        for _u in range(ADA_MERGE[n]):
                            accumulate(64 + 8 * J + u, u % 2, 32 + 4 * J + u // 2, 4 * i + u // 2)
                            u += 1
                        if n in (1, 3):
                            g = n // 2
                            dve.wait_ge(cross3, 4 * J + g + 1)
                            dve.tensor_tensor(gx[:, g, :, :], ps[:, 2 * g:2 * g + 2, 0:TOK], tmp3[:, g, :, :], ALU.add).then_inc(evac3, 2)
                        if n in (4, 5):
                            g = n - 2
                            y = ya if n == 4 else yb
                            dve.wait_ge(cross3, 4 * J + g + 1)
                            dve.tensor_tensor(y[:, :, :], ps[:, 2 * g:2 * g + 2, 0:TOK], tmp3[:, g % 2, :, :], ALU.add).then_inc(evac3, 2)
                            dve.wait_ge(evac3, 8 * J + 2 * (g + 1) + 8)
                            dve.wait_ge(sig_done, 2 * J + g - 1)
                            L.link(dve.tensor_tensor(y[:, :, :], y[:, :, :], sg[:, g - 2, :, :], ALU.mult), wait=n == 5)
                        if n == 5:
                            dve.tensor_tensor(mT[:, ds(2 * J, 2), :], ya[:, :, :], yb[:, :, :], ALU.add).then_inc(m_done, 1)
                assert L.k == MERGE_STEPS, L.k
                S.base += 4 * MERGE_STEPS
                m = (M_SC2, M_SH2)[half]
                dve.wait_ge(mod_done, 4 + half)
                if half == 0:
                    zero_acc(3)
                    link(dve.tensor_tensor(mods[:, m, :], ps[:, 4, 0:KT], cols[:, m * KT:(m + 1) * KT], ALU.add))
                    link(dve.scalar_tensor_tensor(mods[:, m, :], mods[:, m, :], 1.0, cols[:, COL_PRE2:COL_PRE2 + KT],
                                                  ALU.add, ALU.mult))
                else:
                    dve.tensor_tensor(mods[:, m, :], ps[:, 4, 0:KT], cols[:, m * KT:(m + 1) * KT], ALU.add).then_inc(mods_ready, 1)

            def merged_lo(kt):
                dve.wait_ge(m_hi, kt + 1)
                dve.tensor_tensor(hT[:, kt, TOK:], mT[:, kt, :], hT[:, kt, 0:TOK].bitcast(F32), ALU.subtract).then_inc(m_ready, 1)

            for kt in range(4):
                merged_lo(kt)
            split_lo(3, hi4, 1, split4)
            diagonal(dg2, M_GT2)
            for w in range(4, KT + 4):
                split_lo(SLOT4[w % 4], hi4, w - 2, split4)
                if w < KT:
                    merged_lo(w)

            def factors(ysq_count, root):
                dve.wait_ge(ysq, ysq_count)
                dve.reduce_sum(stat[:, 4:6], stat[:, 32:40].rearrange("p (t b) -> p t b", t=TT), AX.X).then_inc(ysqrt, 1)
                dve.wait_ge(ysqrt, root)
                link(dve.reciprocal(stat[:, 4:6], stat[:, 4:6]))

            def gated(dst, tt):
                for b in range(4):
                    ins = dve.scalar_tensor_tensor(dst[:, tt, 512 * b:512 * (b + 1)], ps[:, 4 * tt + b, :], stat[:, 4 + tt:5 + tt],
                                                   G[:, 512 * b:512 * (b + 1)], ALU.mult, ALU.mult)
                link(ins)

            factors(8, 2)
            dve.wait_ge(xr_in, 16)
            dve.wait_ge(g_ready, 1)
            for tt in range(TT):
                gated(yt, tt)
                dve.tensor_tensor(x2[:, tt, :], x2[:, tt, :], yt[:, tt, :], ALU.add).then_inc(x2_ready, 1)
            dve.wait_ge(xsqrt, 2)
            link(dve.reciprocal(stat[:, 6:8], stat[:, 6:8]))
            for tt in range(TT):
                dve.tensor_scalar(yt[:, tt, :], x2[:, tt, :], stat[:, 6 + tt:7 + tt], None, ALU.mult).then_inc(xn_ready, 1)
            to_h(1, h32b, M_SC2, M_SH2)
            link(dve.memset(up[:, :, 0:2], 0.0))

            UP_STEPS = 4
            start = S.base + S.k
            with dve.Fori(0, UP_ITERS) as i:
                L = Loop(start, i, UP_STEPS)
                for n in range(4):
                    split_lo(SLOT4[n], hi4, 4 * i + W_UP + n + 4 - 2, split4)
                    if n % 2 == 0:
                        continue
                    g = n // 2
                    q = 2 * i + g
                    dve.wait_ge(cross5, q + 1)
                    dve.tensor_tensor(up[:, :, 2:], ps[:, 2 * g:2 * g + 2, 0:TOK], cv[:, :, :], ALU.add).then_inc(up_ready, 1)
                    for ct in range(2):
                        f = 2 * i + FT * g + ct
                        dve.wait_ge(cb_done, 2 * q + ct + 1)
                        L.link(dve.scalar_tensor_tensor(cv[:, ct, :], up[:, ct, 1:TOK + 1], cols[:, ds(f + COL_CONV + 2 * FT, 1)],
                                                        cv[:, ct, :], ALU.mult, ALU.add), wait=ct == 1)
                    dst = cv if g else ub
                    for ct in range(2):
                        f = 2 * i + FT * g + ct
                        ins = dve.scalar_tensor_tensor(dst[:, ct, :], up[:, ct, 0:TOK], cols[:, ds(f + COL_CONV, 1)],
                                                       cv[:, ct, :], ALU.mult, ALU.add)
                    ins.then_inc(conv_g if g else conv_done, 1)
                    if g:
                        dve.wait_ge(gelu_done, i + 1)
                        dve.tensor_tensor(aT[:, ds(2 * i, 2), :], cv[:, :, :], ub[:, :, :], ALU.mult).then_inc(conv_done, 1)
            assert L.k == UP_STEPS, L.k
            S.base += UP_ITERS * UP_STEPS

            def act_lo(kt, k):
                dve.wait_ge(a_hi, kt + 1)
                dve.tensor_tensor(asp[:, k, TOK:], aT[:, ds(kt, 1), :], asp[:, k, 0:TOK].bitcast(F32), ALU.subtract).then_inc(a_ready, 1)

            for k in range(4):
                act_lo(k, k)
            with dve.Fori(0, FT // 4 - 1) as i:
                for n in range(4):
                    act_lo(4 * i + 4 + n, n)
                    split_lo(SLOT4[n], hi4, 4 * i + W_DOWN + n + 4 - 2, split4)
            factors(16, 4)
            dve.wait_ge(g_ready, 2)
            for tt in range(TT):
                gated(yo, tt)
                dve.tensor_tensor(yo[:, tt, :], yo[:, tt, :], x2[:, tt, :], ALU.add).then_inc(out_ready, 1)

        @block.tensor
        def _(pe):
            def mm(out_, lhsT, rhs, start=True, stop=True):
                return pe.matmul(out_, lhsT, rhs, start=start, stop=stop)

            def weights_still(slot, acts, k0, kn, bank, used):
                for k in range(8):
                    kk = k0 + k
                    for ct in range(2):
                        cs = slice(P * ct, P * (ct + 1))
                        mm(ps[:, bank + ct, :], ws[:, slot, k, 0, cs], acts[:, kk, :], kk == 0, False)
                        last = mm(ps[:, bank + ct, TOK:], ws[:, slot, k, 1, cs], acts[:, kk, 0:TOK], False, kk == kn - 1)
                last.then_inc(used, 1)

            def tokens_still(slot, k0, bank, used):
                for k in range(8):
                    kk = k0 + k
                    for tt in range(TT):
                        mm(ps[:, bank + tt, :], hT[:, kk, P * tt:P * (tt + 1)], ws[:, slot, k, :, :], kk == 0, False)
                        last = mm(ps[:, bank + tt, TOK:], hT[:, kk, TOK + P * tt:TOK + P * (tt + 1)], ws[:, slot, k, 0, :], False, kk == KT - 1)
                last.then_inc(used, 1)

            def one_row_tile(slot, acts, first, last_, used, order=(0, 1)):
                for tt in order:
                    hi, lo = acts[:, P * tt:P * (tt + 1)], acts[:, TOK + P * tt:TOK + P * (tt + 1)]
                    for b in range(4):
                        w_hi, w_lo = ws[:, slot, 2 * b:2 * b + 2, 0, :], ws[:, slot, 2 * b:2 * b + 2, 1, :]
                        mm(ps[:, 4 * tt + b, :], hi, w_hi, first, False)
                        mm(ps[:, 4 * tt + b, :], hi, w_lo, False, False)
                        ins = mm(ps[:, 4 * tt + b, :], lo, w_hi, False, last_)
                ins.then_inc(used, 1)

            def transposed(first, src):
                for kt in range(KT):
                    if kt >= 4:
                        pe.wait_ge(h_odd if kt % 2 else h_even, first * (KT // 2) + (kt - 4) // 2 + 1)
                    for tt in range(TT):
                        if kt == 0:
                            pe.wait_ge(xn_ready, TT * first + tt + 1)
                        ins = pe.transpose(ps[:, 4 + kt % 4, P * tt:P * (tt + 1)], src[:, tt, P * kt:P * (kt + 1)], ident[:, :])
                    ins.then_inc(xT_done, 1)

            def column_sums(a, col, bank, at_):
                for j in range(KT):
                    ins = mm(ps[:, bank, at_ + j:at_ + j + 1], a[:, col + P * j:col + P * (j + 1)], ones[:, 0:1])
                return ins

            def lay_out(dg):
                for b in range(4):
                    ins = mm(ps[:, b, :], ones[:, :], dg[:, 512 * b:512 * (b + 1)])
                ins.then_inc(g_done, 1)

            pe.wait_ge(pool_step, 4)
            pe.wait_ge(rows_in, 160)
            pe.transpose(ps[:, 0, 0:96], rows[0:96, 0, :], ident[0:96, 0:96])
            pe.transpose(ps[:, 0, 96:162], rows[0:66, 1, :], ident[0:66, 0:66])
            nc_ = 2 * FT
            for j in range(3):
                pe.transpose(ps[:, 0, COL_CONV + nc_ * j:COL_CONV + nc_ * (j + 1)], rows[0:nc_, 2 + j, :], ident[0:nc_, 0:nc_])
            pe.transpose(ps[:, 1, 0:nc_], rows[0:nc_, 5, :], ident[0:nc_, 0:nc_]).then_inc(colsT, 1)
            pe.wait_ge(head_used, 4 + 32)
            column_sums(acc0, 0, 2, 0)
            column_sums(acc0, D, 2, KT).then_inc(mod_done, 1)
            transposed(0, xn)

            pe.wait_ge(h_ready, KT)
            pe.wait_ge(split3, 0 + 4)
            for k in range(KT):
                cs = slice(P * (k % 2), P * (k % 2 + 1))
                mm(ps[:, 6, :], ws[:, 0, k // 2, 0, cs], hT[:, k, :], k == 0, False)
                ins = mm(ps[:, 6, TOK:], ws[:, 0, k // 2, 1, cs], hT[:, k, 0:TOK], False, k == KT - 1)
            ins.then_inc(used3, 1)
            pe.wait_ge(low_ready, 1)
            pe.wait_ge(gate_in, 32)
            for tt in range(TT):
                mm(ps[:, 4 + tt, :], galow[0:RANK, P * tt:P * (tt + 1)], walpha[0:RANK, :], True, False)
                ins = mm(ps[:, 4 + tt, :], ones[0:1, :], balpha[0:1, :], False, True)
            ins.then_inc(z_done, 1)
            pe.wait_ge(la_ready, 1)
            for h in range(HEADS):
                for tt in range(TT):
                    col = TOK * (h % 2) + P * tt
                    ins = mm(ps[:, 6 + h // 2, col:col + P], loga[:, tt, P * h:P * (h + 1)], tri[:, :])
            ins.then_inc(tri_done, 1)

            def gram(I, p):
                bank = 4 if p % 2 else 5
                pe.wait_ge(level_ready, 8 * I + p + 1)
                if p == 0:
                    mm(ps[:, 5, 0:P], Mb[:, 0, 0:P], Mb[:, 0, P:]).then_inc(gram_done, 1)
                    return
                if p == 2:
                    pe.wait_ge(a01_done, I + 1)
                else:
                    pe.wait_ge(select_done, 8 * I + max(p - 1, 1))
                for t in range(TT):
                    m = Mb[:, p % 2, P * t:P * (t + 1)]
                    ins = mm(ps[:, bank, P * t:P * (t + 1)], m, m)
                ins.then_inc(gram_done, 1)

            def causal_product(out_, values, weights):
                mm(out_, values[0], weights[:, 0:2 * P], True, False)
                return mm(out_[:, P:2 * P], values[1], weights[:, 2 * P:3 * P], False, True)

            for half in range(2):
                with pe.Fori(0, 2) as i:
                    I = i + 2 * half
                    for n in range(HEAD_N):
                        a = HEAD_N * I + A_HEAD + n
                        g = n // 2
                        b = 2 * (g % 2)
                        if n % 2 == 0:
                            pe.wait_ge(evac, 12 * I + 2 * g + 2)
                        pe.wait_ge(split3, a + 4)
                        if g in (1, 4):
                            tokens_still((1 + n) % 3, 8 * (n % 2), b, used3)
                        else:
                            weights_still((1 + n) % 3, hT, 8 * (n % 2), KT, b, used3)
                        if n == 2:
                            pe.wait_ge(evac, 12 * I + 2 + 4)
                            for t in range(TT):
                                ts = slice(P * t, P * (t + 1))
                                ins = mm(ps[:, 4, ts], qk[:, 1, ts], qk[:, 0, ts])
                            ins.then_inc(gram_done, 1)
                        if n == 3:
                            gram(I, 0)
                            gram(I, 1)
                        if 4 <= n <= 9:
                            gram(I, n - 2)
                        if n == 8:
                            pe.wait_ge(evac, 12 * I + 8 + 4)
                            for hd in range(2):
                                for qt in range(TT):
                                    ins = mm(ps[:, 6 + hd, TOK * qt:TOK * (qt + 1)], mqk[:, 0, hd, P * qt:P * (qt + 1)], mqk[:, 1, hd, :])
                                ins.then_inc(qk_done, 1)
                        if n == 10:
                            for hd in range(2):
                                pe.wait_ge(pn_ready, 2 * I + hd + 1)
                                for j, (qt, k) in enumerate(((0, 0), (1, 0), (1, 1))):
                                    ins = pe.transpose(ps[:, 6 + hd, P * j:P * (j + 1)],
                                                       ssb[:, hd, TOK * qt + P * k:TOK * qt + P * (k + 1)], ident[:, :])
                                ins.then_inc(pt_done, 1)
                            pe.wait_ge(select_done, 8 * I + 8)
                            Af = A[:, :, :].rearrange("p j i -> p (j i)")
                            for e in range(2):
                                es = slice(P * e, P * (e + 1))
                                ins = causal_product(ps[:, 4, TOK * e:TOK * (e + 1)], (vv[:, 0, es], vv[:, 1, es]), Af)
                            ins.then_inc(av_done, 1)
                        if n == 11:
                            pe.wait_ge(evac, 12 * I + 10 + 4)
                            for hd in range(2):
                                es = slice(P * hd, P * (hd + 1))
                                pe.wait_ge(ptc_done, 2 * I + hd + 1)
                                ins = causal_product(ps[:, 6 + hd, 0:TOK], (mv[:, 0, es], mv[:, 1, es]), pT[:, hd, :])
                            ins.then_inc(pv_done, 1)
                            pe.wait_ge(sq_done, I + 1)
                            mm(ps[:, 5, 0:TOK], ones[:, :], sq[:, 0, :], True, False)
                            mm(ps[:, 5, 0:TOK], ones[:, :], sq[:, 1, :], False, True).then_inc(ss_done, 1)
                pe.wait_ge(ada_used, 2 + 32 * (half + 1))
                column_sums(acc, 0, 4, 0).then_inc(mod_done, 1)

            pe.wait_ge(evac, 4 + 12 * HEADS)
            for half in range(2):
                with pe.Fori(0, 4) as i:
                    J = i + 4 * half
                    for n in range(MERGE_N):
                        a = MERGE_N * J + A_MERGE + n
                        if n in (0, 2, 4, 5):
                            g = n // 2 if n < 4 else n - 2
                            pe.wait_ge(evac3, 8 * J + 2 * g + 2)
                        pe.wait_ge(split3, a + 4)
                        if n < 4:
                            weights_still((1 + n) % 3, hT, 8 * (n % 2), KT, 2 * g, used3)
                        elif n == 4:
                            pe.wait_ge(og_ready, HEADS)
                            weights_still((1 + n) % 3, og, 0, 8, 4, used3)
                        else:
                            pe.wait_ge(om_ready, HEADS)
                            weights_still((1 + n) % 3, om, 0, 8, 6, used3)
                pe.wait_ge(ada_used, 2 + 64 + 32 * (half + 1))
                pe.wait_ge(evac3, 8 + 32 * (half + 1))
                column_sums(acc, 0, 4, 0).then_inc(mod_done, 1)
                if half == 0:
                    pe.wait_ge(dg_ready, 1)
                    lay_out(G)
                    pe.wait_ge(g_ready, 1)

            pe.wait_ge(mods_ready, 2)
            for kt in range(KT):
                if kt < 3:
                    pe.wait_ge(split3, A_WO + kt + 4)
                else:
                    pe.wait_ge(split4, kt - 2)
                pe.wait_ge(m_ready, kt + 1)
                one_row_tile(SLOT4[kt % 4], hT[:, kt, :], kt == 0, kt == KT - 1, used3 if kt < 3 else used4)
            pe.wait_ge(dg_ready, 2)
            pe.wait_ge(x2_ready, 1)
            lay_out(dg2)
            transposed(1, yt)

            pe.wait_ge(h_ready, 2 * KT)
            pe.wait_ge(g_ready, 2)
            with pe.Fori(0, UP_ITERS) as i:
                for n in range(4):
                    if n % 2 == 0:
                        pe.wait_ge(conv_done, 2 * i + n // 2 + 1)
                    pe.wait_ge(split4, 4 * i + W_UP + n - 2)
                    weights_still(SLOT4[n], hT, 8 * (n % 2), KT, 2 * (n // 2), used4)

            def down(i, first=False, last=False):
                for n in range(4):
                    pe.wait_ge(split4, 4 * i + W_DOWN + n - 2)
                    pe.wait_ge(a_ready, 4 * i + n + 1)
                    one_row_tile(SLOT4[n], asp[:, n, :], first and n == 0, last and n == 3, used4, (1, 0))

            down(0, first=True)
            with pe.Fori(1, FT // 4 - 1) as i:
                down(i)
            down(FT // 4 - 1, last=True)


_INS = ["x", "c", "w_ada", "b_ada", "g_pre_mix", "w_in", "w_alpha_up", "b_alpha", "g_gla_head", "w_gla_out",
        "w_moba_out", "w_o", "g_post_mix", "g_pre_ffn", "w_up", "w_conv", "b_conv", "w_down", "g_post_ffn"]


def kernel(**inputs):
    import numpy as np
    import concourse.bacc as bacc
    from concourse.bass_utils import run_bass_kernel_spmd

    nc = bacc.Bacc("TRN2", target_bir_lowering=False, num_devices=1)
    arrays, args = {}, []
    for name in _INS:
        a = np.ascontiguousarray(inputs[name])
        arrays[f"in_{name}"] = a
        args.append(nc.dram_tensor(f"in_{name}", a.shape, mybir.dt.from_np(a.dtype), kind="ExternalInput").ap())
    args.append(nc.dram_tensor("out_0", inputs["x"].shape, F32, kind="ExternalOutput").ap())
    layer_kernel(nc, *args)
    r = run_bass_kernel_spmd(nc, [arrays], core_ids=[0])
    return r.results[0]["out_0"]
```

```python
import concourse.bass as bass
from concourse import mybir
from contextlib import ExitStack

F32 = mybir.dt.float32
F32R = mybir.dt.float32r
U8 = mybir.dt.uint8
ALU = mybir.AluOpType
ACT = mybir.ActivationFunctionType
AX = mybir.AxisListType
ds = bass.ds

P = 128
KB = 1024


def layer_kernel(nc, x, c, w_ada, b_ada, g_pre_mix, w_in, w_alpha_up, b_alpha, g_gla_head, w_gla_out,
                 w_moba_out, w_o, g_post_mix, g_pre_ffn, w_up, w_conv, b_conv, w_down, g_post_ffn, out):
    TOK, D = x.shape[1], x.shape[2]
    TT = TOK // P
    KT = D // P
    FFN = w_down.shape[1]
    FT = FFN // P
    RANK, GLA_K = w_alpha_up.shape[1], w_alpha_up.shape[2]
    DV = g_gla_head.shape[1]
    HEADS = GLA_K // P
    GLA_V = HEADS * DV
    MOBA_W = w_moba_out.shape[1]
    EPS = 1e-6
    SCALE = float(P) ** -0.5
    GATE_TEMP = 16.0
    CW = 2048
    C_GQ, C_GK, C_GV = 0, GLA_K, 2 * GLA_K
    C_GR = C_GV + GLA_V
    C_LOW = C_GR + GLA_V
    C_MQ = C_LOW + RANK
    C_MK, C_MV = C_MQ + MOBA_W, C_MQ + 2 * MOBA_W
    C_GA = C_MQ + 3 * MOBA_W
    C_GB = C_GA + D
    assert (TOK, D, TT, KT, DV, HEADS, GLA_V, MOBA_W) == (256, 2048, 2, 16, 256, 4, 1024, 1024)

    HEAD_N, MERGE_N = 12, 6
    A_HEAD, A_MERGE, A_WO = 1, 1 + HEADS * HEAD_N, 1 + HEADS * HEAD_N + 8 * MERGE_N
    UP_ITERS = FFN // 256
    W_UP, W_DOWN = KT, KT + 4 * UP_ITERS
    SLOT4 = [(A_WO + 0) % 3, (A_WO + 1) % 3, (A_WO + 2) % 3, 3]
    PASS_N = 12
    ADA_UNITS = [0, 1, 1, 1, 1, 1, 2, 2, 2, 1, 2, 2]
    assert sum(ADA_UNITS) == KT and HEAD_N == PASS_N == 2 * MERGE_N
    M_SH1, M_SC1, M_GT1, M_SH2, M_SC2, M_GT2 = range(6)
    PARTS = 8

    win = w_in[0].rearrange("(k p) n -> p k n", p=P)
    wup = w_up[0].rearrange("(k p) n -> p k n", p=P)
    wgo = w_gla_out[0].rearrange("(k p) n -> p k n", p=P)
    wmo = w_moba_out[0].rearrange("(k p) n -> p k n", p=P)
    wo = w_o[0].rearrange("(k p) n -> p k n", p=P)
    wdn = w_down[0].rearrange("(k p) n -> p k n", p=P)
    wada = w_ada[0].rearrange("(p t) n -> p t n", t=KT)
    x_v = x[0].rearrange("(t p) d -> p t d", p=P)
    out_v = out[0].rearrange("(t p) d -> p t d", p=P)

    ctx = ExitStack()
    with ctx:
        base = -(-nc.sbuf_base // 64) * 64

        def at(name, kb, shape, dt=F32):
            return nc.alloc_sbuf_tensor_at(name, [P] + shape, dt, offset=base + int(kb * KB))

        def sem(name):
            return ctx.enter_context(nc.semaphore(name))

        raw = at("raw", 0, [4, CW])
        ws = at("ws", 32, [4, 8, 2, 256], F32R)
        hT = at("hT", 96, [KT, 2 * TOK], F32R)
        NCOL = 96 + 66 + 352
        cols = at("cols", 128, [NCOL])
        ident = at("ident", 130.25, [P])
        ones = at("ones", 130.75, [P])
        mods = at("mods", 131.25, [6, KT])
        ccol = at("ccol", 131.625, [KT])
        scol = at("scol", 131.6875, [KT])
        stat = at("stat", 131.75, [48])
        eps = at("eps", 131.9375, [1])
        modsf = mods[:, :, :].rearrange("p m k -> p (m k)")
        xnat = at("xnat", 132, [TT, D])
        xn = at("xn", 148, [TT, D])
        junk = at("junk", 80, [D])
        rows = at("rows", 88, [6, P])
        maskf = at("maskf", 91, [8, P])
        acc0 = at("acc0", 180, [2 * D])
        h32 = at("h32", 196, [4, TOK])
        walpha = at("walpha", 203.5, [GLA_K])
        balpha = at("balpha", 205.5, [GLA_K])
        zabs = at("zabs", 180, [TT, GLA_K])
        zmin = at("zmin", 184, [TT, GLA_K])
        loga = at("loga", 188, [TT, GLA_K])
        galow = at("galow", 194, [TOK])
        galow_x = at("galow_x", 195, [TOK])
        og = at("og", 132, [8, 2 * TOK], F32R)
        om = at("om", 148, [8, 2 * TOK], F32R)
        ada = at("ada", 164, [2, 1024])
        acc = at("acc", 176, [1024])
        bT = at("bT", 24, [HEADS, TOK])
        bc = at("bc", 28, [TOK])
        eb = at("eb", 29, [2, TOK])
        rs = at("rs", 31, [TOK])
        Mb = at("Mb", 80, [2, TOK])
        A = at("A", 82, [3, P])
        ot = at("ot", 84, [2, TOK])
        sq = at("sq", 86, [2, TOK])
        ssb = at("ssb", 88, [2, 2 * TOK])
        pT = at("pT", 92, [2, 3 * P])
        qk = at("qk", 180, [2, TOK])
        vv = at("vv", 182, [TT, DV])
        grt = at("grt", 184, [2, TOK])
        tg = at("tg", 186, [2, TOK])
        mqk = at("mqk", 188, [2, 2, TOK])
        mv = at("mv", 192, [TT, 256])
        tmp = at("tmp", 196, [2, 2, TOK])
        tri = at("tri", 200, [P])
        causal = at("causal", 200.5, [2 * TOK])
        mask8 = at("mask8", 202.5, [8, P], U8)
        tmp3 = at("tmp3", 24, [2, 2, TOK])
        gx = at("gx", 28, [2, 2, TOK])
        sg = at("sg", 80, [2, 2, TOK])
        ya = at("ya", 84, [2, TOK])
        yb = at("yb", 86, [2, TOK])
        mT = at("mT", 180, [KT, TOK])
        G = at("G", 196, [D])
        x2 = at("x2", 132, [TT, D])
        yt = at("yt", 148, [TT, D])
        junk2 = at("junk2", 164, [D])
        h32b = at("h32b", 188, [4, TOK])
        dg2 = at("dg2", 172, [D])
        aT = at("aT", 148, [FT, TOK])
        cv = at("cv", 192, [2, TOK])
        ub = at("ub", 194, [2, TOK])
        up = at("up", 204, [2, TOK + 2])
        asp = at("asp", 96, [4, 2 * TOK], F32R)
        yo = at("yo", 104, [TT, D])
        junk3 = at("junk3", 120, [D])
        ps = ctx.enter_context(nc.psum_tensor("ps", [P, 8, 512], F32))

        COL_BADA, COL_PRE1, COL_POST1, COL_PRE2, COL_POST2, COL_GH, COL_CONV = 0, 96, 112, 128, 144, 160, 162
        COL_CB = COL_CONV + 3 * 2 * FT

        c_in, x_in, rows_in, gate_in, xr_in = sem("c_in"), sem("x_in"), sem("rows_in"), sem("gate_in"), sem("xr_in")
        head_in = [sem(f"head_in{i}") for i in range(4)]
        raw3_in = [sem(f"raw3_in{i}") for i in range(3)]
        raw4_in = [sem(f"raw4_in{i}") for i in range(4)]
        ada_in = [sem(f"ada_in{i}") for i in range(2)]
        head_used = sem("head_used")
        ada_used = sem("ada_used")
        hi3, split3, used3 = sem("hi3"), sem("split3"), sem("used3")
        hi4, split4, used4 = sem("hi4"), sem("split4"), sem("used4")
        pool_step = sem("pool_step")
        dve_step, act_step, tail_step = sem("dve_step"), sem("act_step"), sem("tail_step")
        scol_ready, xsq, xsqrt, xn_ready = sem("scol_ready"), sem("xsq"), sem("xsqrt"), sem("xn_ready")
        colsT, cols_ready = sem("colsT"), sem("cols_ready")
        mod_done, mods_ready, part_read = sem("mod_done"), sem("mods_ready"), sem("part_read")
        xT_done, h_even, h_odd, h_hi, h_ready = sem("xT_done"), sem("h_even"), sem("h_odd"), sem("h_hi"), sem("h_ready")
        z_done, z_abs, z_ln, la_ready, tri_done, bT_ready = (sem("z_done"), sem("z_abs"), sem("z_ln"),
                                                             sem("la_ready"), sem("tri_done"), sem("bT_ready"))
        low_x, low_ready = sem("low_x"), sem("low_ready")
        cross, evac = sem("cross"), sem("evac")
        e_ready, exp_done, level_ready, gram_done = sem("e_ready"), sem("exp_done"), sem("level_ready"), sem("gram_done")
        select_done, a01_done, av_done, ot_done, sq_done, ss_done = (sem("select_done"), sem("a01_done"), sem("av_done"),
                                                                     sem("ot_done"), sem("sq_done"), sem("ss_done"))
        rs_done, tanh_done, og_f, og_hi, og_ready = sem("rs_done"), sem("tanh_done"), sem("og_f"), sem("og_hi"), sem("og_ready")
        qk_done, nb_ready, p_ready, pn_ready, pt_done, ptc_done, pv_done, om_hi, om_ready = (
            sem("qk_done"), sem("nb_ready"), sem("p_ready"), sem("pn_ready"), sem("pt_done"), sem("ptc_done"),
            sem("pv_done"), sem("om_hi"), sem("om_ready"))
        cross3, evac3, sig_done = sem("cross3"), sem("evac3"), sem("sig_done")
        dg_ready, g_done, g_ready = sem("dg_ready"), sem("g_done"), sem("g_ready")
        m_done, m_hi, m_ready = sem("m_done"), sem("m_hi"), sem("m_ready")
        ysq, ysqrt, x2_ready = sem("ysq"), sem("ysqrt"), sem("x2_ready")
        cross5, up_ready, cb_done, conv_g, gelu_done = (sem("cross5"), sem("up_ready"), sem("cb_done"), sem("conv_g"),
                                                        sem("gelu_done"))
        conv_done = sem("conv_done")
        a_hi, a_ready = sem("a_hi"), sem("a_ready")
        out_ready, out_done = sem("out_ready"), sem("out_done")

        block = ctx.enter_context(nc.Block())

        def raw_blocks(slot):
            return raw[:, slot, :].rearrange("p (b n) -> p b n", n=256)

        def arrived4(w, k):
            return (w - k) // 4 + (1 if k == 3 else 0)

        @block.sync
        def _(sp):
            def load(slot, arrival, src, lo, hi, n):
                dst = raw[:, slot, :].rearrange("p (b n) -> p b n", n=n)
                sp.dma_start(dst[:, lo:hi, :], src).then_inc(arrival, 16)

            def load_k(slot, arrival, w, kh, col, n=256, step=8):
                h = step // 2
                for j in (1, 0):
                    load(slot, arrival, w[:, step * kh + h * j:step * kh + h * (j + 1), ds(col, n)], h * j, h * (j + 1), n)

            def load_row(slot, arrival, w, kt):
                for j in range(2):
                    sp.dma_start(raw[:, slot, 1024 * j:1024 * (j + 1)], w[:, kt, 1024 * j:1024 * (j + 1)]).then_inc(arrival, 16)

            with sp.Fori(0, KT // 2) as i:
                for j in range(4):
                    sp.wait_ge(head_used, 4 * i + j + 1)
                    sp.dma_start(raw[:, j, :], wada[:, ds(2 * i + j // 2, 1), (j % 2) * D:(j % 2 + 1) * D]).then_inc(head_in[j], 16)
            sp.wait_ge(head_used, 4 + 31)
            load_k(0, raw3_in[0], win, 0, C_LOW, n=P, step=16)
            with sp.Fori(0, HEADS) as I:
                for n in range(HEAD_N):
                    slot, arrival, kh = (1 + n) % 3, raw3_in[(1 + n) % 3], n % 2
                    sp.wait_ge(split3, HEAD_N * I + A_HEAD + n + 1)
                    if n < 2:
                        dst = raw[:, slot, :].rearrange("p (k two n) -> p k two n", two=2, n=P)
                        for j, col in enumerate((C_GQ, C_GK)):
                            sp.dma_start(dst[:, :, j, :], win[:, 8 * kh:8 * kh + 8, ds(I * P + col, P)]).then_inc(arrival, 16)
                    else:
                        load_k(slot, arrival, win, kh, I * 256 + (C_GV, C_MQ, C_MK, C_MV, C_GR)[n // 2 - 1])
            with sp.Fori(0, 8) as J:
                for n in range(MERGE_N):
                    slot, arrival = (1 + n) % 3, raw3_in[(1 + n) % 3]
                    sp.wait_ge(split3, MERGE_N * J + A_MERGE + n + 1)
                    if n < 4:
                        load_k(slot, arrival, win, n % 2, J * 256 + (C_GA if n < 2 else C_GB))
                    else:
                        load_k(slot, arrival, wgo if n == 4 else wmo, 0, J * 256)
            for w in range(KT):
                k = w % 4
                if w < 3:
                    sp.wait_ge(split3, A_WO + w + 1)
                    load_row(SLOT4[k], raw3_in[SLOT4[k]], wo, w)
                else:
                    if w in (4, 5, 6):
                        sp.wait_ge(split3, 3 + A_WO + w - 4 + 1)
                    if w >= 7:
                        sp.wait_ge(split4, w - 6)
                    if w == 3:
                        sp.wait_ge(evac3, 8 + 8 * 8)
                        sp.wait_ge(sig_done, 16)
                    load_row(SLOT4[k], raw4_in[k], wo, w)
                if w == 6:
                    sp.wait_ge(used3, A_WO)
                    sp.dma_start(x2[:, :, :], x_v).then_inc(xr_in, 16)
            with sp.Fori(0, UP_ITERS) as i:
                for n in range(4):
                    sp.wait_ge(split4, 4 * i + W_UP + n - 6)
                    load_k(SLOT4[n], raw4_in[n], wup, n % 2, i * 256 + (FFN if n >= 2 else 0))
            with sp.Fori(0, FT // 4) as i:
                for n in range(4):
                    sp.wait_ge(split4, 4 * i + W_DOWN + n - 6)
                    for j in range(2):
                        sp.dma_start(raw[:, SLOT4[n], 1024 * j:1024 * (j + 1)],
                                     wdn[:, ds(4 * i + n, 1), 1024 * j:1024 * (j + 1)]).then_inc(raw4_in[n], 16)
            for tt in range(TT):
                sp.wait_ge(out_ready, tt + 1)
                sp.dma_start(out_v[:, tt, :], yo[:, tt, :]).then_inc(out_done, 16)
            sp.wait_ge(out_done, 16 * TT)

        @block.gpsimd
        def _(pool):
            step = [0]

            def made(ins):
                step[0] += 1
                ins.then_inc(pool_step, 1)
                pool.wait_ge(pool_step, step[0])

            made(pool.memset(ones[:, :], 1.0))
            made(pool.memset(eps[:, :], EPS))
            made(pool.memset(ident[:, :], 0.0))
            made(pool.affine_select(out=ident[:, :], in_=ident[:, :], compare_op=ALU.not_equal, fill=1.0, base=0,
                                    pattern=[[-1, P]], channel_multiplier=1))
            made(pool.memset(maskf[:, 0, :], 0.0))
            made(pool.memset(tri[:, :], 1.0 / GATE_TEMP))
            made(pool.affine_select(out=tri[:, :], in_=tri[:, :], compare_op=ALU.is_ge, fill=0.0, base=0,
                                    pattern=[[1, P]], channel_multiplier=-1))
            made(pool.memset(causal[:, :], 0.0))
            cv4 = causal[:, :].rearrange("p (t k) -> p t k", t=TT)
            made(pool.affine_select(out=cv4, in_=cv4, compare_op=ALU.is_ge, fill=-1e30, base=0,
                                    pattern=[[P, TT], [-1, TOK]], channel_multiplier=1))
            for lv in range(1, 8):
                s = 2 ** (lv - 1)
                m = maskf[:, lv, :].rearrange("p (g two s) -> p g two s", two=2, s=s)
                made(pool.memset(maskf[:, lv, :], 0.0))
                made(pool.memset(m[:, :, 1, :], 1.0))
                m2 = maskf[:, lv, :].rearrange("p (g r) -> p g r", r=2 * s)
                made(pool.affine_select(out=m2, in_=m2, compare_op=ALU.is_ge, fill=0.0, base=0,
                                        pattern=[[-2 * s, P // (2 * s)], [0, 2 * s]], channel_multiplier=1))
                made(pool.affine_select(out=m2, in_=m2, compare_op=ALU.is_ge, fill=0.0, base=s - 1,
                                        pattern=[[2 * s, P // (2 * s)], [0, 2 * s]], channel_multiplier=-1))
            made(pool.affine_select(out=maskf[:, 0, :], in_=maskf[:, 0, :], compare_op=ALU.not_equal, fill=1.0, base=0,
                                    pattern=[[-1, P]], channel_multiplier=1))
            for q in range(PARTS):
                col = M_GT1 * D + 1024 * q
                with pool.Fori(0, KT // 2) as t:
                    for s in range(2):
                        pool.wait_ge(ada_used, 2 * t + (KT * q + s + 1))
                        pool.dma_start(ada[:, s, :], wada[:, ds(2 * t + s, 1), col:col + 1024]).then_inc(ada_in[s], 16)

        @block.scalar
        def _(act):
            steps = [0]

            def link(ins):
                steps[0] += 1
                ins.then_inc(act_step, 1)
                act.wait_ge(act_step, steps[0])

            def split_hi(slot, hi):
                act.activation(ws[:, slot, :, 0, :], raw_blocks(slot), ACT.Copy).then_inc(hi, 1)

            def split3_hi(n, group, need):
                act.wait_ge(raw3_in[n % 3], group * 32 + 32)
                if need is not None:
                    act.wait_ge(used3, need)
                split_hi(n % 3, hi3)

            def split4_hi(k, group, need, sem_used=used4):
                act.wait_ge(raw4_in[k], group * 32)
                if need is not None:
                    act.wait_ge(sem_used, need)
                split_hi(SLOT4[k], hi4)

            def norm_factor(n, srcs, junk_, col, count, done, rooted):
                for i in range(n):
                    act.activation(junk_, srcs[i], ACT.Square, accum_out=stat[:, col + i:col + i + 1]).then_inc(done, 1)

            def to_h(first, hb, sc, sh, need_free):
                for kt in range(KT):
                    n = first * KT + kt
                    if kt % 2 == 0:
                        act.wait_ge(xT_done, n + 1)
                        if kt >= 4:
                            act.wait_ge(h_ready, n - 3)
                        act.activation(hb[:, kt % 4, :], ps[:, 4 + kt % 4, 0:TOK], ACT.Identity,
                                       bias=mods[:, sh, kt:kt + 1], scale=mods[:, sc, kt:kt + 1]).then_inc(h_even, 1)
                        act.wait_ge(h_even, n // 2 + 1)
                    else:
                        act.wait_ge(h_odd, n // 2 + 1)
                    act.activation(hT[:, kt, 0:TOK], hb[:, kt % 4, :], ACT.Copy).then_inc(h_hi, 1)

            act.dma_start(ccol[:, :], c[0].rearrange("(p t) -> p t", t=KT)).then_inc(c_in, 16)
            act.dma_start(xnat[:, :, :], x_v).then_inc(x_in, 16)
            act.dma_start(rows[0:96, 0, :], b_ada[0].rearrange("(r p) -> r p", p=P)).then_inc(rows_in, 16)
            for j, g in enumerate((g_pre_mix, g_post_mix, g_pre_ffn, g_post_ffn)):
                act.dma_start(rows[KT * j:KT * (j + 1), 1, :], g[0].rearrange("(r p) -> r p", p=P)).then_inc(rows_in, 16)
            act.dma_start(rows[64:66, 1, :], g_gla_head[0].rearrange("(r p) -> r p", p=P)).then_inc(rows_in, 16)
            for j in range(3):
                act.dma_start(rows[0:2 * FT, 2 + j, :], w_conv[0, j].rearrange("(r p) -> r p", p=P)).then_inc(rows_in, 16)
            act.dma_start(rows[0:2 * FT, 5, :], b_conv[0].rearrange("(r p) -> r p", p=P)).then_inc(rows_in, 16)
            act.dma_start(walpha[0:RANK, :], w_alpha_up[0]).then_inc(gate_in, 16)
            act.dma_start(balpha[0:1, :], b_alpha).then_inc(gate_in, 16)
            act.wait_ge(c_in, 16)
            act.activation(scol[:, :], ccol[:, :], ACT.Silu).then_inc(scol_ready, 1)
            act.wait_ge(x_in, 16)
            act.wait_ge(pool_step, 2)
            for tt in range(TT):
                act.activation(junk[:, :], xnat[:, tt, :], ACT.Square, accum_out=stat[:, tt:tt + 1]).then_inc(xsq, 1)
                act.wait_ge(xsq, tt + 1)
            act.activation(stat[:, 2:4], stat[:, 0:2], ACT.Sqrt, scale=1.0 / D, bias=eps[:, :]).then_inc(xsqrt, 1)
            act.wait_ge(mods_ready, 1)
            to_h(0, h32, M_SC1, M_SH1, None)
            for n in range(3):
                split3_hi(n, 0, None)

            act.wait_ge(used3, 1)
            act.activation(galow_x[0:RANK, :], ps[0:RANK, 6, TOK:2 * TOK], ACT.Copy).then_inc(low_x, 1)
            split3_hi(0, 1, 1)
            act.wait_ge(z_done, 1)
            act.activation(zabs[:, :, :], ps[:, 4:6, :], ACT.Abs).then_inc(z_abs, 1)
            act.wait_ge(z_abs, 1)
            link(act.activation(zabs[:, :, :], zabs[:, :, :], ACT.Exp, scale=-1.0))
            act.activation(zabs[:, :, :], zabs[:, :, :], ACT.Ln, bias=1.0).then_inc(z_ln, 1)

            def tail(prev, n):
                if n == 0:
                    for hd in range(2):
                        act.wait_ge(pt_done, 2 * prev + hd + 1)
                        act.activation(pT[:, hd, :], ps[:, 6 + hd, 0:3 * P], ACT.Copy).then_inc(ptc_done, 1)
                    act.wait_ge(ss_done, prev + 1)
                    act.activation(rs[:, :], ps[:, 5, 0:TOK], ACT.Sqrt, scale=1.0 / DV, bias=eps[:, :]).then_inc(rs_done, 1)
                    act.wait_ge(evac, 12 * prev + 12 + 4)
                    act.activation(tg[:, :, :], grt[:, :, :], ACT.Tanh, scale=0.5).then_inc(tanh_done, 1)
                if n == 2:
                    act.wait_ge(og_f, prev + 1)
                    act.activation(og[:, ds(2 * prev, 2), 0:TOK], ot[:, :, :], ACT.Copy).then_inc(og_hi, 1)
                    act.wait_ge(pv_done, prev + 1)
                    act.activation(om[:, ds(2 * prev, 2), 0:TOK], ps[:, 6:8, 0:TOK], ACT.Copy).then_inc(om_hi, 1)

            def head_pass(I, first):
                for n in range(HEAD_N):
                    a = HEAD_N * I + A_HEAD + n
                    if n % 2 == 1:
                        g = n // 2
                        b = 2 * (g % 2)
                        act.wait_ge(used3, a + 1)
                        act.wait_ge(evac, 12 * I + 2 * g + 2)
                        if g == 0:
                            act.activation(tmp[:, 0, 0, :], ps[:, 0, TOK:], ACT.Copy, scale=SCALE).then_inc(cross, 1)
                            act.activation(tmp[:, 0, 1, :], ps[:, 1, TOK:], ACT.Copy).then_inc(cross, 1)
                        else:
                            act.activation(tmp[:, g % 2, :, :], ps[:, b:b + 2, TOK:], ACT.Copy).then_inc(cross, 1)
                    split3_hi(1 + n, 4 * I + (1 + n + 3) // 3, a + 1)
                    if not first:
                        tail(I - 1, n)
                    if n == 3:
                        act.wait_ge(gram_done, 9 * I + 2)
                        act.activation(A[:, 1, :], ps[:, 5, 0:P], ACT.Copy).then_inc(a01_done, 1)
                    for p in ((0, 1) if n == 0 else (n,) if 2 <= n <= 7 else ()):
                        act.wait_ge(e_ready, 8 * I + p + 1)
                        act.activation(eb[:, p % 2, :], eb[:, p % 2, :], ACT.Exp).then_inc(exp_done, 1)
                    if n == 9:
                        act.wait_ge(nb_ready, I + 1)
                        for hd in range(2):
                            for qt in range(TT):
                                v = ssb[:, hd, TOK * qt:TOK * (qt + 1)]
                                j = 2 * hd + qt
                                act.activation(v, v, ACT.Exp, scale=SCALE, bias=stat[:, 20 + j:21 + j],
                                               accum_out=stat[:, 24 + j:25 + j]).then_inc(p_ready, 1)
                    if n == 11:
                        act.wait_ge(av_done, I + 1)
                        act.activation(ot[:, :, :], ps[:, 4, :].rearrange("p (e t) -> p e t", e=2), ACT.Copy).then_inc(ot_done, 1)
                        act.activation(sq[:, :, :], ps[:, 4, :].rearrange("p (e t) -> p e t", e=2), ACT.Square).then_inc(sq_done, 1)

            head_pass(0, True)
            with act.Fori(1, HEADS) as I:
                head_pass(I, False)

            def merge_pass(i, first):
                for n in range(PASS_N):
                    J, m = 2 * i + n // MERGE_N, n % MERGE_N
                    a = PASS_N * i + A_MERGE + n
                    if m in (1, 3, 4, 5):
                        g = {1: 0, 3: 1, 4: 2, 5: 3}[m]
                        act.wait_ge(used3, a + 1)
                        act.wait_ge(evac3, 8 * J + 2 * g + 6)
                        act.activation(tmp3[:, g % 2, :, :], ps[:, 2 * g:2 * g + 2, TOK:], ACT.Copy).then_inc(cross3, 1)
                    split3_hi(1 + n, 4 * i + 16 + (1 + n + 3) // 3, a + 1)
                    if m in (1, 3):
                        act.wait_ge(evac3, 8 * J + 2 * (g + 1) + 8)
                        act.activation(sg[:, g, :, :], gx[:, g, :, :], ACT.Sigmoid).then_inc(sig_done, 1)
                    if first:
                        tail(HEADS - 1, n)

            merge_pass(0, True)
            with act.Fori(1, 4) as i:
                merge_pass(i, False)

            def merged_hi(kt):
                act.activation(hT[:, kt, 0:TOK], mT[:, kt, :], ACT.Copy).then_inc(m_hi, 1)

            act.wait_ge(m_done, 8)
            act.wait_ge(used3, A_WO)
            for kt in range(4):
                merged_hi(kt)
            split4_hi(3, 1, None)
            act.wait_ge(g_done, 1)
            act.activation(G[:, :], ps[:, 0:4, :].rearrange("p b n -> p (b n)"), ACT.Copy).then_inc(g_ready, 1)
            for w in range(4, KT + 4):
                if w < 7:
                    split4_hi(w % 4, w // 4, A_WO + w - 4 + 1, used3)
                else:
                    split4_hi(w % 4, arrived4(w, w % 4), w - 6)
                if w < KT:
                    merged_hi(w)

            act.wait_ge(used4, KT - 3)
            for j in range(8):
                act.activation(junk2[:, 0:512], ps[:, j, :], ACT.Square, accum_out=stat[:, 32 + j:33 + j]).then_inc(ysq, 1)
                act.wait_ge(ysq, j + 1)
            act.wait_ge(ysqrt, 1)
            act.activation(stat[:, 4:6], stat[:, 4:6], ACT.Sqrt, scale=1.0 / D, bias=eps[:, :]).then_inc(ysqrt, 1)
            for tt in range(TT):
                act.wait_ge(x2_ready, tt + 1)
                act.activation(junk2[:, :], x2[:, tt, :], ACT.Square, accum_out=stat[:, 6 + tt:7 + tt]).then_inc(xsq, 1)
                act.wait_ge(xsq, TT + tt + 1)
            act.activation(stat[:, 6:8], stat[:, 6:8], ACT.Sqrt, scale=1.0 / D, bias=eps[:, :]).then_inc(xsqrt, 1)
            act.wait_ge(g_done, 2)
            act.activation(G[:, :], ps[:, 0:4, :].rearrange("p b n -> p (b n)"), ACT.Copy).then_inc(g_ready, 1)
            to_h(1, h32b, M_SC2, M_SH2, None)

            def up_tasks(i, n):
                g = (n - 1) // 2
                q = 2 * i + g
                act.wait_ge(used4, 4 * i + W_UP + n - 2)
                act.wait_ge(conv_done, q + 2)
                act.activation(cv[:, :, :], ps[:, 2 * g:2 * g + 2, TOK:], ACT.Copy).then_inc(cross5, 1)
                act.wait_ge(up_ready, q + 1)
                for ct in range(2):
                    f = 2 * i + FT * g + ct
                    act.activation(cv[:, ct, :], up[:, ct, 2:], ACT.Identity, scale=cols[:, ds(f + COL_CONV + 4 * FT, 1)],
                                   bias=cols[:, ds(f + COL_CB, 1)]).then_inc(cb_done, 1)
                if g == 1:
                    act.wait_ge(conv_g, i + 1)
                    act.activation(cv[:, :, :], cv[:, :, :], ACT.Gelu_apprx_tanh).then_inc(gelu_done, 1)

            with act.Fori(0, UP_ITERS) as i:
                for n in range(4):
                    split4_hi(n, i + (W_UP + 4) // 4 + (n == 3), 4 * i + W_UP + n + 4 - 6)
                    if n % 2 == 1:
                        up_tasks(i, n)

            def act_hi(kt, k, need):
                if need is not None:
                    act.wait_ge(used4, need)
                act.activation(asp[:, k, 0:TOK], aT[:, ds(kt, 1), :], ACT.Copy).then_inc(a_hi, 1)

            act.wait_ge(conv_done, 2 + 2 * UP_ITERS)
            act.wait_ge(used4, W_DOWN - 3)
            for k in range(4):
                act_hi(k, k, None)
            with act.Fori(0, FT // 4 - 1) as i:
                for n in range(4):
                    act_hi(4 * i + 4 + n, n, 4 * i + W_DOWN + n + 4 - 6)
                    split4_hi(n, i + (W_DOWN + 4) // 4 + (n == 3), 4 * i + W_DOWN + n + 4 - 6)
            act.wait_ge(used4, W_DOWN + FT - 3)
            for j in range(8):
                act.activation(junk3[:, 0:512], ps[:, j, :], ACT.Square, accum_out=stat[:, 32 + j:33 + j]).then_inc(ysq, 1)
                act.wait_ge(ysq, 8 + j + 1)
            act.wait_ge(ysqrt, 3)
            act.activation(stat[:, 4:6], stat[:, 4:6], ACT.Sqrt, scale=1.0 / D, bias=eps[:, :]).then_inc(ysqrt, 1)

        @block.vector
        def _(dve):
            steps = [0]

            class Loop:
                def __init__(self, base, i=None, size=0, sem=dve_step):
                    self.base, self.i, self.size, self.k, self.sem = base, i, size, 0, sem

                def link(self, ins, wait=True):
                    ins.then_inc(self.sem, 1)
                    self.k += 1
                    if wait:
                        self.wait()

                def wait(self, k=None):
                    k = self.k if k is None else k
                    if self.i is None:
                        dve.wait_ge(self.sem, self.base + k)
                    else:
                        dve.wait_ge(self.sem, self.i * self.size + (self.base + k))

            S = Loop(0)
            link = S.link

            def split_lo(slot, hi, need, done):
                dve.wait_ge(hi, need)
                dve.tensor_tensor(ws[:, slot, :, 1, :], raw_blocks(slot), ws[:, slot, :, 0, :].bitcast(F32),
                                  ALU.subtract).then_inc(done, 1)

            def ada_units(q, n):
                done = sum(ADA_UNITS[:n])
                for k in range(done, done + ADA_UNITS[n]):
                    dve.wait_ge(ada_in[k % 2], (KT // 2 * q + k // 2) * 16 + 16)
                    if k == 0:
                        ins = dve.tensor_scalar(acc[:, :], ada[:, 0, :], scol[:, 0:1], None, ALU.mult)
                    else:
                        dve.wait_ge(ada_used, KT * q + k + 2)
                        ins = dve.scalar_tensor_tensor(acc[:, :], ada[:, k % 2, :], scol[:, k:k + 1], acc[:, :], ALU.mult, ALU.add)
                    ins.then_inc(ada_used, 1)

            def part_sums(q):
                dve.wait_ge(mod_done, q + 1)
                dve.tensor_copy(modsf[:, ds(8 * q + (M_GT1 * KT - 8), 8)], ps[:, 4, 0:8]).then_inc(part_read, 1)

            def to_h(first, hb, sc, sh):
                for kt in range(KT):
                    n = first * KT + kt
                    if kt % 2 == 1:
                        dve.wait_ge(xT_done, n + 1)
                        dve.tensor_scalar(hb[:, kt % 4, :], ps[:, 4 + kt % 4, 0:TOK], mods[:, sc, kt:kt + 1],
                                          mods[:, sh, kt:kt + 1], ALU.mult, ALU.add).then_inc(h_odd, 1)
                    dve.wait_ge(h_hi, n + 1)
                    dve.tensor_tensor(hT[:, kt, TOK:2 * TOK], hb[:, kt % 4, :], hT[:, kt, 0:TOK].bitcast(F32),
                                      ALU.subtract).then_inc(h_ready, 1)

            dve.memset(acc0[:, :], 0.0).then_inc(head_used, 4)
            dve.memset(stat[:, 12:13], 0.0).then_inc(ada_used, 2)
            dve.memset(stat[:, 8:9], 0.0).then_inc(split3, 3)
            dve.memset(stat[:, 9:10], 0.0).then_inc(evac, 4)
            dve.memset(stat[:, 10:11], 0.0).then_inc(evac3, 8)
            dve.memset(stat[:, 11:12], 0.0).then_inc(conv_done, 2)
            dve.wait_ge(scol_ready, 1)

            def head_units(lo, hi):
                with dve.Fori(lo, hi) as i:
                    for j in range(4):
                        dve.wait_ge(head_in[j], i * 16 + 16)
                        dve.wait_ge(head_used, 4 * i + j + 3)
                        v = acc0[:, (j % 2) * D:(j % 2 + 1) * D]
                        dve.scalar_tensor_tensor(v, raw[:, j, :], scol[:, ds(2 * i + j // 2, 1)], v,
                                                 ALU.mult, ALU.add).then_inc(head_used, 1)

            head_units(0, 3)
            dve.wait_ge(colsT, 1)
            link(dve.tensor_copy(cols[:, 0:426], ps[:, 0, 0:426]), wait=False)
            link(dve.tensor_copy(cols[:, 426:NCOL], ps[:, 1, 0:NCOL - 426]))
            link(dve.tensor_scalar(cols[:, COL_GH:COL_GH + 2], cols[:, COL_GH:COL_GH + 2], 0.5, None, ALU.mult), wait=False)
            dve.wait_ge(pool_step, 38)
            link(dve.tensor_copy(mask8[:, :, :], maskf[:, :, :]), wait=False)
            dve.wait_ge(xsqrt, 1)
            link(dve.reciprocal(stat[:, 2:4], stat[:, 2:4]))
            for tt in range(TT):
                dve.tensor_scalar(xn[:, tt, :], xnat[:, tt, :], stat[:, 2 + tt:3 + tt], None, ALU.mult).then_inc(xn_ready, 1)
            head_units(3, KT // 2)

            dve.wait_ge(mod_done, 1)
            link(dve.tensor_tensor(mods[:, M_SH1:M_SC1 + 1, :], ps[:, 2, 0:2 * KT].rearrange("p (m k) -> p m k", m=2),
                                   cols[:, 0:2 * KT].rearrange("p (m k) -> p m k", m=2), ALU.add))
            dve.scalar_tensor_tensor(mods[:, M_SC1, :], mods[:, M_SC1, :], 1.0, cols[:, COL_PRE1:COL_PRE1 + KT],
                                     ALU.add, ALU.mult).then_inc(mods_ready, 1)
            to_h(0, h32, M_SC1, M_SH1)
            for n in range(3):
                split_lo(n, hi3, n + 1, split3)

            dve.wait_ge(low_x, 1)
            dve.tensor_tensor(galow[0:RANK, :], ps[0:RANK, 6, 0:TOK], galow_x[0:RANK, :], ALU.add).then_inc(low_ready, 1)
            split_lo(0, hi3, 4, split3)
            dve.wait_ge(z_abs, 1)
            link(dve.tensor_scalar(zmin[:, :, :], ps[:, 4:6, :], 0.0, None, ALU.min))
            dve.wait_ge(z_ln, 1)
            dve.tensor_tensor(loga[:, :, :], zmin[:, :, :], zabs[:, :, :], ALU.subtract).then_inc(la_ready, 1)
            dve.wait_ge(tri_done, 1)
            dve.tensor_copy(bT[:, :, :].rearrange("p h t -> p (h t)"), ps[:, 6:8, :].rearrange("p b n -> p (b n)")).then_inc(bT_ready, 1)
            dve.wait_ge(bT_ready, 1)

            def level_decay(L, I, p):
                s = P if p == 0 else 2 ** (p - 1)
                v = bc[:, :].rearrange("p (g two s) -> p g two s", two=2, s=s)
                e = eb[:, p % 2, :].rearrange("p (g two s) -> p g two s", two=2, s=s)
                grp = TOK // (2 * s)
                ref = v[:, :, 0, s - 1:s].to_broadcast([P, grp, s])
                if p >= 2:
                    dve.wait_ge(level_ready, 8 * I + p - 1)
                dve.tensor_tensor(e[:, :, 0, :], ref, v[:, :, 0, :], ALU.subtract)
                if p == 0:
                    last = dve.tensor_copy(e[:, :, 1, :], v[:, :, 1, :])
                else:
                    last = dve.tensor_tensor(e[:, :, 1, :], v[:, :, 1, :], ref, ALU.subtract)
                last.then_inc(e_ready, 1)

            def level_operands(I, p):
                s = P if p == 0 else 2 ** (p - 1)
                def halves(t):
                    return t.rearrange("p (g two s) -> p g two s", two=2, s=s)
                e, m = halves(eb[:, p % 2, :]), halves(Mb[:, p % 2, :])
                dve.wait_ge(exp_done, 8 * I + p + 1)
                if p >= 2:
                    dve.wait_ge(gram_done, 9 * I + p)
                dve.tensor_tensor(m[:, :, 0, :], halves(qk[:, 1, :])[:, :, 0, :], e[:, :, 0, :], ALU.mult)
                dve.tensor_tensor(m[:, :, 1, :], halves(qk[:, 0, :])[:, :, 1, :], e[:, :, 1, :], ALU.mult).then_inc(level_ready, 1)

            def before_select(I, lv):
                if lv:
                    dve.wait_ge(select_done, 8 * I + lv)
                dve.wait_ge(gram_done, 9 * I + (1 if lv == 0 else lv + 2))

            def select(I, lv):
                bank = 4 if lv == 0 or lv % 2 else 5
                dve.copy_predicated(A[:, 0:3:2, :], mask8[:, lv, :].unsqueeze(1).to_broadcast([P, 2, P]),
                                    ps[:, bank, 0:TOK].rearrange("p (t i) -> p t i", t=2)).then_inc(select_done, 1)

            def evacuate(I, g, dst):
                b = 2 * (g % 2)
                dve.wait_ge(cross, 7 * I + g + 2)
                dve.tensor_tensor(dst, ps[:, b:b + 2, 0:TOK], tmp[:, g % 2, :, :], ALU.add).then_inc(evac, 2)

            TAIL_STEPS = 3

            def tail(prev, n):
                if n == 1:
                    T = Loop(0, prev, TAIL_STEPS, tail_step)
                    dve.wait_ge(tanh_done, prev + 1)
                    dve.wait_ge(rs_done, prev + 1)
                    T.link(dve.reciprocal(rs[:, :], rs[:, :]), wait=False)
                    T.link(dve.scalar_tensor_tensor(tg[:, :, :], tg[:, :, :], 1.0, grt[:, :, :], ALU.add, ALU.mult), wait=False)
                    dve.wait_ge(ot_done, prev + 1)
                    T.wait(1)
                    T.link(dve.tensor_tensor(ot[:, :, :], ot[:, :, :], rs[:, :].unsqueeze(1).to_broadcast([P, 2, TOK]), ALU.mult))
                    assert T.k == TAIL_STEPS
                    for e in range(2):
                        ins = dve.scalar_tensor_tensor(ot[:, e, :], ot[:, e, :], cols[:, COL_GH + e:COL_GH + e + 1],
                                                       tg[:, e, :], ALU.mult, ALU.mult)
                    ins.then_inc(og_f, 1)
                if n == 2:
                    dve.wait_ge(og_hi, prev + 1)
                    dve.tensor_tensor(og[:, ds(2 * prev, 2), TOK:], ot[:, :, :],
                                      og[:, ds(2 * prev, 2), 0:TOK].bitcast(F32), ALU.subtract).then_inc(og_ready, 1)
                if n == 3:
                    dve.wait_ge(om_hi, prev + 1)
                    dve.tensor_tensor(om[:, ds(2 * prev, 2), TOK:], ps[:, 6:8, 0:TOK],
                                      om[:, ds(2 * prev, 2), 0:TOK].bitcast(F32), ALU.subtract).then_inc(om_ready, 1)

            HEAD_STEPS = 7

            def head_pass(I, first):
                L = Loop(head_start, I, HEAD_STEPS)
                for n in range(HEAD_N):
                    a = HEAD_N * I + A_HEAD + n
                    if n == 0:
                        L.link(dve.tensor_copy(bc[:, :], bT[:, ds(I, 1), :]))
                        level_decay(L, I, 0)
                        level_decay(L, I, 1)
                    if n == 1:
                        dve.wait_ge(cross, 7 * I + 1)
                        dve.scalar_tensor_tensor(qk[:, 0, :], ps[:, 0, 0:TOK], SCALE, tmp[:, 0, 0, :],
                                                 ALU.mult, ALU.add).then_inc(evac, 1)
                        dve.wait_ge(cross, 7 * I + 2)
                        dve.tensor_tensor(qk[:, 1, :], ps[:, 1, 0:TOK], tmp[:, 0, 1, :], ALU.add).then_inc(evac, 1)
                    if n == 9:
                        for hd in range(2):
                            dve.wait_ge(qk_done, 2 * I + hd + 1)
                            L.link(dve.tensor_tensor(ssb[:, hd, :], ps[:, 6 + hd, :], causal[:, :], ALU.add))
                            L.link(dve.reduce_max(stat[:, 16 + 2 * hd:18 + 2 * hd],
                                                  ssb[:, hd, :].rearrange("p (t k) -> p t k", t=TT), AX.X), wait=hd == 1)
                        dve.tensor_scalar(stat[:, 20:24], stat[:, 16:20], -SCALE, None, ALU.mult).then_inc(nb_ready, 1)
                    if n == 2:
                        L.link(dve.memset(A[:, 0:3:2, :], 0.0), wait=False)
                        dve.wait_ge(evac, 12 * I + 2 + 4)
                        level_operands(I, 0)
                        level_operands(I, 1)
                    if 3 <= n <= 10:
                        if n == 3:
                            dve.wait_ge(dve_step, I * HEAD_STEPS + (head_start + 2))
                        before_select(I, max(n - 3, 0))
                        if n - 1 <= 7:
                            level_operands(I, n - 1)
                        if n == 9:
                            evacuate(I, 4, mv[:, :, :])
                        if n == 10:
                            dve.wait_ge(p_ready, 4 * I + 4)
                            L.link(dve.reciprocal(stat[:, 28:32], stat[:, 24:28]), wait=False)
                        select(I, n - 3)
                    if 2 <= n <= 7:
                        level_decay(L, I, n)
                    if n in (3, 5, 7, 11):
                        evacuate(I, n // 2, {3: vv[:, :, :], 5: mqk[:, 0, :, :], 7: mqk[:, 1, :, :], 11: grt[:, :, :]}[n])
                    if n == 10:
                        L.wait()
                        for hd in range(2):
                            for qt in range(TT):
                                v = ssb[:, hd, TOK * qt:TOK * (qt + 1)]
                                j = 28 + 2 * hd + qt
                                ins = dve.tensor_scalar(v, v, stat[:, j:j + 1], None, ALU.mult)
                            ins.then_inc(pn_ready, 1)
                    if not first:
                        tail(I - 1, n)
                        if n == 1:
                            part_sums(I)
                    ada_units(I, n)
                    split_lo((1 + n) % 3, hi3, a + 3 + 1, split3)
                assert L.k == HEAD_STEPS, L.k

            head_start = S.base + S.k
            head_pass(0, True)
            with dve.Fori(1, HEADS) as I:
                head_pass(I, False)
            S.base += HEADS * HEAD_STEPS

            def diagonal(G, m):
                for j in range(KT):
                    ins = dve.tensor_scalar(G[:, P * j:P * (j + 1)], ident[:, :], mods[:, m, j:j + 1], None, ALU.mult)
                ins.then_inc(dg_ready, 1)

            link(dve.tensor_tensor(mods[:, M_GT1, :], mods[:, M_GT1, :], cols[:, M_GT1 * KT:(M_GT1 + 1) * KT], ALU.add))
            link(dve.tensor_tensor(mods[:, M_GT1, :], mods[:, M_GT1, :], cols[:, COL_POST1:COL_POST1 + KT], ALU.mult))
            diagonal(G, M_GT1)

            MERGE_STEPS = 2

            def merge_pass(i, first):
                for n in range(PASS_N):
                    J, m = 2 * i + n // MERGE_N, n % MERGE_N
                    a = PASS_N * i + A_MERGE + n
                    if m == 0:
                        L = Loop(merge_start, J, MERGE_STEPS)
                    if m in (1, 3):
                        g = m // 2
                        dve.wait_ge(cross3, 4 * J + g + 1)
                        dve.tensor_tensor(gx[:, g, :, :], ps[:, 2 * g:2 * g + 2, 0:TOK], tmp3[:, g, :, :], ALU.add).then_inc(evac3, 2)
                    if m in (4, 5):
                        g = m - 2
                        y = ya if m == 4 else yb
                        dve.wait_ge(cross3, 4 * J + g + 1)
                        dve.tensor_tensor(y[:, :, :], ps[:, 2 * g:2 * g + 2, 0:TOK], tmp3[:, g % 2, :, :], ALU.add).then_inc(evac3, 2)
                        dve.wait_ge(evac3, 8 * J + 2 * (g + 1) + 8)
                        dve.wait_ge(sig_done, 2 * J + g - 1)
                        L.link(dve.tensor_tensor(y[:, :, :], y[:, :, :], sg[:, g - 2, :, :], ALU.mult), wait=m == 5)
                    if m == 5:
                        dve.tensor_tensor(mT[:, ds(2 * J, 2), :], ya[:, :, :], yb[:, :, :], ALU.add).then_inc(m_done, 1)
                        assert L.k == MERGE_STEPS
                    if first:
                        tail(HEADS - 1, n)
                    if n == 1:
                        part_sums(HEADS + i)
                    ada_units(HEADS + i, n)
                    split_lo((1 + n) % 3, hi3, a + 3 + 1, split3)

            merge_start = S.base + S.k
            merge_pass(0, True)
            with dve.Fori(1, 4) as i:
                merge_pass(i, False)
            S.base += 8 * MERGE_STEPS

            def merged_lo(kt):
                dve.wait_ge(m_hi, kt + 1)
                dve.tensor_tensor(hT[:, kt, TOK:], mT[:, kt, :], hT[:, kt, 0:TOK].bitcast(F32), ALU.subtract).then_inc(m_ready, 1)

            for kt in range(4):
                merged_lo(kt)
            part_sums(PARTS)
            split_lo(3, hi4, 1, split4)
            for w in range(4, KT + 4):
                split_lo(SLOT4[w % 4], hi4, w - 2, split4)
                if w == 4:
                    dve.wait_ge(part_read, PARTS)
                    link(dve.tensor_tensor(mods[:, M_SH2:, :], mods[:, M_SH2:, :],
                                           cols[:, M_SH2 * KT:6 * KT].rearrange("p (m k) -> p m k", m=3), ALU.add))
                    link(dve.tensor_tensor(mods[:, M_GT2, :], mods[:, M_GT2, :], cols[:, COL_POST2:COL_POST2 + KT], ALU.mult), wait=False)
                    dve.scalar_tensor_tensor(mods[:, M_SC2, :], mods[:, M_SC2, :], 1.0, cols[:, COL_PRE2:COL_PRE2 + KT],
                                             ALU.add, ALU.mult).then_inc(mods_ready, 1)
                if w == 6:
                    S.wait()
                    diagonal(dg2, M_GT2)
                if w < KT:
                    merged_lo(w)

            def factors(ysq_count, root):
                dve.wait_ge(ysq, ysq_count)
                dve.reduce_sum(stat[:, 4:6], stat[:, 32:40].rearrange("p (t b) -> p t b", t=TT), AX.X).then_inc(ysqrt, 1)
                dve.wait_ge(ysqrt, root)
                link(dve.reciprocal(stat[:, 4:6], stat[:, 4:6]))

            def gated(dst, tt):
                for b in range(4):
                    ins = dve.scalar_tensor_tensor(dst[:, tt, 512 * b:512 * (b + 1)], ps[:, 4 * tt + b, :], stat[:, 4 + tt:5 + tt],
                                                   G[:, 512 * b:512 * (b + 1)], ALU.mult, ALU.mult)
                link(ins)

            factors(8, 2)
            dve.wait_ge(xr_in, 16)
            dve.wait_ge(g_ready, 1)
            for tt in range(TT):
                gated(yt, tt)
                dve.tensor_tensor(x2[:, tt, :], x2[:, tt, :], yt[:, tt, :], ALU.add).then_inc(x2_ready, 1)
            dve.wait_ge(xsqrt, 2)
            link(dve.reciprocal(stat[:, 6:8], stat[:, 6:8]))
            for tt in range(TT):
                dve.tensor_scalar(yt[:, tt, :], x2[:, tt, :], stat[:, 6 + tt:7 + tt], None, ALU.mult).then_inc(xn_ready, 1)
            to_h(1, h32b, M_SC2, M_SH2)
            link(dve.memset(up[:, :, 0:2], 0.0))

            UP_STEPS = 4
            start = S.base + S.k
            with dve.Fori(0, UP_ITERS) as i:
                L = Loop(start, i, UP_STEPS)
                for n in range(4):
                    split_lo(SLOT4[n], hi4, 4 * i + W_UP + n + 4 - 2, split4)
                    if n % 2 == 0:
                        continue
                    g = n // 2
                    q = 2 * i + g
                    dve.wait_ge(cross5, q + 1)
                    dve.tensor_tensor(up[:, :, 2:], ps[:, 2 * g:2 * g + 2, 0:TOK], cv[:, :, :], ALU.add).then_inc(up_ready, 1)
                    for ct in range(2):
                        f = 2 * i + FT * g + ct
                        dve.wait_ge(cb_done, 2 * q + ct + 1)
                        L.link(dve.scalar_tensor_tensor(cv[:, ct, :], up[:, ct, 1:TOK + 1], cols[:, ds(f + COL_CONV + 2 * FT, 1)],
                                                        cv[:, ct, :], ALU.mult, ALU.add), wait=ct == 1)
                    dst = cv if g else ub
                    for ct in range(2):
                        f = 2 * i + FT * g + ct
                        ins = dve.scalar_tensor_tensor(dst[:, ct, :], up[:, ct, 0:TOK], cols[:, ds(f + COL_CONV, 1)],
                                                       cv[:, ct, :], ALU.mult, ALU.add)
                    ins.then_inc(conv_g if g else conv_done, 1)
                    if g:
                        dve.wait_ge(gelu_done, i + 1)
                        dve.tensor_tensor(aT[:, ds(2 * i, 2), :], cv[:, :, :], ub[:, :, :], ALU.mult).then_inc(conv_done, 1)
            assert L.k == UP_STEPS, L.k
            S.base += UP_ITERS * UP_STEPS

            def act_lo(kt, k):
                dve.wait_ge(a_hi, kt + 1)
                dve.tensor_tensor(asp[:, k, TOK:], aT[:, ds(kt, 1), :], asp[:, k, 0:TOK].bitcast(F32), ALU.subtract).then_inc(a_ready, 1)

            for k in range(4):
                act_lo(k, k)
            with dve.Fori(0, FT // 4 - 1) as i:
                for n in range(4):
                    act_lo(4 * i + 4 + n, n)
                    split_lo(SLOT4[n], hi4, 4 * i + W_DOWN + n + 4 - 2, split4)
            factors(16, 4)
            dve.wait_ge(g_ready, 2)
            for tt in range(TT):
                gated(yo, tt)
                dve.tensor_tensor(yo[:, tt, :], yo[:, tt, :], x2[:, tt, :], ALU.add).then_inc(out_ready, 1)

        @block.tensor
        def _(pe):
            def mm(out_, lhsT, rhs, start=True, stop=True):
                return pe.matmul(out_, lhsT, rhs, start=start, stop=stop)

            def weights_still(slot, acts, k0, kn, bank, used):
                for k in range(8):
                    kk = k0 + k
                    for ct in range(2):
                        cs = slice(P * ct, P * (ct + 1))
                        mm(ps[:, bank + ct, :], ws[:, slot, k, 0, cs], acts[:, kk, :], kk == 0, False)
                        last = mm(ps[:, bank + ct, TOK:], ws[:, slot, k, 1, cs], acts[:, kk, 0:TOK], False, kk == kn - 1)
                last.then_inc(used, 1)

            def tokens_still(slot, k0, bank, used):
                for k in range(8):
                    kk = k0 + k
                    for tt in range(TT):
                        mm(ps[:, bank + tt, :], hT[:, kk, P * tt:P * (tt + 1)], ws[:, slot, k, :, :], kk == 0, False)
                        last = mm(ps[:, bank + tt, TOK:], hT[:, kk, TOK + P * tt:TOK + P * (tt + 1)], ws[:, slot, k, 0, :], False, kk == KT - 1)
                last.then_inc(used, 1)

            def one_row_tile(slot, acts, first, last_, used, order=(0, 1), done=True):
                for tt in order:
                    hi, lo = acts[:, P * tt:P * (tt + 1)], acts[:, TOK + P * tt:TOK + P * (tt + 1)]
                    for b in range(4):
                        w_hi, w_lo = ws[:, slot, 2 * b:2 * b + 2, 0, :], ws[:, slot, 2 * b:2 * b + 2, 1, :]
                        mm(ps[:, 4 * tt + b, :], hi, w_hi, first, False)
                        mm(ps[:, 4 * tt + b, :], hi, w_lo, False, False)
                        ins = mm(ps[:, 4 * tt + b, :], lo, w_hi, False, last_)
                if done:
                    ins.then_inc(used, 1)

            def transposed(first, src):
                for kt in range(KT):
                    if kt >= 4:
                        pe.wait_ge(h_odd if kt % 2 else h_even, first * (KT // 2) + (kt - 4) // 2 + 1)
                    for tt in range(TT):
                        if kt == 0:
                            pe.wait_ge(xn_ready, TT * first + tt + 1)
                        ins = pe.transpose(ps[:, 4 + kt % 4, P * tt:P * (tt + 1)], src[:, tt, P * kt:P * (kt + 1)], ident[:, :])
                    ins.then_inc(xT_done, 1)

            def column_sums(a, col, bank, at_):
                for j in range(KT):
                    ins = mm(ps[:, bank, at_ + j:at_ + j + 1], a[:, col + P * j:col + P * (j + 1)], ones[:, 0:1])
                return ins

            def lay_out(dg):
                for b in range(4):
                    ins = mm(ps[:, b, :], ones[:, :], dg[:, 512 * b:512 * (b + 1)])
                ins.then_inc(g_done, 1)

            pe.wait_ge(pool_step, 4)
            pe.wait_ge(rows_in, 160)
            pe.transpose(ps[:, 0, 0:96], rows[0:96, 0, :], ident[0:96, 0:96])
            pe.transpose(ps[:, 0, 96:162], rows[0:66, 1, :], ident[0:66, 0:66])
            nc_ = 2 * FT
            for j in range(3):
                pe.transpose(ps[:, 0, COL_CONV + nc_ * j:COL_CONV + nc_ * (j + 1)], rows[0:nc_, 2 + j, :], ident[0:nc_, 0:nc_])
            pe.transpose(ps[:, 1, 0:nc_], rows[0:nc_, 5, :], ident[0:nc_, 0:nc_]).then_inc(colsT, 1)
            pe.wait_ge(head_used, 4 + 32)
            column_sums(acc0, 0, 2, 0)
            column_sums(acc0, D, 2, KT).then_inc(mod_done, 1)
            transposed(0, xn)

            pe.wait_ge(h_ready, KT)
            pe.wait_ge(split3, 0 + 4)
            for k in range(KT):
                cs = slice(P * (k % 2), P * (k % 2 + 1))
                mm(ps[:, 6, :], ws[:, 0, k // 2, 0, cs], hT[:, k, :], k == 0, False)
                ins = mm(ps[:, 6, TOK:], ws[:, 0, k // 2, 1, cs], hT[:, k, 0:TOK], False, k == KT - 1)
            ins.then_inc(used3, 1)
            pe.wait_ge(low_ready, 1)
            pe.wait_ge(gate_in, 32)
            for tt in range(TT):
                mm(ps[:, 4 + tt, :], galow[0:RANK, P * tt:P * (tt + 1)], walpha[0:RANK, :], True, False)
                ins = mm(ps[:, 4 + tt, :], ones[0:1, :], balpha[0:1, :], False, True)
            ins.then_inc(z_done, 1)
            pe.wait_ge(la_ready, 1)
            for h in range(HEADS):
                for tt in range(TT):
                    col = TOK * (h % 2) + P * tt
                    ins = mm(ps[:, 6 + h // 2, col:col + P], loga[:, tt, P * h:P * (h + 1)], tri[:, :])
            ins.then_inc(tri_done, 1)

            def gram(I, p):
                bank = 4 if p % 2 else 5
                pe.wait_ge(level_ready, 8 * I + p + 1)
                if p == 0:
                    mm(ps[:, 5, 0:P], Mb[:, 0, 0:P], Mb[:, 0, P:]).then_inc(gram_done, 1)
                    return
                if p == 2:
                    pe.wait_ge(a01_done, I + 1)
                else:
                    pe.wait_ge(select_done, 8 * I + max(p - 1, 1))
                for t in range(TT):
                    m = Mb[:, p % 2, P * t:P * (t + 1)]
                    ins = mm(ps[:, bank, P * t:P * (t + 1)], m, m)
                ins.then_inc(gram_done, 1)

            def causal_product(out_, values, weights):
                mm(out_, values[0], weights[:, 0:2 * P], True, False)
                return mm(out_[:, P:2 * P], values[1], weights[:, 2 * P:3 * P], False, True)

            def part_sums(q):
                pe.wait_ge(ada_used, KT * q + 2)
                for j in range(8):
                    ins = mm(ps[:, 4, j:j + 1], acc[:, P * j:P * (j + 1)], ones[:, 0:1])
                ins.then_inc(mod_done, 1)

            def tail(prev, n):
                if n == 0:
                    for hd in range(2):
                        pe.wait_ge(pn_ready, 2 * prev + hd + 1)
                        for j, (qt, k) in enumerate(((0, 0), (1, 0), (1, 1))):
                            ins = pe.transpose(ps[:, 6 + hd, P * j:P * (j + 1)],
                                               ssb[:, hd, TOK * qt + P * k:TOK * qt + P * (k + 1)], ident[:, :])
                        ins.then_inc(pt_done, 1)
                    pe.wait_ge(sq_done, prev + 1)
                    mm(ps[:, 5, 0:TOK], ones[:, :], sq[:, 0, :], True, False)
                    mm(ps[:, 5, 0:TOK], ones[:, :], sq[:, 1, :], False, True).then_inc(ss_done, 1)
                if n == 2:
                    for hd in range(2):
                        es = slice(P * hd, P * (hd + 1))
                        pe.wait_ge(ptc_done, 2 * prev + hd + 1)
                        ins = causal_product(ps[:, 6 + hd, 0:TOK], (mv[:, 0, es], mv[:, 1, es]), pT[:, hd, :])
                    ins.then_inc(pv_done, 1)

            def head_pass(I, first):
                for n in range(HEAD_N):
                    a = HEAD_N * I + A_HEAD + n
                    g = n // 2
                    b = 2 * (g % 2)
                    if n % 2 == 0:
                        pe.wait_ge(evac, 12 * I + 2 * g + 2)
                    pe.wait_ge(split3, a + 4)
                    if g in (1, 4):
                        tokens_still((1 + n) % 3, 8 * (n % 2), b, used3)
                    else:
                        weights_still((1 + n) % 3, hT, 8 * (n % 2), KT, b, used3)
                    if not first:
                        tail(I - 1, n)
                        if n == 0:
                            part_sums(I)
                    if n == 3:
                        pe.wait_ge(evac, 12 * I + 2 + 4)
                        if not first:
                            pe.wait_ge(part_read, I)
                        for t in range(TT):
                            ts = slice(P * t, P * (t + 1))
                            ins = mm(ps[:, 4, ts], qk[:, 1, ts], qk[:, 0, ts])
                        ins.then_inc(gram_done, 1)
                    if 3 <= n <= 10:
                        gram(I, n - 3)
                    if n == 9:
                        pe.wait_ge(evac, 12 * I + 8 + 4)
                        for hd in range(2):
                            for qt in range(TT):
                                ins = mm(ps[:, 6 + hd, TOK * qt:TOK * (qt + 1)], mqk[:, 0, hd, P * qt:P * (qt + 1)], mqk[:, 1, hd, :])
                            ins.then_inc(qk_done, 1)
                    if n == 11:
                        pe.wait_ge(evac, 12 * I + 4 + 4)
                        pe.wait_ge(select_done, 8 * I + 8)
                        Af = A[:, :, :].rearrange("p j i -> p (j i)")
                        for e in range(2):
                            es = slice(P * e, P * (e + 1))
                            ins = causal_product(ps[:, 4, TOK * e:TOK * (e + 1)], (vv[:, 0, es], vv[:, 1, es]), Af)
                        ins.then_inc(av_done, 1)

            head_pass(0, True)
            with pe.Fori(1, HEADS) as I:
                head_pass(I, False)

            def merge_pass(i, first):
                for n in range(PASS_N):
                    J, m = 2 * i + n // MERGE_N, n % MERGE_N
                    a = PASS_N * i + A_MERGE + n
                    if m in (0, 2, 4, 5):
                        g = m // 2 if m < 4 else m - 2
                        if first and n in (0, 2):
                            pe.wait_ge(evac, 12 * HEADS + n + 2)
                        pe.wait_ge(evac3, 8 * J + 2 * g + 2)
                    pe.wait_ge(split3, a + 4)
                    if m < 4:
                        weights_still((1 + n) % 3, hT, 8 * (n % 2), KT, 2 * g, used3)
                    elif m == 4:
                        pe.wait_ge(og_ready, HEADS)
                        pe.wait_ge(part_read, HEADS + i)
                        weights_still((1 + n) % 3, og, 0, 8, 4, used3)
                    else:
                        pe.wait_ge(om_ready, HEADS)
                        weights_still((1 + n) % 3, om, 0, 8, 6, used3)
                    if first:
                        tail(HEADS - 1, n)
                    if n == 0:
                        pe.wait_ge(evac3, 8 * J + 6)
                        part_sums(HEADS + i)

            merge_pass(0, True)
            with pe.Fori(1, 4) as i:
                merge_pass(i, False)
            pe.wait_ge(evac3, 8 + 8 * 7 + 4)
            pe.wait_ge(dg_ready, 1)
            lay_out(G)
            pe.wait_ge(evac3, 8 + 8 * 8 - 2)
            part_sums(PARTS)
            pe.wait_ge(evac3, 8 + 8 * 8)

            for kt in range(KT):
                if kt < 3:
                    pe.wait_ge(split3, A_WO + kt + 4)
                else:
                    pe.wait_ge(split4, kt - 2)
                pe.wait_ge(m_ready, kt + 1)
                if kt == 0:
                    pe.wait_ge(part_read, PARTS)
                    one_row_tile(SLOT4[0], hT[:, 0, :], True, False, used3, (1,), False)
                    pe.wait_ge(g_ready, 1)
                    one_row_tile(SLOT4[0], hT[:, 0, :], True, False, used3, (0,))
                else:
                    one_row_tile(SLOT4[kt % 4], hT[:, kt, :], False, kt == KT - 1, used3 if kt < 3 else used4)
            pe.wait_ge(dg_ready, 2)
            pe.wait_ge(x2_ready, 1)
            lay_out(dg2)
            transposed(1, yt)

            pe.wait_ge(h_ready, 2 * KT)
            pe.wait_ge(g_ready, 2)
            with pe.Fori(0, UP_ITERS) as i:
                for n in range(4):
                    if n % 2 == 0:
                        pe.wait_ge(conv_done, 2 * i + n // 2 + 1)
                    pe.wait_ge(split4, 4 * i + W_UP + n - 2)
                    weights_still(SLOT4[n], hT, 8 * (n % 2), KT, 2 * (n // 2), used4)

            def down(i, first=False, last=False):
                for n in range(4):
                    pe.wait_ge(split4, 4 * i + W_DOWN + n - 2)
                    pe.wait_ge(a_ready, 4 * i + n + 1)
                    one_row_tile(SLOT4[n], asp[:, n, :], first and n == 0, last and n == 3, used4, (1, 0))

            down(0, first=True)
            with pe.Fori(1, FT // 4 - 1) as i:
                down(i)
            down(FT // 4 - 1, last=True)


_INS = ["x", "c", "w_ada", "b_ada", "g_pre_mix", "w_in", "w_alpha_up", "b_alpha", "g_gla_head", "w_gla_out",
        "w_moba_out", "w_o", "g_post_mix", "g_pre_ffn", "w_up", "w_conv", "b_conv", "w_down", "g_post_ffn"]


def kernel(**inputs):
    import numpy as np
    import concourse.bacc as bacc
    from concourse.bass_utils import run_bass_kernel_spmd

    nc = bacc.Bacc("TRN2", target_bir_lowering=False, num_devices=1)
    arrays, args = {}, []
    for name in _INS:
        a = np.ascontiguousarray(inputs[name])
        arrays[f"in_{name}"] = a
        args.append(nc.dram_tensor(f"in_{name}", a.shape, mybir.dt.from_np(a.dtype), kind="ExternalInput").ap())
    args.append(nc.dram_tensor("out_0", inputs["x"].shape, F32, kind="ExternalOutput").ap())
    layer_kernel(nc, *args)
    r = run_bass_kernel_spmd(nc, [arrays], core_ids=[0])
    return r.results[0]["out_0"]
```

```python
import concourse.bass as bass
from concourse import mybir
from contextlib import ExitStack

F32 = mybir.dt.float32
F32R = mybir.dt.float32r
U8 = mybir.dt.uint8
ALU = mybir.AluOpType
ACT = mybir.ActivationFunctionType
AX = mybir.AxisListType
ds = bass.ds

P = 128
KB = 1024


def layer_kernel(nc, x, c, w_ada, b_ada, g_pre_mix, w_in, w_alpha_up, b_alpha, g_gla_head, w_gla_out,
                 w_moba_out, w_o, g_post_mix, g_pre_ffn, w_up, w_conv, b_conv, w_down, g_post_ffn, out):
    TOK, D = x.shape[1], x.shape[2]
    TT = TOK // P
    KT = D // P
    FFN = w_down.shape[1]
    FT = FFN // P
    RANK, GLA_K = w_alpha_up.shape[1], w_alpha_up.shape[2]
    DV = g_gla_head.shape[1]
    HEADS = GLA_K // P
    GLA_V = HEADS * DV
    MOBA_W = w_moba_out.shape[1]
    EPS = 1e-6
    SCALE = float(P) ** -0.5
    GATE_TEMP = 16.0
    CW = 2048
    C_GQ, C_GK, C_GV = 0, GLA_K, 2 * GLA_K
    C_GR = C_GV + GLA_V
    C_LOW = C_GR + GLA_V
    C_MQ = C_LOW + RANK
    C_MK, C_MV = C_MQ + MOBA_W, C_MQ + 2 * MOBA_W
    C_GA = C_MQ + 3 * MOBA_W
    C_GB = C_GA + D
    assert (TOK, D, TT, KT, DV, HEADS, GLA_V, MOBA_W) == (256, 2048, 2, 16, 256, 4, 1024, 1024)

    HEAD_N, MERGE_N = 12, 6
    A_HEAD, A_MERGE, A_WO = 1, 1 + HEADS * HEAD_N, 1 + HEADS * HEAD_N + 8 * MERGE_N
    UP_ITERS = FFN // 256
    W_UP, W_DOWN = KT, KT + 4 * UP_ITERS
    SLOT4 = [(A_WO + 0) % 3, (A_WO + 1) % 3, (A_WO + 2) % 3, 3]
    PASS_N = 12
    ADA_HEAD = [0, 1, 1, 1, 1, 1, 2, 2, 2, 1, 2, 2]
    ADA_MERGE = [0, 0, 2, 2, 2, 2, 2, 2, 2, 1, 1, 0]
    assert sum(ADA_HEAD) == sum(ADA_MERGE) == KT and HEAD_N == PASS_N == 2 * MERGE_N
    M_SH1, M_SC1, M_GT1, M_SH2, M_SC2, M_GT2 = range(6)
    PARTS = 8

    win = w_in[0].rearrange("(k p) n -> p k n", p=P)
    wup = w_up[0].rearrange("(k p) n -> p k n", p=P)
    wgo = w_gla_out[0].rearrange("(k p) n -> p k n", p=P)
    wmo = w_moba_out[0].rearrange("(k p) n -> p k n", p=P)
    wo = w_o[0].rearrange("(k p) n -> p k n", p=P)
    wdn = w_down[0].rearrange("(k p) n -> p k n", p=P)
    wada = w_ada[0].rearrange("(p t) n -> p t n", t=KT)
    wada2 = w_ada[0].rearrange("(p t) (m n) -> p t m n", t=KT, m=6)
    x_v = x[0].rearrange("(t p) d -> p t d", p=P)
    out_v = out[0].rearrange("(t p) d -> p t d", p=P)

    ctx = ExitStack()
    with ctx:
        base = -(-nc.sbuf_base // 64) * 64

        def at(name, kb, shape, dt=F32):
            return nc.alloc_sbuf_tensor_at(name, [P] + shape, dt, offset=base + int(kb * KB))

        def sem(name):
            return ctx.enter_context(nc.semaphore(name))

        raw = at("raw", 0, [4, CW])
        ws = at("ws", 32, [4, 8, 2, 256], F32R)
        hT = at("hT", 96, [KT, 2 * TOK], F32R)
        NCOL = 96 + 66 + 352
        cols = at("cols", 128, [NCOL])
        ident = at("ident", 130.25, [P])
        ones = at("ones", 130.75, [P])
        mods = at("mods", 131.25, [6, KT])
        ccol = at("ccol", 131.625, [KT])
        scol = at("scol", 131.6875, [KT])
        stat = at("stat", 131.75, [48])
        eps = at("eps", 131.9375, [1])
        modsf = mods[:, :, :].rearrange("p m k -> p (m k)")
        xnat = at("xnat", 132, [TT, D])
        xn = at("xn", 148, [TT, D])
        junk = at("junk", 80, [D])
        rows = at("rows", 88, [6, P])
        maskf = at("maskf", 91, [8, P])
        acc0 = at("acc0", 180, [4, 2, 512])
        h32 = at("h32", 196, [2, 4, P])
        walpha = at("walpha", 203.5, [GLA_K])
        balpha = at("balpha", 205.5, [GLA_K])
        zabs = at("zabs", 132, [TT, GLA_K])
        zmin = at("zmin", 136, [TT, GLA_K])
        loga = at("loga", 140, [TT, GLA_K])
        galow = at("galow", 144, [TOK])
        galow_x = at("galow_x", 145, [TOK])
        og = at("og", 132, [8, 2 * TOK], F32R)
        om = at("om", 148, [8, 2 * TOK], F32R)
        ada = at("ada", 164, [2, 1024])
        acc = at("acc", 176, [1024])
        bT = at("bT", 24, [HEADS, TOK])
        bc = at("bc", 28, [TOK])
        eb = at("eb", 29, [2, TOK])
        rs = at("rs", 31, [TOK])
        Mb = at("Mb", 80, [2, TOK])
        A = at("A", 82, [3, P])
        ot = at("ot", 84, [2, TOK])
        sq = at("sq", 86, [2, TOK])
        ssb = at("ssb", 88, [2, 2 * TOK])
        pT = at("pT", 92, [2, 3 * P])
        qk = at("qk", 180, [2, TOK])
        vv = at("vv", 182, [TT, DV])
        grt = at("grt", 184, [2, TOK])
        tg = at("tg", 186, [2, TOK])
        mqk = at("mqk", 188, [2, 2, TOK])
        mv = at("mv", 192, [TT, 256])
        tmp = at("tmp", 196, [2, 2, TOK])
        tri = at("tri", 200, [P])
        causal = at("causal", 200.5, [2 * TOK])
        mask8 = at("mask8", 202.5, [8, P], U8)
        tmp3 = at("tmp3", 24, [2, 2, TOK])
        gx = at("gx", 28, [2, 2, TOK])
        sg = at("sg", 80, [2, 2, TOK])
        ya = at("ya", 84, [2, TOK])
        yb = at("yb", 86, [2, TOK])
        mT = at("mT", 180, [KT, TOK])
        G = at("G", 196, [D])
        x2 = at("x2", 132, [TT, D])
        yt = at("yt", 148, [TT, D])
        G1 = at("G1", 164, [D])
        junk2 = at("junk2", 180, [D])
        h32b = at("h32b", 188, [2, 4, P])
        dg2 = at("dg2", 172, [D])
        aT = at("aT", 148, [FT, TOK])
        cv = at("cv", 192, [2, TOK])
        ub = at("ub", 194, [2, TOK])
        up = at("up", 204, [2, TOK + 2])
        asp = at("asp", 96, [4, 2 * TOK], F32R)
        yo = at("yo", 104, [TT, D])
        junk3 = at("junk3", 120, [D])
        ps = ctx.enter_context(nc.psum_tensor("ps", [P, 8, 512], F32))

        COL_BADA, COL_PRE1, COL_POST1, COL_PRE2, COL_POST2, COL_GH, COL_CONV = 0, 96, 112, 128, 144, 160, 162
        COL_CB = COL_CONV + 3 * 2 * FT

        def sems(names):
            return [sem(n) for n in names.split()]

        c_in, x_in, rows_in, gate_in, xr_in = sems("c_in x_in rows_in gate_in xr_in")
        head_in = sems("head_in0 head_in1 head_in2 head_in3")
        raw3_in = sems("raw3_in0 raw3_in1 raw3_in2")
        raw4_in = sems("raw4_in0 raw4_in1 raw4_in2 raw4_in3")
        ada_in = sems("ada_in0 ada_in1")
        hi3, split3, used3, hi4, split4, used4 = sems("hi3 split3 used3 hi4 split4 used4")
        pool_step, dve_step, act_step, tail_step = sems("pool_step dve_step act_step tail_step")
        slot_free = sems("slot_free0 slot_free1 slot_free2 slot_free3")
        acc_step, ada_used, mod_done, mods_ready, part_read = sems("acc_step ada_used mod_done mods_ready part_read")
        scol_ready, xsq, xsqrt, xn_ready, colsT = sems("scol_ready xsq xsqrt xn_ready colsT")
        xT_done = sems("xT_even xT_odd")
        h_even, h_odd, h_hi, h_ready = sems("h_even h_odd h_hi h_ready")
        low_x, low_ready, z_done, z_abs, z_ln, la_ready, tri_done, bT_ready = sems(
            "low_x low_ready z_done z_abs z_ln la_ready tri_done bT_ready")
        cross, evac = sems("cross evac")
        e_ready, exp_done, level_ready, gram_done, select_done, a01_done = sems(
            "e_ready exp_done level_ready gram_done select_done a01_done")
        av_done, ot_done, sq_done, ss_done, rs_done, tanh_done, og_f, og_hi, og_ready = sems(
            "av_done ot_done sq_done ss_done rs_done tanh_done og_f og_hi og_ready")
        qk_done, nb_ready, p_ready, pn_ready, pt_done, ptc_done, pv_done, om_hi, om_ready = sems(
            "qk_done nb_ready p_ready pn_ready pt_done ptc_done pv_done om_hi om_ready")
        cross3, evac3, sig_done, m_done, m_hi, m_ready = sems("cross3 evac3 sig_done m_done m_hi m_ready")
        dg_ready, g_done, g_ready = sems("dg_ready g_done g_ready")
        y_done, ysq, ysum, ysqrt, y_read, x2_ready = sems("y_done ysq ysum ysqrt y_read x2_ready")
        cross5, up_ready, cb_done, conv_g, gelu_done, conv_done = sems("cross5 up_ready cb_done conv_g gelu_done conv_done")
        a_hi, a_ready, out_ready, out_done = sems("a_hi a_ready out_ready out_done")

        block = ctx.enter_context(nc.Block())

        def raw_blocks(slot):
            return raw[:, slot, :].rearrange("p (b n) -> p b n", n=256)

        def arrived4(w, k):
            return (w - k) // 4 + (1 if k == 3 else 0)

        def taken(u):
            return slot_free[u % 4], u // 4 + 1

        def head_place(b):
            return 4 * (b // 2), b % 2, (b // 2) % 2 + 4 * (b % 2)

        def ffn_place(b):
            i = (b - 8) // 2
            return 4 * i, b % 2, (0, 4, 6, 2)[i] + b % 2

        @block.sync
        def _(sp):
            def load(slot, arrival, src, lo, hi, n):
                dst = raw[:, slot, :].rearrange("p (b n) -> p b n", n=n)
                sp.dma_start(dst[:, lo:hi, :], src).then_inc(arrival, 16)

            def load_k(slot, arrival, w, kh, col, n=256, step=8):
                h = step // 2
                for j in (1, 0):
                    load(slot, arrival, w[:, step * kh + h * j:step * kh + h * (j + 1), ds(col, n)], h * j, h * (j + 1), n)

            def load_row(slot, arrival, w, kt):
                for j in range(2):
                    sp.dma_start(raw[:, slot, 1024 * j:1024 * (j + 1)], w[:, kt, 1024 * j:1024 * (j + 1)]).then_inc(arrival, 16)

            for u in range(2 * KT):
                quarter, v = u // 8, u % 8
                if u >= 4:
                    sp.wait_ge(*taken(u - 4))
                dst = raw[:, u % 4, :].rearrange("p (t m n) -> p t m n", t=2, m=2)
                for m in range(2):
                    sp.dma_start(dst[:, :, m, :], wada2[:, 2 * v:2 * v + 2, m, 512 * quarter:512 * (quarter + 1)]).then_inc(head_in[u % 4], 16)
            sp.wait_ge(slot_free[0], 8)
            load_k(0, raw3_in[0], win, 0, C_LOW, n=P, step=16)
            for j in (1, 2):
                sp.wait_ge(slot_free[j], 8)
            with sp.Fori(0, HEADS) as I:
                for n in range(HEAD_N):
                    slot, arrival, kh = (1 + n) % 3, raw3_in[(1 + n) % 3], n % 2
                    sp.wait_ge(split3, HEAD_N * I + A_HEAD + n + 1)
                    if n < 2:
                        dst = raw[:, slot, :].rearrange("p (k two n) -> p k two n", two=2, n=P)
                        for j, col in enumerate((C_GQ, C_GK)):
                            sp.dma_start(dst[:, :, j, :], win[:, 8 * kh:8 * kh + 8, ds(I * P + col, P)]).then_inc(arrival, 16)
                    else:
                        load_k(slot, arrival, win, kh, I * 256 + (C_GV, C_MQ, C_MK, C_MV, C_GR)[n // 2 - 1])
            with sp.Fori(0, 8) as J:
                for n in range(MERGE_N):
                    slot, arrival = (1 + n) % 3, raw3_in[(1 + n) % 3]
                    sp.wait_ge(split3, MERGE_N * J + A_MERGE + n + 1)
                    if n < 4:
                        load_k(slot, arrival, win, n % 2, J * 256 + (C_GA if n < 2 else C_GB))
                    else:
                        load_k(slot, arrival, wgo if n == 4 else wmo, 0, J * 256)
            for w in (0, 1, 2, 4, 3, *range(5, KT)):
                k = w % 4
                if w < 3:
                    sp.wait_ge(split3, A_WO + w + 1)
                    load_row(SLOT4[k], raw3_in[SLOT4[k]], wo, w)
                else:
                    if w in (4, 5, 6):
                        sp.wait_ge(split3, 3 + A_WO + w - 4 + 1)
                    if w >= 7:
                        sp.wait_ge(split4, w - 6)
                    if w == 3:
                        sp.wait_ge(evac3, 8 + 8 * 8)
                        sp.wait_ge(sig_done, 16)
                    load_row(SLOT4[k], raw4_in[k], wo, w)
                if w == 6:
                    sp.wait_ge(used3, A_WO)
                    sp.dma_start(x2[:, :, :], x_v).then_inc(xr_in, 16)
            with sp.Fori(0, UP_ITERS) as i:
                for n in range(4):
                    sp.wait_ge(split4, 4 * i + W_UP + n - 6)
                    load_k(SLOT4[n], raw4_in[n], wup, n % 2, i * 256 + (FFN if n >= 2 else 0))
            with sp.Fori(0, FT // 4) as i:
                for n in range(4):
                    sp.wait_ge(split4, 4 * i + W_DOWN + n - 6)
                    for j in range(2):
                        sp.dma_start(raw[:, SLOT4[n], 1024 * j:1024 * (j + 1)],
                                     wdn[:, ds(4 * i + n, 1), 1024 * j:1024 * (j + 1)]).then_inc(raw4_in[n], 16)
            for tt in range(TT):
                for half in range(2):
                    cs = slice(1024 * half, 1024 * (half + 1))
                    sp.wait_ge(out_ready, 2 * tt + half + 1)
                    sp.dma_start(out_v[:, tt, cs], yo[:, tt, cs]).then_inc(out_done, 16)
            sp.wait_ge(out_done, 32 * TT)

        @block.gpsimd
        def _(pool):
            step = [0]

            def made(ins):
                step[0] += 1
                ins.then_inc(pool_step, 1)
                pool.wait_ge(pool_step, step[0])

            made(pool.memset(ones[:, :], 1.0))
            made(pool.memset(eps[:, :], EPS))
            made(pool.memset(ident[:, :], 0.0))
            made(pool.affine_select(out=ident[:, :], in_=ident[:, :], compare_op=ALU.not_equal, fill=1.0, base=0,
                                    pattern=[[-1, P]], channel_multiplier=1))
            made(pool.memset(maskf[:, 0, :], 0.0))
            made(pool.memset(tri[:, :], 1.0 / GATE_TEMP))
            made(pool.affine_select(out=tri[:, :], in_=tri[:, :], compare_op=ALU.is_ge, fill=0.0, base=0,
                                    pattern=[[1, P]], channel_multiplier=-1))
            made(pool.memset(causal[:, :], 0.0))
            cv4 = causal[:, :].rearrange("p (t k) -> p t k", t=TT)
            made(pool.affine_select(out=cv4, in_=cv4, compare_op=ALU.is_ge, fill=-1e30, base=0,
                                    pattern=[[P, TT], [-1, TOK]], channel_multiplier=1))
            for lv in range(1, 8):
                s = 2 ** (lv - 1)
                m = maskf[:, lv, :].rearrange("p (g two s) -> p g two s", two=2, s=s)
                made(pool.memset(maskf[:, lv, :], 0.0))
                made(pool.memset(m[:, :, 1, :], 1.0))
                m2 = maskf[:, lv, :].rearrange("p (g r) -> p g r", r=2 * s)
                made(pool.affine_select(out=m2, in_=m2, compare_op=ALU.is_ge, fill=0.0, base=0,
                                        pattern=[[-2 * s, P // (2 * s)], [0, 2 * s]], channel_multiplier=1))
                made(pool.affine_select(out=m2, in_=m2, compare_op=ALU.is_ge, fill=0.0, base=s - 1,
                                        pattern=[[2 * s, P // (2 * s)], [0, 2 * s]], channel_multiplier=-1))
            made(pool.affine_select(out=maskf[:, 0, :], in_=maskf[:, 0, :], compare_op=ALU.not_equal, fill=1.0, base=0,
                                    pattern=[[-1, P]], channel_multiplier=1))
            pool.wait_ge(slot_free[3], 8)
            for q in range(PARTS):
                col = M_GT1 * D + 1024 * q
                with pool.Fori(0, KT // 2) as t:
                    for s in range(2):
                        pool.wait_ge(ada_used, 2 * t + (KT * q + s + 1))
                        pool.dma_start(ada[:, s, :], wada[:, ds(2 * t + s, 1), col:col + 1024]).then_inc(ada_in[s], 16)

        @block.scalar
        def _(act):
            steps = [0]

            def link(ins):
                steps[0] += 1
                ins.then_inc(act_step, 1)
                act.wait_ge(act_step, steps[0])

            def split_hi(slot, hi):
                act.activation(ws[:, slot, :, 0, :], raw_blocks(slot), ACT.Copy).then_inc(hi, 1)

            def split3_hi(n, group, need):
                act.wait_ge(raw3_in[n % 3], group * 32 + 32)
                if need is not None:
                    act.wait_ge(used3, need)
                split_hi(n % 3, hi3)

            def split4_hi(k, group, need, sem_used=used4):
                act.wait_ge(raw4_in[k], group * 32)
                if need is not None:
                    act.wait_ge(sem_used, need)
                split_hi(SLOT4[k], hi4)

            def h_batches(lo, hi, hb, sc, sh, place):
                for b in range(lo, hi):
                    kt0, tt, bank = place(b)
                    if b % 2 == 0:
                        act.wait_ge(xT_done[0], b // 2 + 1)
                        if b % 8:
                            act.wait_ge(h_ready, b - 1)
                        for j in range(4):
                            ins = act.activation(hb[:, 0, j, :], ps[:, bank, P * j:P * (j + 1)], ACT.Identity,
                                                 bias=mods[:, sh, kt0 + j:kt0 + j + 1], scale=mods[:, sc, kt0 + j:kt0 + j + 1])
                        ins.then_inc(h_even, 1)
                    act.wait_ge(h_odd if b % 2 else h_even, b // 2 + 1)
                    act.activation(hT[:, kt0:kt0 + 4, P * tt:P * (tt + 1)], hb[:, b % 2, :, :], ACT.Copy).then_inc(h_hi, 1)

            act.dma_start(ccol[:, :], c[0].rearrange("(p t) -> p t", t=KT)).then_inc(c_in, 16)
            act.dma_start(xnat[:, :, :], x_v).then_inc(x_in, 16)
            act.dma_start(rows[0:96, 0, :], b_ada[0].rearrange("(r p) -> r p", p=P)).then_inc(rows_in, 16)
            for j, g in enumerate((g_pre_mix, g_post_mix, g_pre_ffn, g_post_ffn)):
                act.dma_start(rows[KT * j:KT * (j + 1), 1, :], g[0].rearrange("(r p) -> r p", p=P)).then_inc(rows_in, 16)
            act.dma_start(rows[64:66, 1, :], g_gla_head[0].rearrange("(r p) -> r p", p=P)).then_inc(rows_in, 16)
            for j in range(3):
                act.dma_start(rows[0:2 * FT, 2 + j, :], w_conv[0, j].rearrange("(r p) -> r p", p=P)).then_inc(rows_in, 16)
            act.dma_start(rows[0:2 * FT, 5, :], b_conv[0].rearrange("(r p) -> r p", p=P)).then_inc(rows_in, 16)
            act.dma_start(walpha[0:RANK, :], w_alpha_up[0]).then_inc(gate_in, 16)
            act.dma_start(balpha[0:1, :], b_alpha).then_inc(gate_in, 16)
            act.wait_ge(c_in, 16)
            act.activation(scol[:, :], ccol[:, :], ACT.Silu).then_inc(scol_ready, 1)
            act.wait_ge(x_in, 16)
            act.wait_ge(pool_step, 2)
            for tt in range(TT):
                act.activation(junk[:, :], xnat[:, tt, :], ACT.Square, accum_out=stat[:, tt:tt + 1]).then_inc(xsq, 1)
                act.wait_ge(xsq, tt + 1)
            act.activation(stat[:, 2:4], stat[:, 0:2], ACT.Sqrt, scale=1.0 / D, bias=eps[:, :]).then_inc(xsqrt, 1)
            for quarter in range(4):
                if quarter == 3:
                    split3_hi(0, 0, None)
                act.wait_ge(mods_ready, quarter + 1)
                h_batches(2 * quarter, 2 * quarter + 2, h32, M_SC1, M_SH1, head_place)
            for n in (1, 2):
                split3_hi(n, 0, None)

            act.wait_ge(used3, 1)
            act.activation(galow_x[0:RANK, :], ps[0:RANK, 6, TOK:2 * TOK], ACT.Copy).then_inc(low_x, 1)
            split3_hi(0, 1, 1)

            def tail(prev, n):
                if n == 0:
                    for hd in range(2):
                        act.wait_ge(pt_done, 2 * prev + hd + 1)
                        act.activation(pT[:, hd, :], ps[:, 6 + hd, 0:3 * P], ACT.Copy).then_inc(ptc_done, 1)
                    act.wait_ge(ss_done, prev + 1)
                    act.activation(rs[:, :], ps[:, 5, 0:TOK], ACT.Sqrt, scale=1.0 / DV, bias=eps[:, :]).then_inc(rs_done, 1)
                    act.wait_ge(evac, 12 * prev + 12 + 4)
                    act.activation(tg[:, :, :], grt[:, :, :], ACT.Tanh, scale=0.5).then_inc(tanh_done, 1)
                if n == 2:
                    act.wait_ge(og_f, prev + 1)
                    act.activation(og[:, ds(2 * prev, 2), 0:TOK], ot[:, :, :], ACT.Copy).then_inc(og_hi, 1)
                    act.wait_ge(pv_done, prev + 1)
                    act.activation(om[:, ds(2 * prev, 2), 0:TOK], ps[:, 6:8, 0:TOK], ACT.Copy).then_inc(om_hi, 1)

            def head_pass(I, first):
                for n in range(HEAD_N):
                    a = HEAD_N * I + A_HEAD + n
                    if n % 2 == 1:
                        g = n // 2
                        b = 2 * (g % 2)
                        act.wait_ge(used3, a + 1)
                        act.wait_ge(evac, 12 * I + 2 * g + 2)
                        if g == 0:
                            act.activation(tmp[:, 0, 0, :], ps[:, 0, TOK:], ACT.Copy, scale=SCALE).then_inc(cross, 1)
                            act.activation(tmp[:, 0, 1, :], ps[:, 1, TOK:], ACT.Copy).then_inc(cross, 1)
                        else:
                            act.activation(tmp[:, g % 2, :, :], ps[:, b:b + 2, TOK:], ACT.Copy).then_inc(cross, 1)
                    split3_hi(1 + n, 4 * I + (1 + n + 3) // 3, a + 1)
                    if not first:
                        tail(I - 1, n)
                    elif n == 0:
                        act.wait_ge(z_done, 1)
                        act.activation(zabs[:, :, :], ps[:, 4:6, :], ACT.Abs).then_inc(z_abs, 1)
                        act.wait_ge(z_abs, 1)
                        link(act.activation(zabs[:, :, :], zabs[:, :, :], ACT.Exp, scale=-1.0))
                        act.activation(zabs[:, :, :], zabs[:, :, :], ACT.Ln, bias=1.0).then_inc(z_ln, 1)
                    if n == 3:
                        act.wait_ge(gram_done, 9 * I + 2)
                        act.activation(A[:, 1, :], ps[:, 5, 0:P], ACT.Copy).then_inc(a01_done, 1)
                    for p in ((0, 1) if n == int(first) else (n,) if 2 <= n <= 7 else ()):
                        act.wait_ge(e_ready, 8 * I + p + 1)
                        act.activation(eb[:, p % 2, :], eb[:, p % 2, :], ACT.Exp).then_inc(exp_done, 1)
                    if n == 9:
                        act.wait_ge(nb_ready, I + 1)
                        for hd in range(2):
                            for qt in range(TT):
                                v = ssb[:, hd, TOK * qt:TOK * (qt + 1)]
                                j = 2 * hd + qt
                                act.activation(v, v, ACT.Exp, scale=SCALE, bias=stat[:, 20 + j:21 + j],
                                               accum_out=stat[:, 24 + j:25 + j]).then_inc(p_ready, 1)
                    if n == 11:
                        act.wait_ge(av_done, I + 1)
                        act.activation(ot[:, :, :], ps[:, 4, :].rearrange("p (e t) -> p e t", e=2), ACT.Copy).then_inc(ot_done, 1)
                        act.activation(sq[:, :, :], ps[:, 4, :].rearrange("p (e t) -> p e t", e=2), ACT.Square).then_inc(sq_done, 1)

            head_pass(0, True)
            with act.Fori(1, HEADS) as I:
                head_pass(I, False)

            def merged_hi(kt):
                act.activation(hT[:, kt, 0:TOK], mT[:, kt, :], ACT.Copy).then_inc(m_hi, 1)

            def merge_pass(i, first, last=False):
                for n in range(PASS_N):
                    J, m = 2 * i + n // MERGE_N, n % MERGE_N
                    a = PASS_N * i + A_MERGE + n
                    if m in (1, 3, 4, 5):
                        g = {1: 0, 3: 1, 4: 2, 5: 3}[m]
                        act.wait_ge(used3, a + 1)
                        act.wait_ge(evac3, 8 * J + 2 * g + 6)
                        act.activation(tmp3[:, g % 2, :, :], ps[:, 2 * g:2 * g + 2, TOK:], ACT.Copy).then_inc(cross3, 1)
                    split3_hi(1 + n, 4 * i + 16 + (1 + n + 3) // 3, a + 1)
                    if m in (1, 3):
                        act.wait_ge(evac3, 8 * J + 2 * (g + 1) + 8)
                        act.activation(sg[:, g, :, :], gx[:, g, :, :], ACT.Sigmoid).then_inc(sig_done, 1)
                    if last and n == PASS_N - 1:
                        act.wait_ge(used3, A_WO)
                        for kt in range(4):
                            merged_hi(kt)
                    if first:
                        tail(HEADS - 1, n)

            merge_pass(0, True)
            with act.Fori(1, 3) as i:
                merge_pass(i, False)
            merge_pass(3, False, True)

            act.wait_ge(ada_used, 2 + KT * PARTS)
            act.wait_ge(g_done, 1)
            act.activation(G1[:, :], ps[:, 0:4, :].rearrange("p b n -> p (b n)"), ACT.Copy).then_inc(g_ready, 1)
            act.wait_ge(m_done, 8)
            split4_hi(3, 1, None)
            for w in range(4, KT):
                if w < 7:
                    split4_hi(w % 4, w // 4, A_WO + w - 4 + 1, used3)
                else:
                    split4_hi(w % 4, arrived4(w, w % 4), w - 6)
                merged_hi(w)

            def first_up(w):
                split4_hi(w % 4, arrived4(w, w % 4), w - 6)

            def y_factor(branch, tt, junk_):
                if branch == 0 and tt == 1:
                    act.wait_ge(used4, KT - 3)
                else:
                    act.wait_ge(y_done, branch + tt + 1)
                for b in range(4):
                    act.activation(junk_[:, 512 * b:512 * (b + 1)], ps[:, 4 * tt + b, :], ACT.Square,
                                   accum_out=stat[:, 32 + 4 * tt + b:33 + 4 * tt + b]).then_inc(ysq, 1)
                act.wait_ge(ysum, TT * branch + tt + 1)
                act.activation(stat[:, 4 + tt:5 + tt], stat[:, 4 + tt:5 + tt], ACT.Sqrt, scale=1.0 / D, bias=eps[:, :]).then_inc(ysqrt, 1)

            def x2_factor(tt):
                act.wait_ge(x2_ready, tt + 1)
                act.activation(yt[:, tt, :], x2[:, tt, :], ACT.Square, accum_out=stat[:, 6 + tt:7 + tt]).then_inc(xsq, 1)
                act.wait_ge(xsq, TT + tt + 1)
                act.activation(stat[:, 6 + tt:7 + tt], stat[:, 6 + tt:7 + tt], ACT.Sqrt, scale=1.0 / D, bias=eps[:, :]).then_inc(xsqrt, 1)

            y_factor(0, 0, junk2)
            first_up(KT)
            first_up(KT + 1)
            x2_factor(0)
            y_factor(0, 1, junk2)
            act.wait_ge(g_done, 2)
            act.activation(G[:, :], ps[:, 0:4, :].rearrange("p b n -> p (b n)"), ACT.Copy).then_inc(g_ready, 1)
            x2_factor(1)
            first_up(KT + 2)
            h_batches(8, 16, h32b, M_SC2, M_SH2, ffn_place)
            first_up(KT + 3)

            def up_tasks(i, n):
                g = (n - 1) // 2
                q = 2 * i + g
                act.wait_ge(used4, 4 * i + W_UP + n - 2)
                act.wait_ge(conv_done, q + 2)
                act.activation(cv[:, :, :], ps[:, 2 * g:2 * g + 2, TOK:], ACT.Copy).then_inc(cross5, 1)
                act.wait_ge(up_ready, q + 1)
                for ct in range(2):
                    f = 2 * i + FT * g + ct
                    act.activation(cv[:, ct, :], up[:, ct, 2:], ACT.Identity, scale=cols[:, ds(f + COL_CONV + 4 * FT, 1)],
                                   bias=cols[:, ds(f + COL_CB, 1)]).then_inc(cb_done, 1)
                if g == 1:
                    act.wait_ge(conv_g, i + 1)
                    act.activation(cv[:, :, :], cv[:, :, :], ACT.Gelu_apprx_tanh).then_inc(gelu_done, 1)

            def act_hi(kt, k, need):
                if need is not None:
                    act.wait_ge(used4, need)
                act.activation(asp[:, k, 0:TOK], aT[:, ds(kt, 1), :], ACT.Copy).then_inc(a_hi, 1)

            def up_pass(i, last):
                for n in range(4):
                    if last and n == 3:
                        for k in range(4):
                            act_hi(k, k, W_DOWN - 3 if k == 0 else None)
                    split4_hi(n, i + (W_UP + 4) // 4 + (n == 3), 4 * i + W_UP + n + 4 - 6)
                    if n % 2 == 1:
                        up_tasks(i, n)

            with act.Fori(0, UP_ITERS - 1) as i:
                up_pass(i, False)
            up_pass(UP_ITERS - 1, True)

            with act.Fori(0, FT // 4 - 1) as i:
                for n in range(4):
                    act_hi(4 * i + 4 + n, n, 4 * i + W_DOWN + n + 4 - 6)
                    split4_hi(n, i + (W_DOWN + 4) // 4 + (n == 3), 4 * i + W_DOWN + n + 4 - 6)
            for tt in range(TT):
                y_factor(1, tt, junk3)

        @block.vector
        def _(dve):
            steps = [0]

            class Loop:
                def __init__(self, base, i=None, size=0, sem=dve_step):
                    self.base, self.i, self.size, self.k, self.sem = base, i, size, 0, sem

                def link(self, ins, wait=True):
                    ins.then_inc(self.sem, 1)
                    self.k += 1
                    if wait:
                        self.wait()

                def wait(self, k=None):
                    k = self.k if k is None else k
                    if self.i is None:
                        dve.wait_ge(self.sem, self.base + k)
                    else:
                        dve.wait_ge(self.sem, self.i * self.size + (self.base + k))

            S = Loop(0)
            link = S.link

            def split_lo(slot, hi, need, done):
                dve.wait_ge(hi, need)
                dve.tensor_tensor(ws[:, slot, :, 1, :], raw_blocks(slot), ws[:, slot, :, 0, :].bitcast(F32),
                                  ALU.subtract).then_inc(done, 1)

            def ada_units(q, n, table):
                done = sum(table[:n])
                for k in range(done, done + table[n]):
                    dve.wait_ge(ada_in[k % 2], (KT // 2 * q + k // 2) * 16 + 16)
                    if k == 0:
                        ins = dve.tensor_scalar(acc[:, :], ada[:, 0, :], scol[:, 0:1], None, ALU.mult)
                    else:
                        dve.wait_ge(ada_used, KT * q + k + 2)
                        ins = dve.scalar_tensor_tensor(acc[:, :], ada[:, k % 2, :], scol[:, k:k + 1], acc[:, :], ALU.mult, ALU.add)
                    ins.then_inc(ada_used, 1)

            def part_sums(q):
                dve.wait_ge(mod_done, q + 4)
                dve.tensor_copy(modsf[:, ds(8 * q + (M_GT1 * KT - 8), 8)], ps[:, 4, 0:8]).then_inc(part_read, 1)

            def h_batches(lo, hi, hb, sc, sh, place):
                def scale(b):
                    kt0, tt, bank = place(b)
                    dve.wait_ge(xT_done[1], b // 2 + 1)
                    if b % 8 > 1:
                        dve.wait_ge(h_ready, b - 1)
                    for j in range(4):
                        ins = dve.tensor_scalar(hb[:, 1, j, :], ps[:, bank, P * j:P * (j + 1)], mods[:, sc, kt0 + j:kt0 + j + 1],
                                                mods[:, sh, kt0 + j:kt0 + j + 1], ALU.mult, ALU.add)
                    ins.then_inc(h_odd, 1)

                scale(lo + 1)
                for b in range(lo, hi):
                    kt0, tt, bank = place(b)
                    dve.wait_ge(h_hi, b + 1)
                    dve.tensor_tensor(hT[:, kt0:kt0 + 4, TOK + P * tt:TOK + P * (tt + 1)], hb[:, b % 2, :, :],
                                      hT[:, kt0:kt0 + 4, P * tt:P * (tt + 1)].bitcast(F32), ALU.subtract).then_inc(h_ready, 1)
                    if b % 2 == 1 and b + 2 < hi:
                        scale(b + 2)

            dve.memset(stat[:, 12:13], 0.0).then_inc(ada_used, 2)
            dve.memset(stat[:, 8:9], 0.0).then_inc(split3, 3)
            dve.memset(stat[:, 9:10], 0.0).then_inc(evac, 4)
            dve.memset(stat[:, 10:11], 0.0).then_inc(evac3, 8)
            dve.memset(stat[:, 11:12], 0.0).then_inc(conv_done, 2)
            dve.wait_ge(scol_ready, 1)

            def head_unit(quarter, v):
                u = 8 * quarter + v
                steps_before = 3 * (7 * quarter + v - (v > 3))
                before = taken(u - 2 if v == 4 else u - 1)
                dve.wait_ge(head_in[u % 4], 32 * (u // 4) + 32)
                for k in range(4):
                    j, m = k // 2, k % 2
                    src, t, a = raw[:, u % 4, 1024 * j + 512 * m:1024 * j + 512 * (m + 1)], 2 * v + j, acc0[:, quarter, m, :]
                    if t == 0:
                        ins = dve.tensor_scalar(a, src, scol[:, t:t + 1], None, ALU.mult)
                    else:
                        dve.wait_ge(*(before if k == 1 else (acc_step, steps_before + max(k - 1, 0))))
                        ins = dve.scalar_tensor_tensor(a, src, scol[:, t:t + 1], a, ALU.mult, ALU.add)
                    ins.then_inc(slot_free[u % 4] if k == 3 else acc_step, 1)

            def shift_and_scale(quarter):
                qs = slice(4 * quarter, 4 * quarter + 4)
                dve.wait_ge(mod_done, quarter + 1)
                link(dve.tensor_tensor(mods[:, M_SH1:M_SC1 + 1, qs], ps[:, 2 + quarter % 2, 0:8].rearrange("p (m k) -> p m k", m=2),
                                       cols[:, 0:2 * KT].rearrange("p (m k) -> p m k", m=2)[:, :, qs], ALU.add))
                dve.scalar_tensor_tensor(mods[:, M_SC1, qs], mods[:, M_SC1, qs], 1.0, cols[:, COL_PRE1 + 4 * quarter:COL_PRE1 + 4 * quarter + 4],
                                         ALU.add, ALU.mult).then_inc(mods_ready, 1)
                dve.wait_ge(mods_ready, quarter + 1)

            for v in range(3):
                head_unit(0, v)
            dve.wait_ge(colsT, 1)
            link(dve.tensor_copy(cols[:, 0:426], ps[:, 0, 0:426]), wait=False)
            link(dve.tensor_copy(cols[:, 426:NCOL], ps[:, 1, 0:NCOL - 426]))
            link(dve.tensor_scalar(cols[:, COL_GH:COL_GH + 2], cols[:, COL_GH:COL_GH + 2], 0.5, None, ALU.mult), wait=False)
            dve.wait_ge(xsqrt, 1)
            link(dve.reciprocal(stat[:, 2:4], stat[:, 2:4]))
            for tt in range(TT):
                dve.tensor_scalar(xn[:, tt, :], xnat[:, tt, :], stat[:, 2 + tt:3 + tt], None, ALU.mult).then_inc(xn_ready, 1)
            for v in range(4, 8):
                head_unit(0, v)
            for quarter in range(4):
                nxt = quarter + 1
                if nxt < 4:
                    for v in range(2):
                        head_unit(nxt, v)
                else:
                    split_lo(0, hi3, 1, split3)
                shift_and_scale(quarter)
                h_batches(2 * quarter, 2 * quarter + 2, h32, M_SC1, M_SH1, head_place)
                if nxt < 4:
                    for v in (2, 4, 5, 6, 7):
                        head_unit(nxt, v)
            for n in (1, 2):
                split_lo(n, hi3, n + 1, split3)

            dve.wait_ge(low_x, 1)
            dve.tensor_tensor(galow[0:RANK, :], ps[0:RANK, 6, 0:TOK], galow_x[0:RANK, :], ALU.add).then_inc(low_ready, 1)
            split_lo(0, hi3, 4, split3)
            dve.wait_ge(pool_step, 38)
            link(dve.tensor_copy(mask8[:, :, :], maskf[:, :, :]), wait=False)

            def level_decay(I, p):
                s = P if p == 0 else 2 ** (p - 1)
                v = bc[:, :].rearrange("p (g two s) -> p g two s", two=2, s=s)
                e = eb[:, p % 2, :].rearrange("p (g two s) -> p g two s", two=2, s=s)
                grp = TOK // (2 * s)
                ref = v[:, :, 0, s - 1:s].to_broadcast([P, grp, s])
                if p >= 2:
                    dve.wait_ge(level_ready, 8 * I + p - 1)
                dve.tensor_tensor(e[:, :, 0, :], ref, v[:, :, 0, :], ALU.subtract)
                if p == 0:
                    last = dve.tensor_copy(e[:, :, 1, :], v[:, :, 1, :])
                else:
                    last = dve.tensor_tensor(e[:, :, 1, :], v[:, :, 1, :], ref, ALU.subtract)
                last.then_inc(e_ready, 1)

            def level_operands(I, p):
                s = P if p == 0 else 2 ** (p - 1)
                def halves(t):
                    return t.rearrange("p (g two s) -> p g two s", two=2, s=s)
                e, m = halves(eb[:, p % 2, :]), halves(Mb[:, p % 2, :])
                dve.wait_ge(exp_done, 8 * I + p + 1)
                if p >= 2:
                    dve.wait_ge(gram_done, 9 * I + p)
                dve.tensor_tensor(m[:, :, 0, :], halves(qk[:, 1, :])[:, :, 0, :], e[:, :, 0, :], ALU.mult)
                dve.tensor_tensor(m[:, :, 1, :], halves(qk[:, 0, :])[:, :, 1, :], e[:, :, 1, :], ALU.mult).then_inc(level_ready, 1)

            def before_select(I, lv):
                if lv:
                    dve.wait_ge(select_done, 8 * I + lv)
                dve.wait_ge(gram_done, 9 * I + (1 if lv == 0 else lv + 2))

            def select(I, lv):
                bank = 4 if lv == 0 or lv % 2 else 5
                dve.copy_predicated(A[:, 0:3:2, :], mask8[:, lv, :].unsqueeze(1).to_broadcast([P, 2, P]),
                                    ps[:, bank, 0:TOK].rearrange("p (t i) -> p t i", t=2)).then_inc(select_done, 1)

            def evacuate(I, g, dst):
                b = 2 * (g % 2)
                dve.wait_ge(cross, 7 * I + g + 2)
                dve.tensor_tensor(dst, ps[:, b:b + 2, 0:TOK], tmp[:, g % 2, :, :], ALU.add).then_inc(evac, 2)

            TAIL_STEPS = 3

            def tail(prev, n):
                if n == 1:
                    T = Loop(0, prev, TAIL_STEPS, tail_step)
                    dve.wait_ge(tanh_done, prev + 1)
                    dve.wait_ge(rs_done, prev + 1)
                    T.link(dve.reciprocal(rs[:, :], rs[:, :]), wait=False)
                    T.link(dve.scalar_tensor_tensor(tg[:, :, :], tg[:, :, :], 1.0, grt[:, :, :], ALU.add, ALU.mult), wait=False)
                    dve.wait_ge(ot_done, prev + 1)
                    T.wait(1)
                    T.link(dve.tensor_tensor(ot[:, :, :], ot[:, :, :], rs[:, :].unsqueeze(1).to_broadcast([P, 2, TOK]), ALU.mult))
                    assert T.k == TAIL_STEPS
                    for e in range(2):
                        ins = dve.scalar_tensor_tensor(ot[:, e, :], ot[:, e, :], cols[:, COL_GH + e:COL_GH + e + 1],
                                                       tg[:, e, :], ALU.mult, ALU.mult)
                    ins.then_inc(og_f, 1)
                if n == 2:
                    dve.wait_ge(og_hi, prev + 1)
                    dve.tensor_tensor(og[:, ds(2 * prev, 2), TOK:], ot[:, :, :],
                                      og[:, ds(2 * prev, 2), 0:TOK].bitcast(F32), ALU.subtract).then_inc(og_ready, 1)
                if n == 3:
                    dve.wait_ge(om_hi, prev + 1)
                    dve.tensor_tensor(om[:, ds(2 * prev, 2), TOK:], ps[:, 6:8, 0:TOK],
                                      om[:, ds(2 * prev, 2), 0:TOK].bitcast(F32), ALU.subtract).then_inc(om_ready, 1)

            HEAD_STEPS = 7

            def bc_and_decays(L, I):
                L.link(dve.tensor_copy(bc[:, :], bT[:, ds(I, 1), :]))
                level_decay(I, 0)
                level_decay(I, 1)

            def head_pass(I, first):
                L = Loop(head_start, I, HEAD_STEPS)
                for n in range(HEAD_N):
                    a = HEAD_N * I + A_HEAD + n
                    if first and n == 0:
                        dve.wait_ge(z_abs, 1)
                        link(dve.tensor_scalar(zmin[:, :, :], ps[:, 4:6, :], 0.0, None, ALU.min))
                        dve.wait_ge(z_ln, 1)
                        dve.tensor_tensor(loga[:, :, :], zmin[:, :, :], zabs[:, :, :], ALU.subtract).then_inc(la_ready, 1)
                    if not first and n == 0:
                        bc_and_decays(L, I)
                    if n == 1:
                        dve.wait_ge(cross, 7 * I + 1)
                        dve.scalar_tensor_tensor(qk[:, 0, :], ps[:, 0, 0:TOK], SCALE, tmp[:, 0, 0, :],
                                                 ALU.mult, ALU.add).then_inc(evac, 1)
                        dve.wait_ge(cross, 7 * I + 2)
                        dve.tensor_tensor(qk[:, 1, :], ps[:, 1, 0:TOK], tmp[:, 0, 1, :], ALU.add).then_inc(evac, 1)
                    if first and n == 1:
                        dve.wait_ge(tri_done, 1)
                        dve.tensor_copy(bT[:, :, :].rearrange("p h t -> p (h t)"), ps[:, 6:8, :].rearrange("p b n -> p (b n)")).then_inc(bT_ready, 1)
                        dve.wait_ge(bT_ready, 1)
                        bc_and_decays(L, I)
                    if n == 9:
                        for hd in range(2):
                            dve.wait_ge(qk_done, 2 * I + hd + 1)
                            L.link(dve.tensor_tensor(ssb[:, hd, :], ps[:, 6 + hd, :], causal[:, :], ALU.add))
                            L.link(dve.reduce_max(stat[:, 16 + 2 * hd:18 + 2 * hd],
                                                  ssb[:, hd, :].rearrange("p (t k) -> p t k", t=TT), AX.X), wait=hd == 1)
                        dve.tensor_scalar(stat[:, 20:24], stat[:, 16:20], -SCALE, None, ALU.mult).then_inc(nb_ready, 1)
                    if n == 2:
                        L.link(dve.memset(A[:, 0:3:2, :], 0.0), wait=False)
                        dve.wait_ge(evac, 12 * I + 2 + 4)
                        level_operands(I, 0)
                        level_operands(I, 1)
                    if 3 <= n <= 10:
                        if n == 3:
                            dve.wait_ge(dve_step, I * HEAD_STEPS + (head_start + 2))
                        before_select(I, max(n - 3, 0))
                        if n - 1 <= 7:
                            level_operands(I, n - 1)
                        if n == 9:
                            evacuate(I, 4, mv[:, :, :])
                        if n == 10:
                            dve.wait_ge(p_ready, 4 * I + 4)
                            L.link(dve.reciprocal(stat[:, 28:32], stat[:, 24:28]), wait=False)
                        select(I, n - 3)
                    if 2 <= n <= 7:
                        level_decay(I, n)
                    if n in (3, 5, 7, 11):
                        evacuate(I, n // 2, {3: vv[:, :, :], 5: mqk[:, 0, :, :], 7: mqk[:, 1, :, :], 11: grt[:, :, :]}[n])
                    if n == 10:
                        L.wait()
                        for hd in range(2):
                            for qt in range(TT):
                                v = ssb[:, hd, TOK * qt:TOK * (qt + 1)]
                                j = 28 + 2 * hd + qt
                                ins = dve.tensor_scalar(v, v, stat[:, j:j + 1], None, ALU.mult)
                            ins.then_inc(pn_ready, 1)
                    if not first:
                        tail(I - 1, n)
                        if n == 1:
                            part_sums(I)
                    ada_units(I, n, ADA_HEAD)
                    split_lo((1 + n) % 3, hi3, a + 3 + 1, split3)
                assert L.k == HEAD_STEPS, L.k

            head_start = S.base + S.k + 1
            head_pass(0, True)
            with dve.Fori(1, HEADS) as I:
                head_pass(I, False)
            assert S.base + S.k == head_start
            S.base += HEADS * HEAD_STEPS

            def diagonal(G, m):
                for j in range(KT):
                    ins = dve.tensor_scalar(G[:, P * j:P * (j + 1)], ident[:, :], mods[:, m, j:j + 1], None, ALU.mult)
                ins.then_inc(dg_ready, 1)

            link(dve.tensor_tensor(mods[:, M_GT1, :], mods[:, M_GT1, :], cols[:, M_GT1 * KT:(M_GT1 + 1) * KT], ALU.add))
            link(dve.tensor_tensor(mods[:, M_GT1, :], mods[:, M_GT1, :], cols[:, COL_POST1:COL_POST1 + KT], ALU.mult))
            diagonal(G, M_GT1)

            MERGE_STEPS = 2

            def merged_lo(kt):
                dve.wait_ge(m_hi, kt + 1)
                dve.tensor_tensor(hT[:, kt, TOK:], mT[:, kt, :], hT[:, kt, 0:TOK].bitcast(F32), ALU.subtract).then_inc(m_ready, 1)

            def merge_pass(i, first, last=False):
                for n in range(PASS_N):
                    J, m = 2 * i + n // MERGE_N, n % MERGE_N
                    a = PASS_N * i + A_MERGE + n
                    if m == 0:
                        L = Loop(merge_start, J, MERGE_STEPS)
                    if m in (1, 3):
                        g = m // 2
                        dve.wait_ge(cross3, 4 * J + g + 1)
                        dve.tensor_tensor(gx[:, g, :, :], ps[:, 2 * g:2 * g + 2, 0:TOK], tmp3[:, g, :, :], ALU.add).then_inc(evac3, 2)
                    if m in (4, 5):
                        g = m - 2
                        y = ya if m == 4 else yb
                        dve.wait_ge(cross3, 4 * J + g + 1)
                        dve.tensor_tensor(y[:, :, :], ps[:, 2 * g:2 * g + 2, 0:TOK], tmp3[:, g % 2, :, :], ALU.add).then_inc(evac3, 2)
                        if last and n == PASS_N - 1:
                            for kt in range(4):
                                merged_lo(kt)
                            part_sums(PARTS)
                        dve.wait_ge(evac3, 8 * J + 2 * (g + 1) + 8)
                        dve.wait_ge(sig_done, 2 * J + g - 1)
                        L.link(dve.tensor_tensor(y[:, :, :], y[:, :, :], sg[:, g - 2, :, :], ALU.mult), wait=m == 5)
                    if m == 5:
                        dve.tensor_tensor(mT[:, ds(2 * J, 2), :], ya[:, :, :], yb[:, :, :], ALU.add).then_inc(m_done, 1)
                        assert L.k == MERGE_STEPS
                    if first:
                        tail(HEADS - 1, n)
                    if n == 2:
                        part_sums(HEADS + i)
                    ada_units(HEADS + i, n, ADA_MERGE)
                    split_lo((1 + n) % 3, hi3, a + 3 + 1, split3)

            merge_start = S.base + S.k
            merge_pass(0, True)
            with dve.Fori(1, 3) as i:
                merge_pass(i, False)
            merge_pass(3, False, True)
            S.base += 8 * MERGE_STEPS

            split_lo(3, hi4, 1, split4)
            for w in range(4, KT):
                split_lo(SLOT4[w % 4], hi4, w - 2, split4)
                if w == 4:
                    dve.wait_ge(part_read, PARTS)
                    link(dve.tensor_tensor(mods[:, M_SH2:, :], mods[:, M_SH2:, :],
                                           cols[:, M_SH2 * KT:6 * KT].rearrange("p (m k) -> p m k", m=3), ALU.add))
                    link(dve.tensor_tensor(mods[:, M_GT2, :], mods[:, M_GT2, :], cols[:, COL_POST2:COL_POST2 + KT], ALU.mult), wait=False)
                    dve.scalar_tensor_tensor(mods[:, M_SC2, :], mods[:, M_SC2, :], 1.0, cols[:, COL_PRE2:COL_PRE2 + KT],
                                             ALU.add, ALU.mult).then_inc(mods_ready, 1)
                if w == 6:
                    S.wait()
                    diagonal(dg2, M_GT2)
                merged_lo(w)

            def factor(branch, tt):
                dve.wait_ge(ysq, 8 * branch + 4 * tt + 4)
                dve.reduce_sum(stat[:, 4 + tt:5 + tt], stat[:, 32 + 4 * tt:36 + 4 * tt], AX.X).then_inc(ysum, 1)
                dve.wait_ge(ysqrt, TT * branch + tt + 1)
                link(dve.reciprocal(stat[:, 4 + tt:5 + tt], stat[:, 4 + tt:5 + tt]))

            def gated(branch, tt, dst, gate):
                for b in range(4):
                    dve.wait_ge(ysq, 8 * branch + 4 * tt + b + 1)
                    dve.tensor_tensor(dst[:, tt, 512 * b:512 * (b + 1)], ps[:, 4 * tt + b, :], gate[:, 512 * b:512 * (b + 1)],
                                      ALU.mult).then_inc(y_read, 1)

            def mixed(tt):
                gated(0, tt, yt, G1)
                factor(0, tt)
                dve.scalar_tensor_tensor(x2[:, tt, :], yt[:, tt, :], stat[:, 4 + tt:5 + tt], x2[:, tt, :],
                                         ALU.mult, ALU.add).then_inc(x2_ready, 1)

            def normed(tt):
                dve.wait_ge(xsqrt, tt + 2)
                link(dve.reciprocal(stat[:, 6 + tt:7 + tt], stat[:, 6 + tt:7 + tt]))
                dve.tensor_scalar(yt[:, tt, :], x2[:, tt, :], stat[:, 6 + tt:7 + tt], None, ALU.mult).then_inc(xn_ready, 1)

            dve.wait_ge(xr_in, 16)
            dve.wait_ge(g_ready, 1)
            def first_up(w):
                split_lo(SLOT4[w % 4], hi4, w - 2, split4)

            mixed(0)
            first_up(KT)
            normed(0)
            mixed(1)
            first_up(KT + 1)
            normed(1)
            h_batches(8, 16, h32b, M_SC2, M_SH2, ffn_place)
            first_up(KT + 2)
            first_up(KT + 3)
            link(dve.memset(up[:, :, 0:2], 0.0))

            UP_STEPS = 4
            up_start = S.base + S.k

            def act_lo(kt, k):
                dve.wait_ge(a_hi, kt + 1)
                dve.tensor_tensor(asp[:, k, TOK:], aT[:, ds(kt, 1), :], asp[:, k, 0:TOK].bitcast(F32), ALU.subtract).then_inc(a_ready, 1)

            def up_pass(i, last):
                L = Loop(up_start, i, UP_STEPS)
                for n in range(4):
                    if last and n == 3:
                        for k in range(4):
                            act_lo(k, k)
                    split_lo(SLOT4[n], hi4, 4 * i + W_UP + n + 4 - 2, split4)
                    if n % 2 == 0:
                        continue
                    g = n // 2
                    q = 2 * i + g
                    dve.wait_ge(cross5, q + 1)
                    dve.tensor_tensor(up[:, :, 2:], ps[:, 2 * g:2 * g + 2, 0:TOK], cv[:, :, :], ALU.add).then_inc(up_ready, 1)
                    for ct in range(2):
                        f = 2 * i + FT * g + ct
                        dve.wait_ge(cb_done, 2 * q + ct + 1)
                        L.link(dve.scalar_tensor_tensor(cv[:, ct, :], up[:, ct, 1:TOK + 1], cols[:, ds(f + COL_CONV + 2 * FT, 1)],
                                                        cv[:, ct, :], ALU.mult, ALU.add), wait=ct == 1)
                    dst = cv if g else ub
                    for ct in range(2):
                        f = 2 * i + FT * g + ct
                        ins = dve.scalar_tensor_tensor(dst[:, ct, :], up[:, ct, 0:TOK], cols[:, ds(f + COL_CONV, 1)],
                                                       cv[:, ct, :], ALU.mult, ALU.add)
                    ins.then_inc(conv_g if g else conv_done, 1)
                    if g:
                        dve.wait_ge(gelu_done, i + 1)
                        dve.tensor_tensor(aT[:, ds(2 * i, 2), :], cv[:, :, :], ub[:, :, :], ALU.mult).then_inc(conv_done, 1)
                assert L.k == UP_STEPS, L.k

            with dve.Fori(0, UP_ITERS - 1) as i:
                up_pass(i, False)
            up_pass(UP_ITERS - 1, True)
            S.base += UP_ITERS * UP_STEPS

            with dve.Fori(0, FT // 4 - 1) as i:
                for n in range(4):
                    act_lo(4 * i + 4 + n, n)
                    split_lo(SLOT4[n], hi4, 4 * i + W_DOWN + n + 4 - 2, split4)
            dve.wait_ge(g_ready, 2)
            for tt in range(TT):
                gated(1, tt, yo, G)
                factor(1, tt)
                for half in range(2):
                    cs = slice(1024 * half, 1024 * (half + 1))
                    dve.scalar_tensor_tensor(yo[:, tt, cs], yo[:, tt, cs], stat[:, 4 + tt:5 + tt], x2[:, tt, cs],
                                             ALU.mult, ALU.add).then_inc(out_ready, 1)

        @block.tensor
        def _(pe):
            def mm(out_, lhsT, rhs, start=True, stop=True):
                return pe.matmul(out_, lhsT, rhs, start=start, stop=stop)

            def weights_still(slot, acts, k0, kn, bank, used, before=None):
                for k in range(8):
                    kk = k0 + k
                    if before:
                        before(kk)
                    for ct in range(2):
                        cs = slice(P * ct, P * (ct + 1))
                        mm(ps[:, bank + ct, :], ws[:, slot, k, 0, cs], acts[:, kk, :], kk == 0, False)
                        last = mm(ps[:, bank + ct, TOK:], ws[:, slot, k, 1, cs], acts[:, kk, 0:TOK], False, kk == kn - 1)
                last.then_inc(used, 1)

            def tokens_still(slot, k0, bank, used):
                for k in range(8):
                    kk = k0 + k
                    for tt in range(TT):
                        mm(ps[:, bank + tt, :], hT[:, kk, P * tt:P * (tt + 1)], ws[:, slot, k, :, :], kk == 0, False)
                        last = mm(ps[:, bank + tt, TOK:], hT[:, kk, TOK + P * tt:TOK + P * (tt + 1)], ws[:, slot, k, 0, :], False, kk == KT - 1)
                last.then_inc(used, 1)

            def one_row_tile(slot, acts, first, last_, tt):
                hi, lo = acts[:, P * tt:P * (tt + 1)], acts[:, TOK + P * tt:TOK + P * (tt + 1)]
                for b in range(4):
                    w_hi, w_lo = ws[:, slot, 2 * b:2 * b + 2, 0, :], ws[:, slot, 2 * b:2 * b + 2, 1, :]
                    mm(ps[:, 4 * tt + b, :], hi, w_hi, first, False)
                    mm(ps[:, 4 * tt + b, :], hi, w_lo, False, False)
                    ins = mm(ps[:, 4 * tt + b, :], lo, w_hi, False, last_)
                return ins

            def transposed(lo, hi, src, place):
                for b in range(lo, hi):
                    kt0, tt, bank = place(b)
                    for j in range(4):
                        ins = pe.transpose(ps[:, bank, P * j:P * (j + 1)], src[:, tt, P * (kt0 + j):P * (kt0 + j + 1)], ident[:, :])
                    ins.then_inc(xT_done[b % 2], 1)

            def column_sums(a, col, bank, at_):
                for j in range(KT):
                    ins = mm(ps[:, bank, at_ + j:at_ + j + 1], a[:, col + P * j:col + P * (j + 1)], ones[:, 0:1])
                return ins

            def lay_out(dg):
                for b in range(4):
                    ins = mm(ps[:, b, :], ones[:, :], dg[:, 512 * b:512 * (b + 1)])
                ins.then_inc(g_done, 1)

            pe.wait_ge(pool_step, 4)
            pe.wait_ge(rows_in, 160)
            pe.transpose(ps[:, 0, 0:96], rows[0:96, 0, :], ident[0:96, 0:96])
            pe.transpose(ps[:, 0, 96:162], rows[0:66, 1, :], ident[0:66, 0:66])
            nc_ = 2 * FT
            for j in range(3):
                pe.transpose(ps[:, 0, COL_CONV + nc_ * j:COL_CONV + nc_ * (j + 1)], rows[0:nc_, 2 + j, :], ident[0:nc_, 0:nc_])
            pe.transpose(ps[:, 1, 0:nc_], rows[0:nc_, 5, :], ident[0:nc_, 0:nc_]).then_inc(colsT, 1)
            for quarter in range(4):
                u, bank = 8 * quarter + 3, 2 + quarter % 2
                pe.wait_ge(head_in[3], 32 * (u // 4) + 32)
                if quarter == 0:
                    pe.wait_ge(scol_ready, 1)
                for j in range(2):
                    for k in range(8):
                        ins = mm(ps[:, bank, k:k + 1], raw[:, 3, 1024 * j + P * k:1024 * j + P * (k + 1)], scol[:, 6 + j:7 + j], j + k == 0, False)
                ins.then_inc(slot_free[3], 1)
                if quarter == 0:
                    pe.wait_ge(xn_ready, TT)
                if quarter >= 2:
                    pe.wait_ge(h_even, quarter - 1)
                    pe.wait_ge(h_odd, quarter - 1)
                transposed(2 * quarter, 2 * quarter + 2, xn, head_place)
                pe.wait_ge(*taken(8 * quarter + 7))
                for j in range(8):
                    ins = mm(ps[:, bank, j:j + 1], acc0[:, quarter, j // 4, P * (j % 4):P * (j % 4 + 1)], ones[:, 0:1], False, j == 7)
                ins.then_inc(mod_done, 1)

            pe.wait_ge(split3, 0 + 4)
            for k in range(KT):
                if k % 4 == 0:
                    pe.wait_ge(h_ready, k // 2 + 2)
                cs = slice(P * (k % 2), P * (k % 2 + 1))
                mm(ps[:, 6, :], ws[:, 0, k // 2, 0, cs], hT[:, k, :], k == 0, False)
                ins = mm(ps[:, 6, TOK:], ws[:, 0, k // 2, 1, cs], hT[:, k, 0:TOK], False, k == KT - 1)
            ins.then_inc(used3, 1)

            def gates(n):
                if n == 0:
                    pe.wait_ge(low_ready, 1)
                    pe.wait_ge(gate_in, 32)
                    for tt in range(TT):
                        mm(ps[:, 4 + tt, :], galow[0:RANK, P * tt:P * (tt + 1)], walpha[0:RANK, :], True, False)
                        ins = mm(ps[:, 4 + tt, :], ones[0:1, :], balpha[0:1, :], False, True)
                    ins.then_inc(z_done, 1)
                if n == 1:
                    pe.wait_ge(la_ready, 1)
                    for h in range(HEADS):
                        for tt in range(TT):
                            col = TOK * (h % 2) + P * tt
                            ins = mm(ps[:, 6 + h // 2, col:col + P], loga[:, tt, P * h:P * (h + 1)], tri[:, :])
                    ins.then_inc(tri_done, 1)

            def gram(I, p):
                bank = 4 if p % 2 else 5
                pe.wait_ge(level_ready, 8 * I + p + 1)
                if p == 0:
                    mm(ps[:, 5, 0:P], Mb[:, 0, 0:P], Mb[:, 0, P:]).then_inc(gram_done, 1)
                    return
                if p == 2:
                    pe.wait_ge(a01_done, I + 1)
                else:
                    pe.wait_ge(select_done, 8 * I + max(p - 1, 1))
                for t in range(TT):
                    m = Mb[:, p % 2, P * t:P * (t + 1)]
                    ins = mm(ps[:, bank, P * t:P * (t + 1)], m, m)
                ins.then_inc(gram_done, 1)

            def causal_product(out_, values, weights):
                mm(out_, values[0], weights[:, 0:2 * P], True, False)
                return mm(out_[:, P:2 * P], values[1], weights[:, 2 * P:3 * P], False, True)

            def part_sums(q):
                pe.wait_ge(ada_used, KT * q + 2)
                for j in range(8):
                    ins = mm(ps[:, 4, j:j + 1], acc[:, P * j:P * (j + 1)], ones[:, 0:1])
                ins.then_inc(mod_done, 1)

            def tail(prev, n):
                if n == 0:
                    for hd in range(2):
                        pe.wait_ge(pn_ready, 2 * prev + hd + 1)
                        for j, (qt, k) in enumerate(((0, 0), (1, 0), (1, 1))):
                            ins = pe.transpose(ps[:, 6 + hd, P * j:P * (j + 1)],
                                               ssb[:, hd, TOK * qt + P * k:TOK * qt + P * (k + 1)], ident[:, :])
                        ins.then_inc(pt_done, 1)
                    pe.wait_ge(sq_done, prev + 1)
                    mm(ps[:, 5, 0:TOK], ones[:, :], sq[:, 0, :], True, False)
                    mm(ps[:, 5, 0:TOK], ones[:, :], sq[:, 1, :], False, True).then_inc(ss_done, 1)
                if n == 2:
                    for hd in range(2):
                        es = slice(P * hd, P * (hd + 1))
                        pe.wait_ge(ptc_done, 2 * prev + hd + 1)
                        ins = causal_product(ps[:, 6 + hd, 0:TOK], (mv[:, 0, es], mv[:, 1, es]), pT[:, hd, :])
                    ins.then_inc(pv_done, 1)

            def head_pass(I, first):
                for n in range(HEAD_N):
                    a = HEAD_N * I + A_HEAD + n
                    g = n // 2
                    b = 2 * (g % 2)
                    if n % 2 == 0:
                        pe.wait_ge(evac, 12 * I + 2 * g + 2)
                    pe.wait_ge(split3, a + 4)
                    if g in (1, 4):
                        tokens_still((1 + n) % 3, 8 * (n % 2), b, used3)
                    else:
                        weights_still((1 + n) % 3, hT, 8 * (n % 2), KT, b, used3)
                    if first:
                        gates(n)
                    else:
                        tail(I - 1, n)
                        if n == 1:
                            part_sums(I)
                    if n == 3:
                        pe.wait_ge(evac, 12 * I + 2 + 4)
                        if not first:
                            pe.wait_ge(part_read, I)
                        for t in range(TT):
                            ts = slice(P * t, P * (t + 1))
                            ins = mm(ps[:, 4, ts], qk[:, 1, ts], qk[:, 0, ts])
                        ins.then_inc(gram_done, 1)
                    if 3 <= n <= 10:
                        gram(I, n - 3)
                    if n == 9:
                        pe.wait_ge(evac, 12 * I + 8 + 4)
                        for hd in range(2):
                            for qt in range(TT):
                                ins = mm(ps[:, 6 + hd, TOK * qt:TOK * (qt + 1)], mqk[:, 0, hd, P * qt:P * (qt + 1)], mqk[:, 1, hd, :])
                            ins.then_inc(qk_done, 1)
                    if n == 11:
                        pe.wait_ge(evac, 12 * I + 4 + 4)
                        pe.wait_ge(select_done, 8 * I + 8)
                        Af = A[:, :, :].rearrange("p j i -> p (j i)")
                        for e in range(2):
                            es = slice(P * e, P * (e + 1))
                            ins = causal_product(ps[:, 4, TOK * e:TOK * (e + 1)], (vv[:, 0, es], vv[:, 1, es]), Af)
                        ins.then_inc(av_done, 1)

            head_pass(0, True)
            with pe.Fori(1, HEADS) as I:
                head_pass(I, False)

            def merge_pass(i, first, last=False):
                for n in range(PASS_N):
                    J, m = 2 * i + n // MERGE_N, n % MERGE_N
                    a = PASS_N * i + A_MERGE + n
                    if m in (0, 2, 4, 5):
                        g = m // 2 if m < 4 else m - 2
                        if first and n in (0, 2):
                            pe.wait_ge(evac, 12 * HEADS + n + 2)
                        pe.wait_ge(evac3, 8 * J + 2 * g + 2)
                    pe.wait_ge(split3, a + 4)
                    if m < 4:
                        weights_still((1 + n) % 3, hT, 8 * (n % 2), KT, 2 * g, used3)
                    elif m == 4:
                        pe.wait_ge(og_ready, HEADS)
                        pe.wait_ge(part_read, HEADS + i)
                        weights_still((1 + n) % 3, og, 0, 8, 4, used3)
                    else:
                        pe.wait_ge(om_ready, HEADS)
                        weights_still((1 + n) % 3, om, 0, 8, 6, used3)
                    if first:
                        tail(HEADS - 1, n)
                    if n == 2:
                        pe.wait_ge(evac3, 8 * J + 6)
                        part_sums(HEADS + i)

            merge_pass(0, True)
            with pe.Fori(1, 4) as i:
                merge_pass(i, False)
            pe.wait_ge(evac3, 8 + 8 * 7 + 4)
            pe.wait_ge(dg_ready, 1)
            lay_out(G)
            pe.wait_ge(evac3, 8 + 8 * 8 - 2)
            part_sums(PARTS)
            pe.wait_ge(evac3, 8 + 8 * 8)

            for kt in range(KT):
                if kt < 3:
                    pe.wait_ge(split3, A_WO + kt + 4)
                else:
                    pe.wait_ge(split4, kt - 2)
                pe.wait_ge(m_ready, kt + 1)
                slot, acts = SLOT4[kt % 4], hT[:, kt, :]
                if kt == 0:
                    pe.wait_ge(part_read, PARTS)
                    one_row_tile(slot, acts, True, False, 1)
                    pe.wait_ge(g_ready, 1)
                    one_row_tile(slot, acts, True, False, 0).then_inc(used3, 1)
                elif kt < KT - 4:
                    one_row_tile(slot, acts, False, False, 0)
                    one_row_tile(slot, acts, False, False, 1).then_inc(used3 if kt < 3 else used4, 1)
                else:
                    ins = one_row_tile(slot, acts, False, kt == KT - 1, 0)
            ins.then_inc(y_done, 1)
            for kt in range(KT - 4, KT):
                one_row_tile(SLOT4[kt % 4], hT[:, kt, :], False, kt == KT - 1, 1).then_inc(used4, 1)
            pe.wait_ge(y_read, 4)
            pe.wait_ge(dg_ready, 2)
            lay_out(dg2)
            pe.wait_ge(xn_ready, TT + 1)
            pe.wait_ge(g_ready, 2)
            pe.wait_ge(y_read, 8)
            for b in range(8, 16, 2):
                transposed(b, b + 1, yt, ffn_place)
            pe.wait_ge(xn_ready, TT + 2)
            for b in range(9, 16, 2):
                transposed(b, b + 1, yt, ffn_place)

            def h_is_ready(k):
                if k % 4 == 0:
                    pe.wait_ge(h_ready, 8 + k // 2 + 2)

            with pe.Fori(0, UP_ITERS) as i:
                for n in range(4):
                    if n % 2 == 0:
                        pe.wait_ge(conv_done, 2 * i + n // 2 + 1)
                    pe.wait_ge(split4, 4 * i + W_UP + n - 2)
                    weights_still(SLOT4[n], hT, 8 * (n % 2), KT, 2 * (n // 2), used4, h_is_ready if n < 2 else None)

            def down(i, first=False):
                for n in range(4):
                    pe.wait_ge(split4, 4 * i + W_DOWN + n - 2)
                    pe.wait_ge(a_ready, 4 * i + n + 1)
                    one_row_tile(SLOT4[n], asp[:, n, :], first and n == 0, False, 1)
                    if first and n == 0:
                        pe.wait_ge(up_ready, 2 * UP_ITERS)
                    one_row_tile(SLOT4[n], asp[:, n, :], first and n == 0, False, 0).then_inc(used4, 1)

            down(0, first=True)
            with pe.Fori(1, FT // 4 - 1) as i:
                down(i)
            for tt in range(TT):
                for n in range(4):
                    if tt == 0:
                        pe.wait_ge(split4, W_DOWN + FT - 4 + n - 2)
                        pe.wait_ge(a_ready, FT - 4 + n + 1)
                    ins = one_row_tile(SLOT4[n], asp[:, n, :], False, n == 3, tt)
                ins.then_inc(y_done, 1)


_INS = ["x", "c", "w_ada", "b_ada", "g_pre_mix", "w_in", "w_alpha_up", "b_alpha", "g_gla_head", "w_gla_out",
        "w_moba_out", "w_o", "g_post_mix", "g_pre_ffn", "w_up", "w_conv", "b_conv", "w_down", "g_post_ffn"]


def kernel(**inputs):
    import numpy as np
    import concourse.bacc as bacc
    from concourse.bass_utils import run_bass_kernel_spmd

    nc = bacc.Bacc("TRN2", target_bir_lowering=False, num_devices=1)
    arrays, args = {}, []
    for name in _INS:
        a = np.ascontiguousarray(inputs[name])
        arrays[f"in_{name}"] = a
        args.append(nc.dram_tensor(f"in_{name}", a.shape, mybir.dt.from_np(a.dtype), kind="ExternalInput").ap())
    args.append(nc.dram_tensor("out_0", inputs["x"].shape, F32, kind="ExternalOutput").ap())
    layer_kernel(nc, *args)
    r = run_bass_kernel_spmd(nc, [arrays], core_ids=[0])
    return r.results[0]["out_0"]
```
